# Optimizing a Trainium2 kernel written in Bass

```python
import jax, jax.numpy as jnp
from jax import lax
import numpy as np

D_MODEL = 1024
BATCH = 1
SEQ = 512
DEPTH = 2
DEC_BATCH = 1
DEC_SEQ = 32
PAST_LEN = 128

CHUNK = 64
N_MIXERS = 2
N_POOL_LAYERS = (DEPTH + 1) // 2
N_ATTN_LAYERS = DEPTH // 2
POOL_WINDOWS = (2, 4, 8, 16)
N_POOL_GROUPS = 4
POOL_GROUP = D_MODEL // N_POOL_GROUPS
POOL_HIST = max(POOL_WINDOWS) - 1
N_HEADS = 16
HEAD_DIM = D_MODEL // N_HEADS
LEFT_CHUNKS = 8
BAND_CHUNKS = LEFT_CHUNKS + 1
REL_MAX = 256
N_REL = CHUNK + REL_MAX
N_GROUPS = 4
EXPERTS_PER_GROUP = 8
N_EXPERTS = N_GROUPS * EXPERTS_PER_GROUP
TOP_K = 2
D_EXPERT = D_MODEL // 2
MOE_BLOCK = 128
EPS = 1e-6

kernel_name = "streaming_pool_bandattn_hmoe"

f32 = jnp.float32

def rms_norm(x, g):
    xf = x.astype(f32)
    y = xf * lax.rsqrt(jnp.mean(xf * xf, axis=-1, keepdims=True) + EPS)
    return (y * g.astype(f32)).astype(x.dtype)

def pool_mix(h, hist, pos0, w_pool, pool_scale):
    B, L, D = h.shape
    ext = jnp.concatenate([hist.astype(h.dtype), h], axis=1)
    cs = jnp.cumsum(ext.astype(f32), axis=1)
    cs = jnp.concatenate([jnp.zeros((B, 1, D), f32), cs], axis=1)
    end = cs[:, POOL_HIST + 1:]
    pos = pos0 + jnp.arange(L, dtype=jnp.int32)
    outs = []
    for g, w in enumerate(POOL_WINDOWS):
        sl = slice(g * POOL_GROUP, (g + 1) * POOL_GROUP)
        start = cs[:, POOL_HIST + 1 - w: POOL_HIST + 1 - w + L, sl]
        cnt = jnp.minimum(pos + 1, w).astype(f32)[None, :, None]
        outs.append((end[..., sl] - start) / cnt)
    pooled = jnp.stack(outs, axis=2)
    delta = pooled - h.reshape(B, L, N_POOL_GROUPS, POOL_GROUP).astype(f32)
    y = jnp.einsum('blgc,gcd->blgd', delta, w_pool.astype(f32)).reshape(B, L, D)
    y = (y * pool_scale.astype(f32)).astype(h.dtype)
    return y, ext[:, -POOL_HIST:]

def attn_project(h, w_qkv, q_gain, k_gain):
    B, L, _ = h.shape
    qkv = jnp.einsum('bld,de->ble', h, w_qkv).reshape(B, L, 3, N_HEADS, HEAD_DIM)
    q = rms_norm(qkv[:, :, 0], q_gain)
    k = rms_norm(qkv[:, :, 1], k_gain)
    v = qkv[:, :, 2]
    return q, k, v

def band_attention(q, k, v, qpos, kpos, rel_bias):
    qc = qpos[:, :, None] // CHUNK
    kc = kpos[:, None, :] // CHUNK
    visible = (kpos[:, None, :] >= 0) & (kc <= qc) & (qc - kc <= LEFT_CHUNKS)
    rel = qpos[:, :, None] - kpos[:, None, :]
    idx = jnp.clip(rel, -(CHUNK - 1), REL_MAX) + (CHUNK - 1)
    bias = jnp.moveaxis(rel_bias[:, idx], 0, 1).astype(f32)
    s = jnp.einsum('bnqhd,bnkhd->bnhqk', q.astype(f32), k.astype(f32)) * (HEAD_DIM ** -0.5) + bias[None]
    s = jnp.where(visible[None, :, None], s, -1e30)
    p = jax.nn.softmax(s, axis=-1)
    return jnp.einsum('bnhqk,bnkhd->bnqhd', p, v.astype(f32)).astype(q.dtype)

def attn_prompt(h, w_qkv, w_o, q_gain, k_gain, rel_bias):
    B, S, D = h.shape
    q, k, v = attn_project(h, w_qkv, q_gain, k_gain)
    nc = S // CHUNK
    pad = LEFT_CHUNKS * CHUNK

    def band(t):
        tp = jnp.pad(t, ((0, 0), (pad, 0), (0, 0), (0, 0))).reshape(B, nc + LEFT_CHUNKS, CHUNK, N_HEADS, HEAD_DIM)
        return jnp.stack([tp[:, j:j + nc] for j in range(BAND_CHUNKS)], axis=2).reshape(
            B, nc, BAND_CHUNKS * CHUNK, N_HEADS, HEAD_DIM)

    qpos = jnp.arange(S, dtype=jnp.int32).reshape(nc, CHUNK)
    kpos = (jnp.arange(nc, dtype=jnp.int32)[:, None] * CHUNK - pad) + jnp.arange(BAND_CHUNKS * CHUNK, dtype=jnp.int32)[None, :]
    o = band_attention(q.reshape(B, nc, CHUNK, N_HEADS, HEAD_DIM), band(k), band(v), qpos, kpos, rel_bias)
    y = jnp.einsum('bse,ed->bsd', o.reshape(B, S, D), w_o)
    keep = min(LEFT_CHUNKS * CHUNK, S)
    return y, k[:, S - keep:], v[:, S - keep:]

def attn_sample(h, cache_k, cache_v, w_qkv, w_o, q_gain, k_gain, rel_bias):
    B, L, D = h.shape
    q, k, v = attn_project(h, w_qkv, q_gain, k_gain)
    keep = cache_k.shape[1]
    kk = jnp.concatenate([cache_k.astype(k.dtype), k], axis=1)[:, None]
    vv = jnp.concatenate([cache_v.astype(v.dtype), v], axis=1)[:, None]
    qpos = (PAST_LEN + jnp.arange(L, dtype=jnp.int32))[None]
    kpos = (PAST_LEN - keep + jnp.arange(keep + L, dtype=jnp.int32))[None]
    o = band_attention(q[:, None], kk, vv, qpos, kpos, rel_bias)
    y = jnp.einsum('bse,ed->bsd', o.reshape(B, L, D), w_o)
    return y, k, v

def hier_moe(x, w_r1, b_r1, w_r2, b_r2, w_gate, w_up, w_down):
    B, L, D = x.shape
    xt = x.reshape(-1, D)
    T = xt.shape[0]
    logit1 = (xt @ w_r1).astype(f32) + b_r1.astype(f32)
    p1 = jax.nn.softmax(logit1, axis=-1)
    grp = jnp.argmax(logit1, axis=-1)
    p_grp = jnp.max(p1, axis=-1, keepdims=True)
    logit2_all = jnp.einsum('td,gde->tge', xt, w_r2).astype(f32) + b_r2.astype(f32)
    logit2 = jnp.einsum('tg,tge->te', jax.nn.one_hot(grp, N_GROUPS, dtype=f32), logit2_all)
    p2 = jax.nn.softmax(logit2, axis=-1)
    top_p, top_e = lax.top_k(p2, TOP_K)
    gates = p_grp * top_p / jnp.sum(top_p, axis=-1, keepdims=True)
    expert = grp[:, None].astype(jnp.int32) * EXPERTS_PER_GROUP + top_e.astype(jnp.int32)

    A = T * TOP_K
    n_blocks = -(-A // MOE_BLOCK) + N_EXPERTS
    P = n_blocks * MOE_BLOCK
    flat_e = expert.reshape(-1)
    flat_tok = jnp.repeat(jnp.arange(T, dtype=jnp.int32), TOP_K)
    flat_g = gates.reshape(-1)
    order = jnp.argsort(flat_e)
    se, stok, sg = flat_e[order], flat_tok[order], flat_g[order]
    counts = jnp.bincount(flat_e, length=N_EXPERTS).astype(jnp.int32)
    start = jnp.cumsum(counts) - counts
    pcounts = (counts + MOE_BLOCK - 1) // MOE_BLOCK * MOE_BLOCK
    pend = jnp.cumsum(pcounts)
    pstart = pend - pcounts
    dest = pstart[se] + (jnp.arange(A, dtype=jnp.int32) - start[se])
    row_tok = jnp.full((P,), T, jnp.int32).at[dest].set(stok)
    row_gate = jnp.zeros((P,), f32).at[dest].set(sg)
    blk_expert = jnp.minimum(jnp.searchsorted(pend, jnp.arange(n_blocks, dtype=jnp.int32) * MOE_BLOCK, side='right'),
                             N_EXPERTS - 1).astype(jnp.int32)
    xpad = jnp.concatenate([xt, jnp.zeros((1, D), xt.dtype)], axis=0)

    def run_block(args):
        tok, e = args
        xb = xpad[tok]
        hidden = jax.nn.silu(xb @ w_gate[e]) * (xb @ w_up[e])
        return hidden @ w_down[e]

    yb = lax.map(run_block, (row_tok.reshape(n_blocks, MOE_BLOCK), blk_expert))
    y = jax.ops.segment_sum(yb.reshape(P, D).astype(f32) * row_gate[:, None], row_tok, num_segments=T + 1)[:T]
    return y.reshape(B, L, D).astype(x.dtype)

def setup_inputs(seed: int = 0) -> dict:
    key = jax.random.key(seed)
    ks = jax.random.split(key, 24)

    def nrm(k, shape, scale):
        return scale * jax.random.normal(k, shape, f32)

    kv_keep = min(LEFT_CHUNKS * CHUNK, PAST_LEN)
    return {
        "x_prompt": nrm(ks[0], (BATCH, SEQ, D_MODEL), 1.0),
        "x_sample": nrm(ks[1], (DEC_BATCH, DEC_SEQ, D_MODEL), 1.0),
        "cache_pool": nrm(ks[2], (N_POOL_LAYERS, DEC_BATCH, POOL_HIST, D_MODEL), 1.0),
        "cache_k": nrm(ks[3], (N_ATTN_LAYERS, DEC_BATCH, kv_keep, N_HEADS, HEAD_DIM), 1.0),
        "cache_v": nrm(ks[4], (N_ATTN_LAYERS, DEC_BATCH, kv_keep, N_HEADS, HEAD_DIM), 1.0),
        "norm_mix": 1.0 + nrm(ks[5], (DEPTH, D_MODEL), 0.02),
        "norm_ffn": 1.0 + nrm(ks[6], (DEPTH, D_MODEL), 0.02),
        "pool_w": nrm(ks[7], (N_POOL_LAYERS, N_POOL_GROUPS, POOL_GROUP, POOL_GROUP), POOL_GROUP ** -0.5),
        "pool_scale": 0.3 + nrm(ks[8], (N_POOL_LAYERS, D_MODEL), 0.05),
        "attn_w_qkv": nrm(ks[9], (N_ATTN_LAYERS, D_MODEL, 3 * D_MODEL), D_MODEL ** -0.5),
        "attn_w_o": nrm(ks[10], (N_ATTN_LAYERS, D_MODEL, D_MODEL), D_MODEL ** -0.5),
        "attn_q_gain": 1.0 + nrm(ks[11], (N_ATTN_LAYERS, HEAD_DIM), 0.02),
        "attn_k_gain": 1.0 + nrm(ks[12], (N_ATTN_LAYERS, HEAD_DIM), 0.02),
        "attn_rel_bias": nrm(ks[13], (N_ATTN_LAYERS, N_HEADS, N_REL), 0.1),
        "moe_w_r1": nrm(ks[14], (DEPTH, D_MODEL, N_GROUPS), D_MODEL ** -0.5),
        "moe_b_r1": nrm(ks[15], (DEPTH, N_GROUPS), 0.01),
        "moe_w_r2": nrm(ks[16], (DEPTH, N_GROUPS, D_MODEL, EXPERTS_PER_GROUP), D_MODEL ** -0.5),
        "moe_b_r2": nrm(ks[17], (DEPTH, N_GROUPS, EXPERTS_PER_GROUP), 0.01),
        "moe_w_gate": nrm(ks[18], (DEPTH, N_EXPERTS, D_MODEL, D_EXPERT), D_MODEL ** -0.5),
        "moe_w_up": nrm(ks[19], (DEPTH, N_EXPERTS, D_MODEL, D_EXPERT), D_MODEL ** -0.5),
        "moe_w_down": nrm(ks[20], (DEPTH, N_EXPERTS, D_EXPERT, D_MODEL), D_EXPERT ** -0.5),
    }

def reference(x_prompt, x_sample, cache_pool, cache_k, cache_v, norm_mix, norm_ffn, pool_w, pool_scale,
              attn_w_qkv, attn_w_o, attn_q_gain, attn_k_gain, attn_rel_bias,
              moe_w_r1, moe_b_r1, moe_w_r2, moe_b_r2, moe_w_gate, moe_w_up, moe_w_down):
    xp, xs = x_prompt, x_sample
    pool_new_p, pool_new_s, k_new_p, v_new_p, k_new_s, v_new_s = [], [], [], [], [], []
    for i in range(DEPTH):
        hp = rms_norm(xp, norm_mix[i])
        hs = rms_norm(xs, norm_mix[i])
        if i % N_MIXERS == 0:
            a = i // N_MIXERS
            zero_hist = jnp.zeros((hp.shape[0], POOL_HIST, D_MODEL), hp.dtype)
            yp, stp = pool_mix(hp, zero_hist, 0, pool_w[a], pool_scale[a])
            ys, sts = pool_mix(hs, cache_pool[a], PAST_LEN, pool_w[a], pool_scale[a])
            pool_new_p.append(stp)
            pool_new_s.append(sts)
        else:
            a = i // N_MIXERS
            yp, kp, vp = attn_prompt(hp, attn_w_qkv[a], attn_w_o[a], attn_q_gain[a], attn_k_gain[a], attn_rel_bias[a])
            ys, ks_, vs_ = attn_sample(hs, cache_k[a], cache_v[a], attn_w_qkv[a], attn_w_o[a],
                                       attn_q_gain[a], attn_k_gain[a], attn_rel_bias[a])
            k_new_p.append(kp)
            v_new_p.append(vp)
            k_new_s.append(ks_)
            v_new_s.append(vs_)
        xp = xp + yp
        xs = xs + ys
        moe_args = (moe_w_r1[i], moe_b_r1[i], moe_w_r2[i], moe_b_r2[i], moe_w_gate[i], moe_w_up[i], moe_w_down[i])
        xp = xp + hier_moe(rms_norm(xp, norm_ffn[i]), *moe_args)
        xs = xs + hier_moe(rms_norm(xs, norm_ffn[i]), *moe_args)
    state_pool_prompt = jnp.stack(pool_new_p, axis=0)
    state_pool_sample = jnp.stack(pool_new_s, axis=0)
    k_prompt = jnp.stack(k_new_p, axis=0)
    v_prompt = jnp.stack(v_new_p, axis=0)
    k_sample = jnp.stack(k_new_s, axis=0)
    v_sample = jnp.stack(v_new_s, axis=0)
    return (xp, xs, state_pool_prompt, state_pool_sample, k_prompt, v_prompt, k_sample, v_sample)


_drawn_inputs = setup_inputs


def setup_inputs(seed=0):
    import zlib

    import numpy as np

    out = dict(_drawn_inputs(seed))
    spreads = {}
    factors = {'attn_q_gain': 6.623, 'attn_k_gain': 3.13, 'moe_b_r1': 3.589, 'attn_rel_bias': 2.718}
    for name, (base, spread) in spreads.items():
        noise = np.random.default_rng([zlib.crc32(name.encode()), seed]).standard_normal(out[name].shape)
        drawn = base * np.exp(spread * noise) if base else spread * noise
        out[name] = __import__('jax').numpy.asarray(drawn.astype(out[name].dtype))
    for name, factor in factors.items():
        out[name] = (out[name] * factor).astype(out[name].dtype)
    return out
```

```python
from contextlib import ExitStack

import numpy as np

import concourse.bass as bass
from concourse import mybir

P = 128
F32 = mybir.dt.float32
I32 = mybir.dt.int32
ALU = mybir.AluOpType
ACT = mybir.ActivationFunctionType
AX = mybir.AxisListType

EPS = 1e-6
POOL_WINDOWS = (2, 4, 8, 16)
HIST = max(POOL_WINDOWS) - 1
HALO = 16
BLK = 64
NEG = -1e30
PAD = 4096.0
CHUNK = 64
REL_MAX = 256


def shape_constants(T, NT, NB, NEXP, EPG, NG):
    cols, parts = {}, []

    def put(name, a):
        a = np.asarray(a, np.float32)
        if a.ndim == 1:
            a = np.broadcast_to(a, (P, a.size))
        a = a.reshape(P, -1)
        at = sum(x.shape[1] for x in parts)
        cols[name] = (at, a.shape[1])
        parts.append(a)

    p = np.arange(P)
    put("ident", np.eye(P))
    put("flip", np.eye(P)[::-1])
    put("flip_sample", np.eye(P)[::-1][P - 32:, :].repeat(4, 0) * 0 + np.where(
        (p[:, None] < 32) & (p[None, :] == 31 - p[:, None]), 1.0, 0.0))
    put("before", p[:, None] < p[None, :])
    put("ones", np.ones((P, P)))
    d = p[None, :] - p[:, None]
    for g, w in enumerate(POOL_WINDOWS):
        inside = (d >= 0) & (d < w)
        put(f"band{g}", inside / np.float32(w) - np.eye(P))
        put(f"band_first{g}", inside / np.minimum(p + 1, w)[None, :].astype(np.float32) - np.eye(P))
        put(f"band_halo{g}", ((d + P < w)[:, :HALO]) / np.float32(w))
    tok = np.arange(NT)[None, :] * P + p[:, None]
    put("valid", tok < T)
    put("token", tok - PAD)
    put("row0", 2 * tok - PAD)
    put("row1", 2 * tok + 1 - PAD)
    put("rank_group", NG - np.arange(NG))
    put("rank_expert", EPG - np.arange(EPG))
    put("iota_expert", np.arange(NEXP))
    put("iota_slot", np.arange(BLK))
    put("iota_block", np.arange(NB))
    put("steps", BLK * (1 + np.arange(-(-T // BLK))))
    put("eps", np.full(1, EPS))
    return np.ascontiguousarray(np.concatenate(parts, 1)), cols


def encoder(nc, A, O, cols):
    S, D = A["x_prompt"].shape[1:]
    SS = A["x_sample"].shape[1]
    T = S + SS
    NT = -(-T // P)
    ROWS = [P] * (NT - 1) + [SS]
    assert S == (NT - 1) * P and SS == 32 and T == S + SS
    KT = D // P
    NH, HD = A["cache_k"].shape[3:]
    PAIRS = NH // 2
    KEEP = A["cache_k"].shape[2]
    L, NEXP, _, FE = A["moe_w_gate"].shape
    FT = FE // P
    NG = A["moe_w_r1"].shape[2]
    EPG = A["moe_w_r2"].shape[3]
    NR = NG + NEXP
    OVF = (2 * T - 1) // BLK
    NB = NEXP + OVF
    STEPS = -(-T // BLK)
    PW = D // len(POOL_WINDOWS)
    XROWS, YROWS = T, 2 * T
    SLOTS = 6
    SLOT = KT * 512
    assert FE == 512 and FT * D == SLOT and KEEP == P
    ATT_PIECES = 3 * D // 512 + D // 512
    QKV_PIECES = 3 * D // 512

    xn_dram = [nc.dram_tensor(f"xn{l}", (XROWS, D), F32, kind="Internal").ap() for l in range(L)]
    yb_dram = [nc.dram_tensor(f"yb{l}", (YROWS, D), F32, kind="Internal").ap() for l in range(L)]

    ctx = ExitStack()
    with ctx:
        def sb(name, shape, dt=F32):
            return ctx.enter_context(nc.sbuf_tensor(name, shape, dt))

        def sem(name):
            return ctx.enter_context(nc.semaphore(name))

        def per_layer(name):
            return [sem(f"{name}_{l}") for l in range(L)]

        ring = sb("ring", [P, SLOTS, SLOT])
        x = sb("x", [P, NT, D])
        nat = sb("nat", [P, NT * D])
        hT = sb("hT", [P, KT, T])
        qk = sb("qk", [P, 2, KT * T])
        gain = sb("gain", [P, D])
        cst = sb("cst", [P, A["consts"].shape[1]])
        qk_gain = sb("qk_gain", [P, 2, HD])
        ssq = sb("ssq", [P, 4, NT])
        std = sb("std", [P, 4, NT])
        rstd = sb("rstd", [P, 4, NT])
        idx_gather = sb("idx_gather", [BLK, NB], I32)
        idx_scatter = sb("idx_scatter", [BLK, NB], I32)
        slot_gate = sb("slot_gate", [BLK, NB])
        ovf_expert = sb("ovf_expert", [1, OVF], I32)
        ovf_count = sb("ovf_count", [1, 1], I32)
        gcol = [sb(f"gcol{u}", [BLK, 1], I32) for u in range(2)]
        scol = [sb(f"scol{u}", [BLK, 1], I32) for u in range(2)]
        ps = ctx.enter_context(nc.psum_tensor("ps", [P, 8, 512], F32))

        def const(name, rows=P):
            at, n = cols[name]
            return cst[0:rows, at:at + n]

        ident = const("ident")

        pool_h = nat[:, :].rearrange("p (i d) -> p i d", i=NT)
        v_nat = pool_h
        xg = [nat[0:BLK, u * D:(u + 1) * D] for u in range(2)]
        yb = [nat[0:BLK, (2 + u) * D:(3 + u) * D] for u in range(2)]
        yc = [nat[:, 2 * u * D:2 * (u + 1) * D] for u in range(2)]
        qk_flat = qk[:, :, :].rearrange("p a n -> p (a n)")
        qT = qk[:, 0, :].rearrange("p (c t) -> p c t", c=PAIRS)
        kT = qk[:, 1, :].rearrange("p (c t) -> p c t", c=PAIRS)
        rows_h = qk_flat[:, 0:NT * D].rearrange("p (i d) -> p i d", i=NT)
        at = NT * D
        xT = [qk_flat[:, at + u * KT * BLK:at + (u + 1) * KT * BLK].rearrange("p (k s) -> p k s", k=KT)
              for u in range(2)]
        at += 2 * KT * BLK
        silu = [qk_flat[:, at + u * FT * BLK:at + (u + 1) * FT * BLK] for u in range(2)]
        at += 2 * FT * BLK
        hidden = [qk_flat[:, at + u * FT * BLK:at + (u + 1) * FT * BLK] for u in range(2)]
        at += 2 * FT * BLK
        route_at = at
        pool_gain = qk_flat[:, 0:D]
        pool_scale = qk_flat[:, D:2 * D]
        hist = qk_flat[:, 2 * D:3 * D]
        band_w = qk_flat[:, 3 * D:3 * D + 2 * PW * len(POOL_WINDOWS)].rearrange(
            "p (c n) -> p c n", c=2 * len(POOL_WINDOWS))
        y_tmp = qk_flat[:, 3 * D + 2 * PW * len(POOL_WINDOWS):4 * D + 2 * PW * len(POOL_WINDOWS)]
        assert 4 * D + 2 * PW * len(POOL_WINDOWS) <= 2 * KT * T

        taken = {"nat": 0, "qk": route_at}

        def scratch(where, *shape):
            n = int(np.prod(shape))
            flat = nat[:, :] if where == "nat" else qk_flat
            a = flat[:, taken[where]:taken[where] + n]
            taken[where] += n
            assert taken[where] <= (NT * D if where == "nat" else 2 * KT * T), where
            if len(shape) == 2:
                a = a.rearrange("p (a b) -> p a b", a=shape[0])
            if len(shape) == 3:
                a = a.rearrange("p (a b c) -> p a b c", a=shape[0], b=shape[1])
            return a

        r = {}
        for name in ("m1", "s1", "pg", "kk", "ma", "mb", "dg", "eg", "den", "rden", "pad"):
            r[name] = scratch("nat", NT)
        for k in range(2):
            for name in ("gate", "pos", "exp", "off", "step", "slot", "blk", "is0"):
                r[f"{name}{k}"] = scratch("nat", NT)
            r[f"A{k}"] = scratch("nat", NT, NEXP)
            r[f"S{k}"] = scratch("nat", NT, BLK)
            r[f"V{k}"] = scratch("nat", NT, 3, NB)
        r["logit"] = scratch("nat", NT, NR)
        for name in ("d1", "e1", "eq1", "oh1"):
            r[name] = scratch("nat", NT, NG)
        for name in ("l2", "l2b", "eq2", "a0", "a1"):
            r[name] = scratch("nat", NT, EPG)
        r["tmp"] = scratch("qk", max(NT * max(NEXP, NB, STEPS), NEXP * STEPS, OVF * NEXP))
        r["tmp2"] = scratch("qk", max(NT * NB, OVF * NEXP))
        r["M"] = scratch("nat", NT, NEXP)
        r["C"] = scratch("nat", NT + 1, NEXP)
        for name in ("extra", "incl", "offs"):
            r[name] = scratch("nat", NEXP)
        r["bias"] = sb("router_bias", [P, NR])[:, :]
        rw = sb("rw", [P, KT, NR])

        a4 = ring[:, SLOTS - 2, :]
        a5 = ring[:, SLOTS - 1, :]
        kcT = a4[:, 0:PAIRS * KEEP].rearrange("p (c t) -> p c t", c=PAIRS)
        v_cache = a4[:, D:2 * D]
        o_nat = [a4[:, 2 * D + u * NT * P:2 * D + (u + 1) * NT * P].rearrange("p (i c) -> p i c", i=NT)
                 for u in range(2)]
        small = a4[:, 2 * D + 2 * NT * P:2 * D + 2 * NT * P + 64]
        bias_h = [a5[:, u * 512:(u + 1) * 512] for u in range(2)]
        s_sb = [a5[:, (2 + u) * 512:(3 + u) * 512] for u in range(2)]
        p_sb = [a5[:, (4 + u) * 512:(5 + u) * 512] for u in range(2)]
        pT_sb = [a5[:, (6 + u) * 512:(7 + u) * 512] for u in range(2)]
        k_cache_nat = a5[:, 1024:2048]
        sq = [nat[:, u * 512:(u + 1) * 512] for u in range(2)]
        qn = [nat[:, (2 + u) * 512:(3 + u) * 512] for u in range(4)]
        qstat = nat[:, 6 * 512:6 * 512 + 64]

        x_in = [sem(f"x_in{i}") for i in range(NT)]
        hist_zero = sem("hist_zero")
        hist_in = sem("hist_in")
        consts_in = sem("consts_in")
        pool_gain_in = sem("pool_gain_in")
        pool_scale_in = sem("pool_scale_in")
        pool_w_in = sem("pool_w_in")
        gain_in = [sem(f"gain_in{n}") for n in range(3)]
        router_in = per_layer("router_in")
        piece_in = [sem(f"piece_in{s}") for s in range(SLOTS)]
        pieces_used = sem("pieces_used")
        act_own = sem("act_own")
        dve_own = sem("dve_own")
        std_ready = sem("std_ready")
        h_ready = sem("h_ready")
        delta_ps = sem("delta_ps")
        delta_sb = sem("delta_sb")
        pool_y = sem("pool_y")
        x_mixed = per_layer("x_mixed")
        state_out = sem("state_out")
        hT_ps = sem("hT_ps")
        hT_sb = sem("hT_sb")
        xn_stored = per_layer("xn_stored")
        logit_ps = sem("logit_ps")
        logit_sb = sem("logit_sb")
        route_exp_in = sem("route_exp_in")
        route_exp = sem("route_exp")
        chosen = sem("chosen")
        ranks_ps = sem("ranks_ps")
        slots_ready = sem("slots_ready")
        table_ps = sem("table_ps")
        table_sb = sem("table_sb")
        xg_zero = sem("xg_zero")
        col_set = per_layer("col_set")
        gathered = [[sem(f"gathered{l}_{u}") for u in range(2)] for l in range(L)]
        xT_ps = per_layer("xT_ps")
        xT_sb = per_layer("xT_sb")
        silu_sb = per_layer("silu_sb")
        hidden_sb = per_layer("hidden_sb")
        y_lo = per_layer("y_lo")
        y_hi = per_layer("y_hi")
        scattered = [[sem(f"scattered{l}_{u}") for u in range(2)] for l in range(L)]
        o_piece_in = per_layer("o_piece_in")
        o_col = per_layer("o_col")
        o_gathered = per_layer("o_gathered")
        o_xT_ps = per_layer("o_xT_ps")
        o_xT_sb = per_layer("o_xT_sb")
        o_gu_ps = per_layer("o_gu_ps")
        o_silu = per_layer("o_silu")
        o_hidden = per_layer("o_hidden")
        o_y_ps = per_layer("o_y_ps")
        o_y_lo = per_layer("o_y_lo")
        o_y_hi = per_layer("o_y_hi")
        o_scattered = per_layer("o_scattered")
        yc_in = [[sem(f"yc_in{l}_{u}") for u in range(2)] for l in range(L)]
        x_done = per_layer("x_done")
        qk_gain_in = sem("qk_gain_in")
        raw_ps = sem("raw_ps")
        q_sq = sem("q_sq")
        q_ssq = sem("q_ssq")
        q_std = sem("q_std")
        q_scaled = sem("q_scaled")
        q_gained = sem("q_gained")
        qkT_ps = sem("qkT_ps")
        qkT_sb = sem("qkT_sb")
        v_sb = sem("v_sb")
        k_out = [sem(f"k_out{u}") for u in range(4)]
        v_out = sem("v_out")
        kc_in = sem("kc_in")
        vc_in = sem("vc_in")
        kcT_ps = sem("kcT_ps")
        kcT_sb = sem("kcT_sb")
        bias_in = [sem(f"bias_in{u}") for u in range(2)]
        bias_ready = sem("bias_ready")
        s_ps = sem("s_ps")
        s_biased = sem("s_biased")
        s_max = sem("s_max")
        p_ready = sem("p_ready")
        pT_ps = sem("pT_ps")
        pT_ready = sem("pT_ready")
        o_ps = sem("o_ps")
        o_sb = sem("o_sb")
        oT_ps = sem("oT_ps")
        oT_sb = sem("oT_sb")
        att_y = sem("att_y")
        x_half = sem("x_half")
        out_done = sem("out_done")
        wait_carrier = sem("wait_carrier")

        wg = A["moe_w_gate"].rearrange("l e (p k) f -> (l e) p (k f)", k=KT)
        wu = A["moe_w_up"].rearrange("l e (p k) f -> (l e) p (k f)", k=KT)
        wd = A["moe_w_down"].rearrange("l e (k p) d -> (l e) p k d", p=P)
        wqkv = A["attn_w_qkv"][0].rearrange("(p k) e -> p k e", k=KT)
        wo = A["attn_w_o"][0].rearrange("(k p) d -> p k d", p=P)
        x_rows = A["x_prompt"][0]
        xs_rows = A["x_sample"][0]
        rel_t = A["rel_bias_reversed"]
        REL_W = rel_t.shape[1]

        def x_source(i):
            return x_rows[i * P:(i + 1) * P, :] if i < NT - 1 else xs_rows

        def tok(i):
            return slice(i * P, i * P + ROWS[i])

        FIRST = [0, 3 * NEXP + ATT_PIECES]
        att_first = 3 * NEXP

        def used(l, b, m):
            return b * 3 + (3 * NEXP * l + m + 1)

        GATE, UP, DOWN = range(3)
        XT_BANK, GATE_BANK, UP_BANK, Y_BANK = 0, 1, 2, 3
        S_BANK, PT_BANK, O_BANK, OT_BANK = 0, 2, 4, 6

        block = ctx.enter_context(nc.Block())

        @block.sync
        def _(sp):
            for i in range(NT):
                sp.dma_start(x[0:ROWS[i], i, :], x_source(i)).then_inc(x_in[i], 16)
            sp.dma_start(pool_gain, A["norm_mix"][0:1, :].broadcast_to((P, D))).then_inc(pool_gain_in, 16)
            sp.dma_start(cst[:, :], A["consts"]).then_inc(consts_in, 16)
            sp.wait_ge(hist_zero, 1)
            sp.dma_start(hist[P - HIST:P, :], A["cache_pool"][0, 0]).then_inc(hist_in, 16)
            sp.dma_start(band_w, A["pool_w"][0].rearrange("g (k p) n -> p (g k) n", p=P)).then_inc(pool_w_in, 16)
            sp.dma_start(pool_scale, A["pool_scale"][0:1, :].broadcast_to((P, D))).then_inc(pool_scale_in, 16)
            sp.dma_start(gain[:, :], A["norm_ffn"][0:1, :].broadcast_to((P, D))).then_inc(gain_in[0], 16)

            def slot_free(n):
                prev = n - SLOTS
                if prev < 0:
                    return
                if prev < att_first:
                    sp.wait_ge(pieces_used, prev + 1)
                elif prev < att_first + QKV_PIECES:
                    sp.wait_ge(raw_ps, NT * (prev - att_first + 1))
                else:
                    sp.wait_ge(att_y, NT * (prev - att_first - QKV_PIECES + 1))

            def expert_piece(e, m, s):
                to = ring[:, s, :]
                src = (wg, wu, wd)[m][bass.ds(e, 1)]
                if m == DOWN:
                    return to.rearrange("p (k d) -> p k d", k=FT), src.rearrange("e p k d -> (e p) k d")
                return to, src.rearrange("e p n -> (e p) n")

            for l in range(L):
                first = FIRST[l]
                for b in range(2):
                    for m in range(3):
                        n = first + 3 * b + m
                        s = n % SLOTS
                        slot_free(n)
                        if l == 1 and s == SLOTS - 2:
                            sp.wait_ge(oT_sb, PAIRS)
                        to, src = expert_piece(l * NEXP + b, m, s)
                        sp.dma_start(to, src).then_inc(piece_in[s], 16)
                with sp.Fori(1, NEXP // 2) as it:
                    for u in range(2):
                        for m in range(3):
                            s = (first + 3 * u + m) % SLOTS
                            to, src = expert_piece(it * 2 + (l * NEXP + u), m, s)
                            sp.wait_ge(pieces_used, used(l, it * 2 + (u - 2), m))
                            sp.dma_start(to, src).then_inc(piece_in[s], 16)
                sp.wait_ge(table_sb, l + 1)
                n_ovf = sp.value_load(ovf_count[0:1, 0:1], min_val=0, max_val=OVF)
                with sp.If(n_ovf > 0):
                    sp.wait_ge(pieces_used, used(l, NEXP - 1, DOWN))
                    with sp.Fori(0, n_ovf) as j:
                        e = sp.value_load(ovf_expert[0:1, bass.ds(j, 1)], min_val=0, max_val=NEXP - 1)
                        for m in range(3):
                            to, src = expert_piece(e + l * NEXP, m, (first + m) % SLOTS)
                            sp.dma_start(to, src).then_inc(o_piece_in[l], 16)
                        sp.wait_ge(o_y_ps[l], j + 1)
                        sp.sem_inc(wait_carrier, 1)
                if l == 0:
                    for j in range(ATT_PIECES):
                        n = att_first + j
                        slot_free(n)
                        to = ring[:, n % SLOTS, :].rearrange("p (k e) -> p k e", k=KT)
                        src = (wqkv[:, :, j * 512:(j + 1) * 512] if j < QKV_PIECES
                               else wo[:, :, (j - QKV_PIECES) * 512:(j - QKV_PIECES + 1) * 512])
                        sp.dma_start(to, src).then_inc(piece_in[n % SLOTS], 16)

        def piece_count(n):
            return 16 * (n // SLOTS + 1)

        @block.gpsimd
        def _(pool):
            pool.memset(hist, 0.0).then_inc(hist_zero, 1)
            rw1 = lambda l: A["moe_w_r1"][l].rearrange("(p k) g -> p k g", k=KT)
            rw2 = lambda l, g: A["moe_w_r2"][l, g].rearrange("(p k) e -> p k e", k=KT)

            def load_router(l):
                pool.dma_start(rw[:, :, 0:NG], rw1(l)).then_inc(router_in[l], 16)
                for g in range(NG):
                    pool.dma_start(rw[:, :, NG + g * EPG:NG + (g + 1) * EPG], rw2(l, g)).then_inc(router_in[l], 16)
                pool.dma_start(r["bias"][:, 0:NG], A["moe_b_r1"][l:l + 1, :].broadcast_to((P, NG))).then_inc(router_in[l], 16)
                pool.dma_start(r["bias"][:, NG:NR], A["moe_b_r2"][l:l + 1].rearrange("o g e -> o (g e)").broadcast_to((P, NEXP))).then_inc(router_in[l], 16)

            def block_io(l, b, u, count, first=False, last=False):
                if not last:
                    v = 1 - u
                    if not (first and v == 1):
                        pool.wait_ge(gathered[l][v], (count + u) * 16)
                    pool.tensor_copy(gcol[v][:, :], idx_gather[:, bass.ds(b + 1, 1)]).then_inc(col_set[l], 1)
                    pool.wait_ge(col_set[l], 2 * b + 2)
                    if not (first and v == 1):
                        pool.wait_ge(xT_ps[l], b)
                    pool.sem_inc(wait_carrier, 1)
                    pool.indirect_dma_start(
                        out=xg[v], out_offset=None, in_=xn_dram[l],
                        in_offset=bass.IndirectOffsetOnAxis(ap=gcol[v][:, :], axis=0),
                        bounds_check=XROWS - 1, oob_is_err=False).then_inc(gathered[l][v], 16)
                if not first:
                    pool.wait_ge(scattered[l][u], count * 16)
                pool.tensor_copy(scol[u][:, :], idx_scatter[:, bass.ds(b, 1)]).then_inc(col_set[l], 1)
                pool.wait_ge(col_set[l], 2 * b + (2 if last else 3))
                pool.wait_ge(y_lo[l], b + 1)
                pool.wait_ge(y_hi[l], b + 1)
                pool.sem_inc(wait_carrier, 1)
                pool.indirect_dma_start(
                    out=yb_dram[l], out_offset=bass.IndirectOffsetOnAxis(ap=scol[u][:, :], axis=0),
                    in_=yb[u], in_offset=None,
                    bounds_check=YROWS - 1, oob_is_err=False).then_inc(scattered[l][u], 16)

            def experts(l):
                pool.wait_ge(table_sb, l + 1)
                for u in range(2):
                    last = pool.memset(xg[u], 0.0)
                last.then_inc(xg_zero, 1)
                pool.tensor_copy(gcol[0][:, :], idx_gather[:, 0:1]).then_inc(col_set[l], 1)
                pool.wait_ge(xg_zero, l + 1)
                pool.wait_ge(col_set[l], 1)
                pool.wait_ge(xn_stored[l], 16 * NT)
                pool.sem_inc(wait_carrier, 1)
                pool.indirect_dma_start(
                    out=xg[0], out_offset=None, in_=xn_dram[l],
                    in_offset=bass.IndirectOffsetOnAxis(ap=gcol[0][:, :], axis=0),
                    bounds_check=XROWS - 1, oob_is_err=False).then_inc(gathered[l][0], 16)
                block_io(l, 0, 0, 0, first=True)
                block_io(l, 1, 1, 0, first=True)
                with pool.Fori(1, NEXP // 2 - 1) as it:
                    for u in range(2):
                        block_io(l, it * 2 + u, u, it)
                block_io(l, NEXP - 2, 0, NEXP // 2 - 1)
                block_io(l, NEXP - 1, 1, NEXP // 2 - 1, last=True)
                n_ovf = pool.value_load(ovf_count[0:1, 0:1], min_val=0, max_val=OVF)
                with pool.If(n_ovf > 0):
                    for u in range(2):
                        pool.wait_ge(gathered[l][u], 16 * (NEXP // 2))
                        pool.wait_ge(scattered[l][u], 16 * (NEXP // 2))
                    pool.wait_ge(xT_ps[l], NEXP)
                    with pool.Fori(0, n_ovf) as j:
                        pool.tensor_copy(gcol[0][:, :], idx_gather[:, bass.ds(j + NEXP, 1)]).then_inc(o_col[l], 1)
                        pool.tensor_copy(scol[0][:, :], idx_scatter[:, bass.ds(j + NEXP, 1)]).then_inc(o_col[l], 1)
                        pool.wait_ge(o_col[l], 2 * j + 2)
                        pool.sem_inc(wait_carrier, 1)
                        pool.indirect_dma_start(
                            out=xg[0], out_offset=None, in_=xn_dram[l],
                            in_offset=bass.IndirectOffsetOnAxis(ap=gcol[0][:, :], axis=0),
                            bounds_check=XROWS - 1, oob_is_err=False).then_inc(o_gathered[l], 16)
                        pool.wait_ge(o_y_lo[l], j + 1)
                        pool.wait_ge(o_y_hi[l], j + 1)
                        pool.sem_inc(wait_carrier, 1)
                        pool.indirect_dma_start(
                            out=yb_dram[l], out_offset=bass.IndirectOffsetOnAxis(ap=scol[0][:, :], axis=0),
                            in_=yb[0], in_offset=None,
                            bounds_check=YROWS - 1, oob_is_err=False).then_inc(o_scattered[l], 16)
                        pool.wait_ge(o_scattered[l], j * 16 + 16)
                        pool.sem_inc(wait_carrier, 1)
                for u in range(2):
                    pool.wait_ge(scattered[l][u], 16 * (NEXP // 2))

            def combine_loads(l):
                for i in range(NT):
                    if i >= 2:
                        pool.wait_ge(x_done[l], i - 1)
                    n = ROWS[i]
                    pool.dma_start(yc[i % 2][0:n, :], yb_dram[l][2 * i * P:2 * (i * P + n), :].rearrange(
                        "(t k) d -> t (k d)", k=2)).then_inc(yc_in[l][i % 2], 16)

            load_router(0)
            experts(0)
            combine_loads(0)
            load_router(1)

            units = (QKV_PIECES - 2) * NT
            for m in range(units):
                j, i = divmod(m, NT)
                n = ROWS[i]
                if m == 0:
                    pool.wait_ge(qk_gain_in, 32)
                pool.wait_ge(q_scaled, m + 1)
                v = qn[m % 4][0:n, :].rearrange("p (h d) -> p h d", d=HD)
                g = qk_gain[0:n, j // 2, :].unsqueeze(1).broadcast_to((n, 512 // HD, HD))
                pool.tensor_tensor(v, v, g, ALU.mult).then_inc(q_gained, 1)
                if j >= 2:
                    pool.wait_ge(q_gained, m + 1)
                    half = slice((j - 2) * 512, (j - 1) * 512)
                    dst = (O[4][0, 0].rearrange("t h d -> t (h d)")[i * P:(i + 1) * P, half] if i < NT - 1
                           else O[6][0, 0].rearrange("t h d -> t (h d)")[:, half])
                    pool.dma_start(dst, qn[m % 4][0:n, :]).then_inc(k_out[m % 4], 16)
            for m in range(2 * NT):
                j, i = divmod(m, NT)
                n = ROWS[i]
                half = slice(j * 512, (j + 1) * 512)
                pool.wait_ge(v_sb, m + 1)
                dst = (O[5][0, 0].rearrange("t h d -> t (h d)")[i * P:(i + 1) * P, half] if i < NT - 1
                       else O[7][0, 0].rearrange("t h d -> t (h d)")[:, half])
                pool.dma_start(dst, v_nat[0:n, i, half]).then_inc(v_out, 16)
            pool.wait_ge(raw_ps, NT * QKV_PIECES)
            pool.dma_start(k_cache_nat, A["cache_k"][0, 0].rearrange("t h d -> t (h d)")).then_inc(kc_in, 16)
            pool.dma_start(v_cache, A["cache_v"][0, 0].rearrange("t h d -> t (h d)")).then_inc(vc_in, 16)
            for h in range(NH):
                if h >= 2:
                    pool.wait_ge(s_biased, NT * (h - 1))
                pool.dma_start(bias_h[h % 2], bass.AP(tensor=rel_t.tensor, offset=h * REL_W,
                                                      ap=[[1, P], [1, 512]])).then_inc(bias_in[h % 2], 16)
            experts(1)
            combine_loads(1)
            for i in range(NT):
                pool.wait_ge(x_done[1], i + 1)
                dst = O[0][0, i * P:(i + 1) * P, :] if i < NT - 1 else O[1][0]
                pool.dma_start(dst, x[0:ROWS[i], i, :]).then_inc(out_done, 16)
            pool.wait_ge(out_done, 16 * NT)
            for u in range(4):
                n_k = len([m for m in range(2 * NT, 4 * NT) if m % 4 == u])
                pool.wait_ge(k_out[u], 16 * n_k)
            pool.wait_ge(state_out, 32)

        @block.scalar
        def _(act):
            own = [0]

            def link(ins):
                own[0] += 1
                ins.then_inc(act_own, 1)
                act.wait_ge(act_own, own[0])

            def root_mean_square(ph, i, out):
                n = ROWS[i]
                link(act.activation(out, x[0:n, i, :], ACT.Square, accum_out=ssq[0:n, ph, i:i + 1]))
                act.activation(std[0:n, ph, i:i + 1], ssq[0:n, ph, i:i + 1], ACT.Sqrt,
                               bias=const("eps", n), scale=1.0 / D).then_inc(std_ready, 1)

            def transpose_out(ph, i):
                n = ROWS[i]
                act.wait_ge(hT_ps, (ph - 1) * NT + i + 1)
                b = 2 * (i % 2)
                act.activation(hT[:, 0:KT, i * P:i * P + n],
                               ps[:, b:b + 2, :].rearrange("p b (c t) -> p (b c) t", c=4)[:, :, 0:n],
                               ACT.Copy).then_inc(hT_sb, 1)

            act.wait_ge(consts_in, 16)
            for i in range(NT):
                act.wait_ge(x_in[i], 16)
                root_mean_square(0, i, pool_h[0:ROWS[i], i, :])
            act.wait_ge(h_ready, NT)
            act.dma_start(O[2][0, 0], pool_h[P - HIST:P, NT - 2, :]).then_inc(state_out, 16)
            act.dma_start(O[3][0, 0], pool_h[SS - HIST:SS, NT - 1, :]).then_inc(state_out, 16)
            for i in range(NT):
                n = ROWS[i]
                act.wait_ge(delta_ps, i + 1)
                b = 2 * (i % 2)
                act.activation(hT[:, 0:KT, i * P:i * P + n],
                               ps[:, b:b + 2, :].rearrange("p b (c t) -> p (b c) t", c=4)[:, :, 0:n],
                               ACT.Copy).then_inc(delta_sb, 1)

            def route_rows(l):
                ph = 1 + 2 * l
                for i in range(NT + 1):
                    if i < NT:
                        act.wait_ge(x_mixed[l], i + 1)
                        if i == 0 and l == 0:
                            act.wait_ge(x_mixed[0], NT)
                        root_mean_square(ph, i, rows_h[0:ROWS[i], i, :])
                    if i > 0:
                        k = i - 1
                        act.wait_ge(h_ready, ph * NT + k + 1)
                        act.dma_start(xn_dram[l][k * P:k * P + ROWS[k], :],
                                      rows_h[0:ROWS[k], k, :]).then_inc(xn_stored[l], 16)
                        transpose_out(ph, k)
                if l == 0:
                    act.dma_start(gain[:, :], A["norm_mix"][1:2, :].broadcast_to((P, D))).then_inc(gain_in[1], 16)
                act.wait_ge(route_exp_in, l * 2 + 1)
                act.activation(r["e1"], r["d1"], ACT.Exp).then_inc(route_exp, 1)
                act.wait_ge(route_exp_in, l * 2 + 2)
                act.activation(r["eg"], r["dg"], ACT.Exp).then_inc(route_exp, 1)

            def xT_out(l, b, u):
                act.wait_ge(xT_ps[l], b + 1)
                act.activation(xT[u], ps[:, XT_BANK, :].rearrange("p (k s) -> p k s", k=KT), ACT.Copy).then_inc(xT_sb[l], 1)

            def experts(l):
                xT_out(l, 0, 0)

                def body(b, u, count, first, last):
                    act.wait_ge(pieces_used, used(l, b, GATE))
                    if not first:
                        act.wait_ge(hidden_sb[l], b - 1)
                    act.activation(silu[u], ps[:, GATE_BANK, 0:FT * BLK], ACT.Silu).then_inc(silu_sb[l], 1)
                    if not last:
                        xT_out(l, b + 1, 1 - u)
                    act.wait_ge(pieces_used, used(l, b, DOWN))
                    if not first:
                        act.wait_ge(scattered[l][u], count * 16)
                    act.activation(yb[u][:, 0:512], ps[0:BLK, Y_BANK, :], ACT.Copy,
                                   scale=slot_gate[:, bass.ds(b, 1)]).then_inc(y_lo[l], 1)

                body(0, 0, 0, True, False)
                body(1, 1, 0, True, False)
                with act.Fori(1, NEXP // 2 - 1) as it:
                    for u in range(2):
                        body(it * 2 + u, u, it, False, False)
                body(NEXP - 2, 0, NEXP // 2 - 1, False, False)
                body(NEXP - 1, 1, NEXP // 2 - 1, False, True)
                n_ovf = act.value_load(ovf_count[0:1, 0:1], min_val=0, max_val=OVF)
                with act.If(n_ovf > 0):
                    act.wait_ge(hidden_sb[l], NEXP)
                    with act.Fori(0, n_ovf) as j:
                        act.wait_ge(o_xT_ps[l], j + 1)
                        act.activation(xT[0], ps[:, XT_BANK, :].rearrange("p (k s) -> p k s", k=KT),
                                       ACT.Copy).then_inc(o_xT_sb[l], 1)
                        act.wait_ge(o_gu_ps[l], j + 1)
                        act.activation(silu[0], ps[:, GATE_BANK, 0:FT * BLK], ACT.Silu).then_inc(o_silu[l], 1)
                        act.wait_ge(o_y_ps[l], j + 1)
                        act.activation(yb[0][:, 0:512], ps[0:BLK, Y_BANK, :], ACT.Copy,
                                       scale=slot_gate[:, bass.ds(j + NEXP, 1)]).then_inc(o_y_lo[l], 1)

            route_rows(0)
            experts(0)

            for k in range(2):
                src = A["attn_q_gain" if k == 0 else "attn_k_gain"]
                act.dma_start(qk_gain[:, k, :], src[0:1, :].broadcast_to((P, HD))).then_inc(qk_gain_in, 16)
            for i in range(NT):
                act.wait_ge(x_done[0], i + 1)
                root_mean_square(2, i, rows_h[0:ROWS[i], i, :])
            for i in range(NT):
                transpose_out(2, i)
            act.dma_start(gain[:, :], A["norm_ffn"][1:2, :].broadcast_to((P, D))).then_inc(gain_in[2], 16)
            units = (QKV_PIECES - 2) * NT

            def qkT_out(m):
                j, i = divmod(m, NT)
                n = ROWS[i]
                act.wait_ge(qkT_ps, m + 1)
                dst = (qT if j < 2 else kT)[:, 4 * (j % 2):4 * (j % 2) + 4, i * P:i * P + n]
                act.activation(dst, ps[:, 4 + m % 2, :].rearrange("p (c t) -> p c t", c=4)[:, :, 0:n],
                               ACT.Copy).then_inc(qkT_sb, 1)

            for m in range(units):
                j, i = divmod(m, NT)
                n = ROWS[i]
                act.wait_ge(raw_ps, m + 1)
                if m >= 2:
                    act.wait_ge(q_ssq, m - 1)
                act.activation(sq[m % 2][0:n, :], ps[0:n, m % 4, :], ACT.Square).then_inc(q_sq, 1)
                act.wait_ge(q_ssq, m + 1)
                c = 24 * (m % 2)
                act.activation(qstat[0:n, c + 8:c + 16], qstat[0:n, c:c + 8], ACT.Sqrt,
                               bias=const("eps", n), scale=1.0 / HD).then_inc(q_std, 1)
                if m >= 2:
                    qkT_out(m - 2)
            qkT_out(units - 2)
            qkT_out(units - 1)
            for m in range(2 * NT):
                j, i = divmod(m, NT)
                n = ROWS[i]
                act.wait_ge(raw_ps, units + m + 1)
                if m == 0:
                    for u in range(4):
                        act.wait_ge(k_out[u], 16 * len([q for q in range(2 * NT, 4 * NT) if q % 4 == u]))
                act.activation(v_nat[0:n, i, j * 512:(j + 1) * 512], ps[0:n, (units + m) % 4, :],
                               ACT.Copy).then_inc(v_sb, 1)
            for c in range(2):
                act.wait_ge(kcT_ps, c + 1)
                act.activation(kcT[:, 4 * c:4 * c + 4, :], ps[:, 4 + c, :].rearrange("p (c t) -> p c t", c=4),
                               ACT.Copy).then_inc(kcT_sb, 1)

            UNITS = NH * NT
            for t in range(UNITS + 4):
                if t < UNITS:
                    i = t % NT
                    n = ROWS[i]
                    nk = (i + 1) * P if i < NT - 1 else KEEP + SS
                    c = 4 * (t % 4)
                    act.wait_ge(s_max, t + 1)
                    if t >= 2:
                        act.wait_ge(pT_ps, t - 1)
                    act.activation(p_sb[t % 2][0:n, 0:nk], s_sb[t % 2][0:n, 0:nk], ACT.Exp,
                                   bias=small[0:n, c + 1:c + 2], accum_out=small[0:n, c + 2:c + 3]).then_inc(p_ready, 1)
                if t >= 3 and (t - 3) % (2 * NT) == 2 * NT - 1:
                    pr = (t - 3) // (2 * NT)
                    act.wait_ge(oT_ps, pr + 1)
                    act.activation(hT[:, pr, 0:S], ps[:, 6, :], ACT.Copy)
                    act.activation(hT[:, pr, S:T], ps[:, 7, 0:SS], ACT.Copy).then_inc(oT_sb, 1)
            route_rows(1)
            experts(1)

        @block.vector
        def _(dve):
            own = [0]

            def link(ins):
                own[0] += 1
                ins.then_inc(dve_own, 1)
                dve.wait_ge(dve_own, own[0])

            V = nc.vector

            def normalise(ph, i, out, g):
                n = ROWS[i]
                dve.wait_ge(std_ready, ph * NT + i + 1)
                link(V.reciprocal(rstd[0:n, ph, i:i + 1], std[0:n, ph, i:i + 1]))
                V.scalar_tensor_tensor(out=out, in0=x[0:n, i, :], scalar=rstd[0:n, ph, i:i + 1], in1=g[0:n, :],
                                       op0=ALU.mult, op1=ALU.mult).then_inc(h_ready, 1)

            dve.wait_ge(pool_gain_in, 16)
            for i in range(NT):
                normalise(0, i, pool_h[0:ROWS[i], i, :], pool_gain)
            dve.wait_ge(pool_scale_in, 16)
            for i in range(NT):
                n = ROWS[i]
                dve.wait_ge(pool_y, i + 1)
                b = 4 + 2 * (i % 2)
                link(V.tensor_tensor(y_tmp[0:n, :], ps[0:n, b:b + 2, :].rearrange("p b c -> p (b c)"),
                                     pool_scale[0:n, :], ALU.mult))
                ins = V.tensor_tensor(x[0:n, i, :], x[0:n, i, :], y_tmp[0:n, :], ALU.add)
                ins.then_inc(x_mixed[0], 1)
                dve.wait_ge(x_mixed[0], i + 1)

            def bc(a, shape, axis):
                return a.unsqueeze(axis).broadcast_to(shape)

            def route(l):
                ph = 1 + 2 * l
                lg = r["logit"]
                if l == 0:
                    dve.wait_ge(state_out, 32)
                else:
                    dve.wait_ge(v_out, 16 * 2 * NT)
                link(V.memset(lg, 0.0))
                dve.wait_ge(gain_in[2 * l], 16)
                for i in range(NT):
                    normalise(ph, i, rows_h[0:ROWS[i], i, :], gain)
                dve.wait_ge(router_in[l], 16 * (NG + 3))
                for i in range(NT):
                    n = ROWS[i]
                    dve.wait_ge(logit_ps, l * NT + i + 1)
                    ins = V.tensor_tensor(lg[0:n, i, :], ps[0:n, 4 + i % 2, 0:NR], r["bias"][0:n, :], ALU.add)
                    ins.then_inc(logit_sb, 1)
                dve.wait_ge(logit_sb, l * NT + NT)
                l1 = lg[:, :, 0:NG]
                sg = (P, NT, NG)
                se = (P, NT, EPG)
                sx = (P, NT, NEXP)
                link(V.reduce_max(r["m1"], l1, AX.X))
                ins = V.tensor_tensor(r["d1"], l1, bc(r["m1"], sg, 2), ALU.subtract)
                ins.then_inc(route_exp_in, 1)
                link(V.tensor_tensor(r["eq1"], l1, bc(r["m1"], sg, 2), ALU.is_equal))
                link(V.tensor_tensor(r["eq1"], r["eq1"], bc(const("rank_group"), sg, 1), ALU.mult))
                link(V.reduce_max(r["kk"], r["eq1"], AX.X))
                link(V.tensor_tensor(r["oh1"], r["eq1"], bc(r["kk"], sg, 2), ALU.is_equal))
                link(V.tensor_tensor(r["oh1"], r["oh1"], bc(const("valid"), sg, 2), ALU.mult))
                t4 = r["tmp"][:, 0:NT * NEXP].rearrange("p (i g e) -> p i g e", i=NT, g=NG)
                l2g = lg[:, :, NG:NR].rearrange("p i (g e) -> p i g e", g=NG)
                oh4 = r["oh1"].unsqueeze(3).broadcast_to((P, NT, NG, EPG))
                link(V.tensor_tensor(t4, l2g, oh4, ALU.mult))
                link(V.reduce_sum(r["l2"], t4.rearrange("p i g e -> p i e g"), AX.X))
                src = r["l2"]
                for k in range(2):
                    m = r["ma" if k == 0 else "mb"]
                    link(V.reduce_max(m, src, AX.X))
                    link(V.tensor_tensor(r["eq2"], src, bc(m, se, 2), ALU.is_equal))
                    link(V.tensor_tensor(r["eq2"], r["eq2"], bc(const("rank_expert"), se, 1), ALU.mult))
                    link(V.reduce_max(r["kk"], r["eq2"], AX.X))
                    link(V.tensor_tensor(r[f"a{k}"], r["eq2"], bc(r["kk"], se, 2), ALU.is_equal))
                    if k == 0:
                        link(V.scalar_tensor_tensor(out=r["l2b"], in0=r["a0"], scalar=NEG, in1=r["l2"],
                                                    op0=ALU.mult, op1=ALU.add))
                        src = r["l2b"]
                V.tensor_tensor(r["dg"], r["mb"], r["ma"], ALU.subtract).then_inc(route_exp_in, 1)
                for k in range(2):
                    a4 = r[f"a{k}"].unsqueeze(2).broadcast_to((P, NT, NG, EPG))
                    link(V.tensor_tensor(r[f"A{k}"].rearrange("p i (g e) -> p i g e", g=NG), a4, oh4, ALU.mult))
                V.tensor_tensor(r["M"], r["A0"], r["A1"], ALU.add).then_inc(chosen, 1)
                dve.wait_ge(route_exp, l * 2 + 2)
                link(V.reduce_sum(r["s1"], r["e1"], AX.X))
                link(V.reciprocal(r["pg"], r["s1"]))
                link(V.tensor_scalar(r["den"], r["eg"], 1.0, None, ALU.add))
                link(V.reciprocal(r["rden"], r["den"]))
                link(V.tensor_tensor(r["gate0"], r["pg"], r["rden"], ALU.mult))
                link(V.tensor_tensor(r["gate1"], r["gate0"], r["eg"], ALU.mult))
                dve.wait_ge(ranks_ps, l + 1)
                link(V.tensor_copy(r["C"], ps[:, 0, 0:(NT + 1) * NEXP].rearrange("p (i e) -> p i e", e=NEXP)))
                cnt = r["C"][:, NT, :]
                sc = (P, NEXP, STEPS)
                t = r["tmp"][:, 0:NEXP * STEPS].rearrange("p (e s) -> p e s", e=NEXP)
                link(V.tensor_tensor(t, bc(cnt, sc, 2), bc(const("steps"), sc, 1), ALU.is_gt))
                link(V.reduce_sum(r["extra"], t, AX.X))
                link(V.tensor_tensor_scan(out=r["incl"], data0=const("ones")[:, 0:NEXP], data1=r["extra"],
                                          initial=0.0, op0=ALU.mult, op1=ALU.add))
                link(V.tensor_tensor(r["offs"], r["incl"], r["extra"], ALU.subtract))
                for k in range(2):
                    t = r["tmp"][:, 0:NT * NEXP].rearrange("p (i e) -> p i e", i=NT)
                    for name, w in (("pos", r["C"][:, 0:NT, :]), ("exp", bc(const("iota_expert"), sx, 1)),
                                    ("off", bc(r["offs"], sx, 1))):
                        link(V.tensor_tensor(t, r[f"A{k}"], w, ALU.mult))
                        link(V.reduce_sum(r[f"{name}{k}"], t, AX.X))
                    ts = r["tmp"][:, 0:NT * STEPS].rearrange("p (i s) -> p i s", i=NT)
                    ss = (P, NT, STEPS)
                    link(V.tensor_tensor(ts, bc(r[f"pos{k}"], ss, 2), bc(const("steps"), ss, 1), ALU.is_ge))
                    link(V.reduce_sum(r[f"step{k}"], ts, AX.X))
                    link(V.scalar_tensor_tensor(out=r[f"slot{k}"], in0=r[f"step{k}"], scalar=-float(BLK),
                                                in1=r[f"pos{k}"], op0=ALU.mult, op1=ALU.add))
                    link(V.tensor_scalar(r["pad"], const("valid"), 1.0, PAD, ALU.subtract, ALU.mult))
                    link(V.tensor_tensor(r[f"slot{k}"], r[f"slot{k}"], r["pad"], ALU.add))
                    link(V.tensor_scalar(r[f"is0{k}"], r[f"step{k}"], 0.0, None, ALU.is_equal))
                    link(V.tensor_tensor(r[f"blk{k}"], r[f"off{k}"], r[f"step{k}"], ALU.add))
                    link(V.tensor_scalar(r[f"blk{k}"], r[f"blk{k}"], float(NEXP - 1), None, ALU.add))
                    link(V.tensor_tensor(r[f"exp{k}"], r[f"exp{k}"], r[f"blk{k}"], ALU.subtract))
                    link(V.tensor_tensor(r[f"exp{k}"], r[f"exp{k}"], r[f"is0{k}"], ALU.mult))
                    link(V.tensor_tensor(r[f"blk{k}"], r[f"blk{k}"], r[f"exp{k}"], ALU.add))
                    so, sn = (P, NT, BLK), (P, NT, NB)
                    V.tensor_tensor(r[f"S{k}"], bc(r[f"slot{k}"], so, 2), bc(const("iota_slot"), so, 1), ALU.is_equal)
                    tb = r["tmp2"][:, 0:NT * NB].rearrange("p (i b) -> p i b", i=NT)
                    link(V.tensor_tensor(tb, bc(r[f"blk{k}"], sn, 2), bc(const("iota_block"), sn, 1), ALU.is_equal))
                    for c, val in enumerate((const("token"), const(f"row{k}"), r[f"gate{k}"])):
                        link(V.tensor_tensor(r[f"V{k}"][:, :, c, :], tb, bc(val, sn, 2), ALU.mult))
                so = (P, OVF, NEXP)
                ta = r["tmp"][:, 0:OVF * NEXP].rearrange("p (b e) -> p b e", e=NEXP)
                tb = r["tmp2"][:, 0:OVF * NEXP].rearrange("p (b e) -> p b e", e=NEXP)
                iota_o = bc(const("iota_block")[:, 0:OVF], so, 2)
                ins = V.tensor_tensor(ta, iota_o, bc(r["offs"], so, 1), ALU.is_ge)
                ins.then_inc(slots_ready, 1)
                dve.wait_ge(slots_ready, l + 1)
                link(V.tensor_tensor(tb, iota_o, bc(r["incl"], so, 1), ALU.is_lt))
                link(V.tensor_tensor(ta, ta, tb, ALU.mult))
                link(V.tensor_tensor(ta, ta, bc(const("iota_expert"), so, 1), ALU.mult))
                link(V.reduce_sum(r["extra"][:, 0:OVF], ta, AX.X))
                link(V.tensor_copy(ovf_expert[0:1, :], r["extra"][0:1, 0:OVF]))
                V.tensor_copy(ovf_count[0:1, :], r["incl"][0:1, NEXP - 1:NEXP])
                dve.wait_ge(table_ps, l + 1)
                V.tensor_scalar(idx_gather[:, :], ps[0:BLK, 1, 0:NB], PAD, None, ALU.add)
                V.tensor_scalar(idx_scatter[:, :], ps[0:BLK, 1, NB:2 * NB], PAD, None, ALU.add)
                V.tensor_copy(slot_gate[:, :], ps[0:BLK, 1, 2 * NB:3 * NB]).then_inc(table_sb, 1)

            def experts(l):
                def body(b, u, count, first):
                    dve.wait_ge(pieces_used, used(l, b, UP))
                    dve.wait_ge(silu_sb[l], b + 1)
                    if not first:
                        dve.wait_ge(pieces_used, used(l, b - 2, DOWN))
                    V.tensor_tensor(hidden[u], silu[u], ps[:, UP_BANK, 0:FT * BLK],
                                    ALU.mult).then_inc(hidden_sb[l], 1)
                    dve.wait_ge(pieces_used, used(l, b, DOWN))
                    if not first:
                        dve.wait_ge(scattered[l][u], count * 16)
                    V.tensor_scalar(yb[u][:, 512:D], ps[0:BLK, Y_BANK + 1, :], slot_gate[:, bass.ds(b, 1)], None,
                                    ALU.mult).then_inc(y_hi[l], 1)

                body(0, 0, 0, True)
                body(1, 1, 0, True)
                with dve.Fori(1, NEXP // 2) as it:
                    for u in range(2):
                        body(it * 2 + u, u, it, False)
                n_ovf = dve.value_load(ovf_count[0:1, 0:1], min_val=0, max_val=OVF)
                with dve.If(n_ovf > 0):
                    dve.wait_ge(pieces_used, used(l, NEXP - 1, DOWN))
                    with dve.Fori(0, n_ovf) as j:
                        dve.wait_ge(o_gu_ps[l], j + 1)
                        dve.wait_ge(o_silu[l], j + 1)
                        V.tensor_tensor(hidden[0], silu[0], ps[:, UP_BANK, 0:FT * BLK],
                                        ALU.mult).then_inc(o_hidden[l], 1)
                        dve.wait_ge(o_y_ps[l], j + 1)
                        V.tensor_scalar(yb[0][:, 512:D], ps[0:BLK, Y_BANK + 1, :], slot_gate[:, bass.ds(j + NEXP, 1)], None,
                                        ALU.mult).then_inc(o_y_hi[l], 1)

            def combine(l):
                for i in range(NT):
                    n = ROWS[i]
                    dve.wait_ge(yc_in[l][i % 2], 16 * (i // 2 + 1))
                    link(V.tensor_tensor(x[0:n, i, :], x[0:n, i, :], yc[i % 2][0:n, 0:D], ALU.add))
                    V.tensor_tensor(x[0:n, i, :], x[0:n, i, :], yc[i % 2][0:n, D:2 * D], ALU.add).then_inc(x_done[l], 1)

            route(0)
            experts(0)
            combine(0)

            dve.wait_ge(gain_in[1], 16)
            for i in range(NT):
                normalise(2, i, rows_h[0:ROWS[i], i, :], gain)
            units = (QKV_PIECES - 2) * NT

            def head_sums(m):
                n = ROWS[m % NT]
                dve.wait_ge(q_sq, m + 1)
                c = 24 * (m % 2)
                V.reduce_sum(qstat[0:n, c:c + 8], sq[m % 2][0:n, :].rearrange("p (h d) -> p h d", d=HD),
                             AX.X).then_inc(q_ssq, 1)

            for m in range(units):
                j, i = divmod(m, NT)
                n = ROWS[i]
                head_sums(m)
                c = 24 * (m % 2)
                dve.wait_ge(q_std, m + 1)
                link(V.reciprocal(qstat[0:n, c + 16:c + 24], qstat[0:n, c + 8:c + 16]))
                if m >= 4:
                    dve.wait_ge(qkT_ps, m - 3)
                    if m - 4 >= 2 * NT:
                        n_k = len([q for q in range(2 * NT, m - 3) if q % 4 == m % 4])
                        dve.wait_ge(k_out[m % 4], 16 * n_k)
                V.tensor_tensor(qn[m % 4][0:n, :].rearrange("p (h d) -> p h d", d=HD),
                                ps[0:n, m % 4, :].rearrange("p (h d) -> p h d", d=HD),
                                bc(qstat[0:n, c + 16:c + 24], (n, 512 // HD, HD), 2),
                                ALU.mult).then_inc(q_scaled, 1)

            def scores(h, i):
                a = h * NT + i
                n = ROWS[i]
                nk = (i + 1) * P if i < NT - 1 else KEEP + SS
                m0 = 512 - nk
                if i == 0:
                    dve.wait_ge(bias_in[h % 2], 16 * (h // 2 + 1))
                    link(V.tensor_scalar(bias_h[h % 2], bias_h[h % 2], float(HD) ** 0.5, None, ALU.mult))
                    link(V.memset(bias_h[h % 2][CHUNK:P, 512 - CHUNK:512], NEG))
                dve.wait_ge(s_ps, a + 1)
                if a >= 2:
                    dve.wait_ge(p_ready, a - 1)
                c = 4 * (a % 4)
                V.tensor_tensor_reduce(out=s_sb[a % 2][0:n, 0:nk], in0=ps[0:n, S_BANK + a % 2, 0:nk],
                                       in1=bias_h[h % 2][0:n, m0:512], scale=float(HD) ** -0.5, scalar=-3e38,
                                       op0=ALU.add, op1=ALU.max, accum_out=small[0:n, c:c + 1]).then_inc(s_biased, 1)
                dve.wait_ge(s_biased, a + 1)
                V.tensor_scalar(small[0:n, c + 1:c + 2], small[0:n, c:c + 1], -1.0, None,
                                ALU.mult).then_inc(s_max, 1)

            def pT_out(a):
                i = a % NT
                nk = (i + 1) * P if i < NT - 1 else KEEP + SS
                kt = -(-nk // P)
                n = ROWS[i]
                dve.wait_ge(pT_ps, a + 1)
                if a >= 2:
                    dve.wait_ge(o_ps, a - 1)
                if i < NT - 1:
                    V.tensor_copy(pT_sb[a % 2][:, 0:kt * P], ps[:, PT_BANK + a % 2, 0:kt * P]).then_inc(pT_ready, 1)
                else:
                    V.tensor_copy(pT_sb[a % 2][:, 0:n], ps[:, PT_BANK + a % 2, 0:n])
                    V.tensor_copy(pT_sb[a % 2][0:SS, P:P + n], ps[0:SS, PT_BANK + a % 2, P:P + n]).then_inc(pT_ready, 1)

            def o_out(a):
                h, i = divmod(a, NT)
                n = ROWS[i]
                c = 4 * (a % 4)
                dve.wait_ge(p_ready, a + 1)
                link(V.reciprocal(small[0:n, c + 3:c + 4], small[0:n, c + 2:c + 3]))
                dve.wait_ge(o_ps, a + 1)
                if i == 0 and h % 2 == 0 and h >= 4:
                    dve.wait_ge(oT_ps, h // 2 - 1)
                V.tensor_scalar(o_nat[(h // 2) % 2][0:n, i, (h % 2) * HD:(h % 2 + 1) * HD],
                                ps[0:n, O_BANK + a % 2, 0:HD], small[0:n, c + 3:c + 4], None,
                                ALU.mult).then_inc(o_sb, 1)

            UNITS = NH * NT
            for a in range(UNITS + 3):
                if a < UNITS:
                    scores(*divmod(a, NT))
                if 0 <= a - 1 < UNITS:
                    pT_out(a - 1)
                if 0 <= a - 2 < UNITS:
                    o_out(a - 2)

            for hf in range(2):
                for i in range(NT):
                    n = ROWS[i]
                    m = hf * NT + i
                    dve.wait_ge(att_y, m + 1)
                    ins = V.tensor_tensor(x[0:n, i, hf * 512:(hf + 1) * 512], x[0:n, i, hf * 512:(hf + 1) * 512],
                                          ps[0:n, m % 4, :], ALU.add)
                    ins.then_inc(x_mixed[1] if hf == 1 else x_half, 1)
            route(1)
            experts(1)
            combine(1)

        @block.tensor
        def _(pe):
            mm = nc.tensor.matmul

            def transposes(ph, i):
                n = ROWS[i]
                pe.wait_ge(h_ready, ph * NT + i + 1)
                if i >= 2:
                    pe.wait_ge(hT_sb, (ph - 1) * NT + i - 1)
                src = rows_h[0:n, i, :].rearrange("p (c k) -> p k c", k=KT)
                for k in range(KT):
                    last = nc.tensor.transpose(ps[:, 2 * (i % 2) + k // 4, 128 * (k % 4):128 * (k % 4) + n],
                                               src[:, k, :], ident[0:n, 0:n])
                last.then_inc(hT_ps, 1)

            pe.wait_ge(consts_in, 16)

            def deltas(i):
                n = ROWS[i]
                pe.wait_ge(h_ready, i + 1)
                if i >= 2:
                    pe.wait_ge(delta_sb, i - 1)
                if i == NT - 1:
                    pe.wait_ge(hist_in, 16)
                for c in range(KT):
                    g = c * P // PW
                    out = ps[:, 2 * (i % 2) + c // 4, 128 * (c % 4):128 * (c % 4) + n]
                    band = const(f"band_first{g}" if i == 0 else f"band{g}")
                    last = mm(out, pool_h[0:n, i, c * P:(c + 1) * P], band[0:n, 0:n], start=True, stop=True,
                              skip_group_check=True)
                    if i > 0:
                        prev = pool_h[:, i - 1, :] if i < NT - 1 else hist
                        last = mm(out[:, 0:HALO], prev[:, c * P:(c + 1) * P], const(f"band_halo{g}"),
                                  start=False, stop=True, skip_group_check=True)
                last.then_inc(delta_ps, 1)

            deltas(0)
            pe.wait_ge(pool_w_in, 16)
            for i in range(NT):
                if i + 1 < NT:
                    deltas(i + 1)
                n = ROWS[i]
                pe.wait_ge(delta_sb, i + 1)
                if i >= 2:
                    pe.wait_ge(x_mixed[0], i - 1)
                for g in range(len(POOL_WINDOWS)):
                    out = ps[0:n, 4 + 2 * (i % 2) + g // 2, PW * (g % 2):PW * (g % 2 + 1)]
                    for k in range(2):
                        last = mm(out, hT[:, 2 * g + k, tok(i)], band_w[:, 2 * g + k, :], start=(k == 0), stop=(k == 1))
                last.then_inc(pool_y, 1)

            def route(l):
                ph = 1 + 2 * l
                pe.wait_ge(x_mixed[l], NT)
                transposes(ph, 0)
                pe.wait_ge(router_in[l], 16 * (NG + 3))
                for i in range(NT):
                    if i + 1 < NT:
                        transposes(ph, i + 1)
                    n = ROWS[i]
                    pe.wait_ge(hT_sb, (ph - 1) * NT + i + 1)
                    if i >= 2:
                        pe.wait_ge(logit_sb, l * NT + i - 1)
                    for k in range(KT):
                        last = mm(ps[0:n, 4 + i % 2, 0:NR], hT[:, k, tok(i)], rw[:, k, :], start=(k == 0), stop=(k == KT - 1))
                    last.then_inc(logit_ps, 1)
                pe.wait_ge(chosen, l + 1)
                pe.wait_ge(hT_sb, (ph - 1) * NT + NT)
                M = r["M"]
                mm(ps[:, 0, 0:NT * NEXP], const("before"), M.rearrange("p i e -> p (i e)"), start=True, stop=True,
                   skip_group_check=True)
                for i in range(NT):
                    for k in range(i + 1, NT + 1):
                        last = mm(ps[:, 0, k * NEXP:(k + 1) * NEXP], const("ones"), M[:, i, :],
                                  start=False, stop=True, skip_group_check=True)
                last.then_inc(ranks_ps, 1)
                pe.wait_ge(slots_ready, l + 1)
                for k in range(2):
                    for i in range(NT):
                        last = mm(ps[0:BLK, 1, 0:3 * NB], r[f"S{k}"][:, i, :],
                                  r[f"V{k}"][:, i, :, :].rearrange("p c b -> p (c b)"),
                                  start=(k == 0 and i == 0), stop=(k == 1 and i == NT - 1))
                last.then_inc(table_ps, 1)

            def block_transposes(u):
                src = xg[u].rearrange("s (c k) -> s k c", k=KT)
                for k in range(KT):
                    last = nc.tensor.transpose(ps[:, XT_BANK, k * BLK:(k + 1) * BLK], src[:, k, :], ident[0:BLK, 0:BLK])
                return last

            def product(s, bank, buf):
                w = ring[:, s, :].rearrange("p (k f) -> p k f", k=KT)
                for f in range(FT):
                    for k in range(KT):
                        last = mm(ps[:, bank, f * BLK:(f + 1) * BLK], w[:, k, f * P:(f + 1) * P],
                                  xT[buf][:, k, :], start=(k == 0), stop=(k == KT - 1))
                return last

            def down(u, s):
                w = ring[:, s, :].rearrange("p (k d) -> p k d", k=FT)
                for hf in range(2):
                    for k in range(FT):
                        last = mm(ps[0:BLK, Y_BANK + hf, :], hidden[u][:, k * BLK:(k + 1) * BLK],
                                  w[:, k, hf * 512:(hf + 1) * 512], start=(k == 0), stop=(k == FT - 1))
                return last

            def experts(l):
                first_piece = FIRST[l]

                def body(b, u, count, early, last):
                    def slot_ready(m):
                        n0 = first_piece + 3 * u + m
                        pe.wait_ge(piece_in[n0 % SLOTS], count * 16 + 16 * (n0 // SLOTS + 1))
                        return n0 % SLOTS

                    s = slot_ready(GATE)
                    pe.wait_ge(xT_sb[l], b + 1)
                    if not early:
                        pe.wait_ge(silu_sb[l], b)
                    product(s, GATE_BANK, u).then_inc(pieces_used, 1)
                    s = slot_ready(UP)
                    if not early:
                        pe.wait_ge(hidden_sb[l], b)
                    product(s, UP_BANK, u).then_inc(pieces_used, 1)
                    if not last:
                        pe.wait_ge(gathered[l][1 - u], count * 16 + 16 * (1 + u))
                        pe.sem_inc(wait_carrier, 1)
                        block_transposes(1 - u).then_inc(xT_ps[l], 1)
                    s = slot_ready(DOWN)
                    pe.wait_ge(hidden_sb[l], b + 1)
                    if not early:
                        pe.wait_ge(y_lo[l], b)
                        pe.wait_ge(y_hi[l], b)
                    down(u, s).then_inc(pieces_used, 1)

                pe.wait_ge(table_sb, l + 1)
                pe.wait_ge(gathered[l][0], 16)
                block_transposes(0).then_inc(xT_ps[l], 1)
                body(0, 0, 0, True, False)
                body(1, 1, 0, False, False)
                with pe.Fori(1, NEXP // 2 - 1) as it:
                    for u in range(2):
                        body(it * 2 + u, u, it, False, False)
                body(NEXP - 2, 0, NEXP // 2 - 1, False, False)
                body(NEXP - 1, 1, NEXP // 2 - 1, False, True)
                n_ovf = pe.value_load(ovf_count[0:1, 0:1], min_val=0, max_val=OVF)
                with pe.If(n_ovf > 0):
                    pe.wait_ge(y_lo[l], NEXP)
                    pe.wait_ge(y_hi[l], NEXP)
                    with pe.Fori(0, n_ovf) as j:
                        pe.wait_ge(o_gathered[l], j * 16 + 16)
                        pe.sem_inc(wait_carrier, 1)
                        block_transposes(0).then_inc(o_xT_ps[l], 1)
                        pe.wait_ge(o_xT_sb[l], j + 1)
                        pe.wait_ge(o_piece_in[l], j * 48 + 48)
                        s = first_piece % SLOTS
                        product(s, GATE_BANK, 0)
                        product((s + 1) % SLOTS, UP_BANK, 0).then_inc(o_gu_ps[l], 1)
                        pe.wait_ge(o_hidden[l], j + 1)
                        down(0, (s + 2) % SLOTS).then_inc(o_y_ps[l], 1)

            route(0)
            experts(0)

            pe.wait_ge(x_done[0], NT)
            for i in range(NT):
                transposes(2, i)
            units = (QKV_PIECES - 2) * NT

            def qk_transposes(m):
                j, i = divmod(m, NT)
                n = ROWS[i]
                pe.wait_ge(q_gained, m + 1)
                if m >= 2:
                    pe.wait_ge(qkT_sb, m - 1)
                for c in range(4):
                    out = ps[:, 4 + m % 2, 128 * c:128 * c + n]
                    src = qn[m % 4][0:n, 128 * c:128 * (c + 1)]
                    if j < 2:
                        flip = const("flip") if i < NT - 1 else const("flip_sample")[0:n, 0:n]
                        last = mm(out, src, flip, start=True, stop=True)
                    else:
                        last = nc.tensor.transpose(out, src, ident[0:n, 0:n])
                last.then_inc(qkT_ps, 1)

            pe.wait_ge(hT_sb, (2 - 1) * NT + NT)
            for m in range(QKV_PIECES * NT):
                j, i = divmod(m, NT)
                n = ROWS[i]
                piece = att_first + j
                s = piece % SLOTS
                if i == 0:
                    pe.wait_ge(piece_in[s], piece_count(piece))
                if m >= 4:
                    if m - 4 < units:
                        pe.wait_ge(q_scaled, m - 3)
                    else:
                        pe.wait_ge(v_sb, m - 3 - units)
                w = ring[:, s, :].rearrange("p (k e) -> p k e", k=KT)
                for k in range(KT):
                    last = mm(ps[0:n, m % 4, :], hT[:, k, tok(i)], w[:, k, :], start=(k == 0), stop=(k == KT - 1))
                last.then_inc(raw_ps, 1)
                if 0 <= m - 1 < units:
                    qk_transposes(m - 1)
            pe.wait_ge(kc_in, 16)
            pe.wait_ge(qkT_sb, units)
            for c in range(KT):
                last = nc.tensor.transpose(ps[:, 4 + c // 4, 128 * (c % 4):128 * (c % 4 + 1)],
                                           k_cache_nat[:, c * P:(c + 1) * P], ident)
                if c % 4 == 3:
                    last.then_inc(kcT_ps, 1)
            pe.wait_ge(kcT_sb, 2)
            pe.wait_ge(vc_in, 16)
            pe.wait_ge(v_sb, 2 * NT)

            def scores(a):
                h, i = divmod(a, NT)
                n = ROWS[i]
                lo = HD * (h % 2)
                if a >= 2:
                    pe.wait_ge(s_biased, a - 1)
                q = qT[lo:lo + HD, h // 2, tok(i)]
                if i < NT - 1:
                    last = mm(ps[0:n, S_BANK + a % 2, 0:(i + 1) * P], q, kT[lo:lo + HD, h // 2, 0:(i + 1) * P], start=True, stop=True)
                else:
                    mm(ps[0:n, S_BANK + a % 2, 0:KEEP], q, kcT[lo:lo + HD, h // 2, :], start=True, stop=True)
                    last = mm(ps[0:n, S_BANK + a % 2, KEEP:KEEP + SS], q, kT[lo:lo + HD, h // 2, tok(i)], start=True, stop=True)
                last.then_inc(s_ps, 1)

            def p_transposes(a):
                i = a % NT
                n = ROWS[i]
                nk = (i + 1) * P if i < NT - 1 else KEEP + SS
                pe.wait_ge(p_ready, a + 1)
                if a >= 2:
                    pe.wait_ge(pT_ready, a - 1)
                for k in range(-(-nk // P)):
                    w = min(P, nk - k * P)
                    last = nc.tensor.transpose(ps[0:w, PT_BANK + a % 2, k * P:k * P + n],
                                               p_sb[a % 2][0:n, k * P:k * P + w], ident[0:n, 0:n])
                last.then_inc(pT_ps, 1)

            def values(a):
                h, i = divmod(a, NT)
                n = ROWS[i]
                pe.wait_ge(pT_ready, a + 1)
                if a >= 2:
                    pe.wait_ge(o_sb, a - 1)
                out = ps[0:n, O_BANK + a % 2, 0:HD]
                cols_h = slice(h * HD, (h + 1) * HD)
                if i < NT - 1:
                    for k in range(i + 1):
                        last = mm(out, pT_sb[a % 2][:, k * P:(k + 1) * P], v_nat[:, k, cols_h], start=(k == 0), stop=(k == i))
                else:
                    mm(out, pT_sb[a % 2][:, 0:n], v_cache[:, cols_h], start=True, stop=False)
                    last = mm(out, pT_sb[a % 2][0:SS, P:P + n], v_nat[0:SS, i, cols_h], start=False, stop=True)
                last.then_inc(o_ps, 1)

            def pair_out(pr):
                pe.wait_ge(o_sb, 2 * NT * (pr + 1))
                if pr >= 1:
                    pe.wait_ge(oT_sb, pr)
                o = o_nat[pr % 2]
                for i in range(NT):
                    n = ROWS[i]
                    out = ps[:, 6, i * P:(i + 1) * P] if i < NT - 1 else ps[:, 7, 0:n]
                    flip = const("flip") if i < NT - 1 else const("flip_sample")[0:n, 0:n]
                    last = mm(out, o[0:n, i, :], flip, start=True, stop=True)
                last.then_inc(oT_ps, 1)

            UNITS = NH * NT
            for a in range(UNITS + 3):
                if a < UNITS:
                    scores(a)
                if 0 <= a - 1 < UNITS:
                    p_transposes(a - 1)
                if 0 <= a - 2 < UNITS:
                    values(a - 2)
                if a - 3 >= 0 and (a - 3) % (2 * NT) == 2 * NT - 1:
                    pair_out((a - 3) // (2 * NT))
            pe.wait_ge(oT_sb, PAIRS)
            pe.wait_ge(o_sb, UNITS)
            for hf in range(2):
                piece = att_first + QKV_PIECES + hf
                s = piece % SLOTS
                pe.wait_ge(piece_in[s], piece_count(piece))
                w = ring[:, s, :].rearrange("p (k e) -> p k e", k=KT)
                for i in range(NT):
                    m = hf * NT + i
                    n = ROWS[i]
                    if m >= 4:
                        if m - 4 < NT:
                            pe.wait_ge(x_half, m - 3)
                        else:
                            pe.wait_ge(x_mixed[1], m - 3 - NT)
                    for k in range(KT):
                        last = mm(ps[0:n, m % 4, :], hT[:, k, tok(i)], w[:, k, :], start=(k == 0), stop=(k == KT - 1))
                    last.then_inc(att_y, 1)
            route(1)
            experts(1)


_INS = ["x_prompt", "x_sample", "cache_pool", "cache_k", "cache_v", "norm_mix", "norm_ffn", "pool_w", "pool_scale",
        "attn_w_qkv", "attn_w_o", "attn_q_gain", "attn_k_gain", "moe_w_r1", "moe_b_r1", "moe_w_r2", "moe_b_r2",
        "moe_w_gate", "moe_w_up", "moe_w_down"]


def kernel(**inputs):
    import numpy as _np
    import concourse.bacc as _bacc
    from concourse import mybir as _mybir
    from concourse.bass_utils import run_bass_kernel_spmd as _run

    nc = _bacc.Bacc("TRN2", target_bir_lowering=False, num_devices=1)
    arrays, aps = {}, {}

    def give(name, a):
        a = _np.ascontiguousarray(a)
        arrays[f"in_{name}"] = a
        aps[name] = nc.dram_tensor(f"in_{name}", a.shape, _mybir.dt.from_np(a.dtype), kind="ExternalInput").ap()

    for name in _INS:
        give(name, inputs[name])
    B, S, D = inputs["x_prompt"].shape
    SS = inputs["x_sample"].shape[1]
    T = S + SS
    NEXP = inputs["moe_w_gate"].shape[1]
    NG, _, EPG = inputs["moe_w_r2"].shape[1:]
    distance = (S - 1) - _np.arange(S + P - 1)
    index = _np.clip(distance, -(CHUNK - 1), REL_MAX) + CHUNK - 1
    give("rel_bias_reversed", _np.asarray(inputs["attn_rel_bias"])[0][:, index])
    consts, cols = shape_constants(T, -(-T // P), NEXP + (2 * T - 1) // BLK, NEXP, EPG, NG)
    give("consts", consts)

    NH, HD = inputs["cache_k"].shape[3:]
    hist = inputs["cache_pool"].shape[2]
    shapes = [(1, S, D), (1, SS, D), (1, 1, hist, D), (1, 1, hist, D),
              (1, 1, S, NH, HD), (1, 1, S, NH, HD), (1, 1, SS, NH, HD), (1, 1, SS, NH, HD)]
    outs = [nc.dram_tensor(f"out_{i}", s, F32, kind="ExternalOutput").ap() for i, s in enumerate(shapes)]
    encoder(nc, aps, outs, cols)
    res = _run(nc, [arrays], core_ids=[0])
    return tuple(res.results[0][f"out_{i}"] for i in range(len(shapes)))
```

```python
from contextlib import ExitStack

import numpy as np

import concourse.bass as bass
from concourse import mybir

P = 128
F32 = mybir.dt.float32
F32R = mybir.dt.float32r
I32 = mybir.dt.int32
ALU = mybir.AluOpType
ACT = mybir.ActivationFunctionType
AX = mybir.AxisListType

EPS = 1e-6
POOL_WINDOWS = (2, 4, 8, 16)
HIST = max(POOL_WINDOWS) - 1
HALO = 16
BLK = 64
NEG = -1e30
PAD = 4096.0
CHUNK = 64
REL_MAX = 256


def shape_constants(T, NT, NB, NEXP, EPG, NG):
    cols, parts = {}, []

    def put(name, a):
        a = np.asarray(a, np.float32)
        if a.ndim == 1:
            a = np.broadcast_to(a, (P, a.size))
        a = a.reshape(P, -1)
        at = sum(x.shape[1] for x in parts)
        cols[name] = (at, a.shape[1])
        parts.append(a)

    p = np.arange(P)
    put("ident", np.eye(P))
    put("flip", np.eye(P)[::-1])
    put("before", p[:, None] < p[None, :])
    put("ones", np.ones((P, P)))
    d = p[None, :] - p[:, None]
    bands = []
    for g, w in enumerate(POOL_WINDOWS):
        inside = (d >= 0) & (d < w)
        bands += [inside / np.float32(w) - np.eye(P),
                  inside / np.minimum(p + 1, w)[None, :].astype(np.float32) - np.eye(P)]
        put(f"band_halo{g}", ((d + P < w)[:, :HALO]) / np.float32(w))
    tok = np.arange(NT)[None, :] * P + p[:, None]
    put("valid", tok < T)
    put("token", tok - PAD)
    put("row0", 2 * tok - PAD)
    put("row1", 2 * tok + 1 - PAD)
    put("rank_group", NG - np.arange(NG))
    put("rank_expert", EPG - np.arange(EPG))
    put("iota_expert", np.arange(NEXP))
    put("iota_slot", np.arange(BLK))
    put("iota_block", np.arange(NB))
    put("steps", BLK * (1 + np.arange(-(-T // BLK))))
    put("eps", np.full(1, EPS))
    return np.concatenate(parts, 1), np.concatenate(bands, 1).astype(np.float32), cols


def encoder(nc, A, O, cols):
    S, D = A["x_prompt"].shape[1:]
    SS = A["x_sample"].shape[1]
    T = S + SS
    NT = -(-T // P)
    ROWS = [P] * (NT - 1) + [SS]
    assert S == (NT - 1) * P and SS == 32 and T == S + SS
    KT = D // P
    NH, HD = A["cache_k"].shape[3:]
    PAIRS = NH // 2
    KEEP = A["cache_k"].shape[2]
    L, NEXP, _, FE = A["moe_w_gate"].shape
    FT = FE // P
    NG = A["moe_w_r1"].shape[2]
    EPG = A["moe_w_r2"].shape[3]
    NR = NG + NEXP
    OVF = (2 * T - 1) // BLK
    NB = NEXP + OVF
    STEPS = -(-T // BLK)
    PW = D // len(POOL_WINDOWS)
    XROWS, YROWS = T, 2 * T
    SLOTS = 3
    QUARTERS = 4
    SLOT = KT * 512
    QUART = SLOT // QUARTERS
    assert FE == 512 and FT * D == SLOT and KEEP == P
    ATT_PIECES = 3 * D // 512 + D // 512
    QKV_PIECES = 3 * D // 512

    xn_dram = [nc.dram_tensor(f"xn{l}", (XROWS, D), F32, kind="Internal").ap() for l in range(L)]
    yb_dram = [nc.dram_tensor(f"yb{l}", (YROWS, D), F32, kind="Internal").ap() for l in range(L)]

    ctx = ExitStack()
    with ctx:
        def sb(name, shape, dt=F32):
            return ctx.enter_context(nc.sbuf_tensor(name, shape, dt))

        def sem(name):
            return ctx.enter_context(nc.semaphore(name))

        def per_layer(name):
            return [sem(f"{name}_{l}") for l in range(L)]

        ring = sb("ring", [P, SLOTS, SLOT])
        w_hi = sb("w_hi", [P, QUARTERS, QUART], F32R)
        w_lo = sb("w_lo", [P, QUARTERS, QUART], F32R)
        x = sb("x", [P, NT, D])
        nat = sb("nat", [P, NT * D])
        hT_hi = sb("hT_hi", [P, KT, T], F32R)
        hT_lo = sb("hT_lo", [P, KT, T], F32R)
        xT_hi = sb("xT_hi", [P, 2, KT * BLK], F32R)
        xT_lo = sb("xT_lo", [P, 2, KT * BLK], F32R)
        hid_hi = sb("hid_hi", [P, FT * BLK], F32R)
        hid_lo = sb("hid_lo", [P, FT * BLK], F32R)
        qk = sb("qk", [P, 2, KT * T])
        gain = sb("gain", [P, D])
        cst = sb("cst", [P, A["consts"].shape[1]])
        qk_gain = sb("qk_gain", [P, 2, HD])
        ssq = sb("ssq", [P, 4, NT])
        std = sb("std", [P, 4, NT])
        rstd = sb("rstd", [P, 4, NT])
        idx_gather = sb("idx_gather", [BLK, NB], I32)
        idx_scatter = sb("idx_scatter", [BLK, NB], I32)
        slot_gate = sb("slot_gate", [BLK, NB])
        ovf_expert = sb("ovf_expert", [1, OVF], I32)
        ovf_count = sb("ovf_count", [1, 1], I32)
        gcol = [sb(f"gcol{u}", [BLK, 1], I32) for u in range(2)]
        scol = [sb(f"scol{u}", [BLK, 1], I32) for u in range(2)]
        ps = ctx.enter_context(nc.psum_tensor("ps", [P, 8, 512], F32))

        def const(name, rows=P):
            at, n = cols[name]
            return cst[0:rows, at:at + n]

        ident = const("ident")
        flip_sample = const("flip")[0:SS, P - SS:P]

        pool_h = nat[:, :].rearrange("p (i d) -> p i d", i=NT)
        v_nat = pool_h
        xg = [nat[0:BLK, u * D:(u + 1) * D] for u in range(2)]
        yb = [nat[0:BLK, (2 + u) * D:(3 + u) * D] for u in range(2)]
        yc = [nat[:, 2 * u * D:2 * (u + 1) * D] for u in range(2)]
        qk_flat = qk[:, :, :].rearrange("p a n -> p (a n)")
        qT = qk[:, 0, :].rearrange("p (c t) -> p c t", c=PAIRS)
        kT = qk[:, 1, :].rearrange("p (c t) -> p c t", c=PAIRS)
        rows_h = qk_flat[:, 0:NT * D].rearrange("p (i d) -> p i d", i=NT)
        at = NT * D
        silu = qk_flat[0:BLK, at:at + FE]
        hidden = qk_flat[0:BLK, at + FE:at + 2 * FE]
        route_at = at + 2 * FE
        pool_gain = qk_flat[:, 0:D]
        pool_scale = qk_flat[:, D:2 * D]
        hist = qk_flat[:, 2 * D:3 * D]
        band_w = qk_flat[:, 3 * D:3 * D + 2 * PW * len(POOL_WINDOWS)].rearrange(
            "p (c n) -> p c n", c=2 * len(POOL_WINDOWS))
        y_tmp = qk_flat[:, 3 * D + 2 * PW * len(POOL_WINDOWS):4 * D + 2 * PW * len(POOL_WINDOWS)]
        dT_at = 4 * D + 2 * PW * len(POOL_WINDOWS)
        dT = [qk_flat[:, dT_at + u * D:dT_at + (u + 1) * D].rearrange("p (c t) -> p c t", c=KT) for u in range(2)]
        assert dT_at + 2 * D <= 2 * KT * T

        taken = {"nat": 0, "qk": route_at}

        def scratch(where, *shape):
            n = int(np.prod(shape))
            flat = nat[:, :] if where == "nat" else qk_flat
            a = flat[:, taken[where]:taken[where] + n]
            taken[where] += n
            assert taken[where] <= (NT * D if where == "nat" else 2 * KT * T), where
            if len(shape) == 2:
                a = a.rearrange("p (a b) -> p a b", a=shape[0])
            if len(shape) == 3:
                a = a.rearrange("p (a b c) -> p a b c", a=shape[0], b=shape[1])
            return a

        r = {}
        for name in ("m1", "s1", "pg", "kk", "ma", "mb", "dg", "eg", "den", "rden", "pad"):
            r[name] = scratch("nat", NT)
        for k in range(2):
            for name in ("gate", "pos", "exp", "off", "step", "slot", "blk", "is0"):
                r[f"{name}{k}"] = scratch("nat", NT)
            r[f"A{k}"] = scratch("nat", NT, NEXP)
            r[f"S{k}"] = scratch("nat", NT, BLK)
            r[f"V{k}"] = scratch("nat", NT, 3, NB)
        r["logit"] = scratch("nat", NT, NR)
        for name in ("d1", "e1", "eq1", "oh1"):
            r[name] = scratch("nat", NT, NG)
        for name in ("l2", "l2b", "eq2", "a0", "a1"):
            r[name] = scratch("nat", NT, EPG)
        r["tmp"] = scratch("qk", max(NT * max(NEXP, NB, STEPS), NEXP * STEPS, OVF * NEXP))
        r["tmp2"] = scratch("qk", max(NT * NB, OVF * NEXP))
        r["M"] = scratch("nat", NT, NEXP)
        r["C"] = scratch("nat", NT + 1, NEXP)
        for name in ("extra", "incl", "offs"):
            r[name] = scratch("nat", NEXP)
        r["bias"] = sb("router_bias", [P, NR])[:, :]
        rw = sb("rw", [P, KT, NR])

        a4 = ring[:, 1, :]
        a5 = ring[:, 2, :]
        kcT = a4[:, 0:PAIRS * KEEP].rearrange("p (c t) -> p c t", c=PAIRS)
        v_cache = a4[:, D:2 * D]
        o_nat = [a4[:, 2 * D + u * NT * P:2 * D + (u + 1) * NT * P].rearrange("p (i c) -> p i c", i=NT)
                 for u in range(2)]
        small = a4[:, 2 * D + 2 * NT * P:2 * D + 2 * NT * P + 64]
        bias_h = [a5[:, u * 512:(u + 1) * 512] for u in range(2)]
        s_sb = [a5[:, (2 + u) * 512:(3 + u) * 512] for u in range(2)]
        p_sb = [a5[:, (4 + u) * 512:(5 + u) * 512] for u in range(2)]
        pT_sb = [a5[:, (6 + u) * 512:(7 + u) * 512] for u in range(2)]
        k_cache_nat = a5[:, 1024:2048]
        sq = [nat[:, u * 512:(u + 1) * 512] for u in range(2)]
        qn = [nat[:, (2 + u) * 512:(3 + u) * 512] for u in range(4)]
        qstat = nat[:, 6 * 512:6 * 512 + 64]

        x_in = [sem(f"x_in{i}") for i in range(NT)]
        hist_zero = sem("hist_zero")
        hist_in = sem("hist_in")
        consts_in = sem("consts_in")
        bands_in = sem("bands_in")
        pool_gain_in = sem("pool_gain_in")
        pool_scale_in = sem("pool_scale_in")
        pool_w_in = sem("pool_w_in")
        gain_in = [sem(f"gain_in{n}") for n in range(3)]
        router_in = per_layer("router_in")
        piece_in = [sem(f"piece_in{s}") for s in range(SLOTS)]
        split_hi = sem("split_hi")
        split_lo = sem("split_lo")
        quarters_used = sem("quarters_used")
        act_own = sem("act_own")
        dve_own = sem("dve_own")
        std_ready = sem("std_ready")
        h_ready = sem("h_ready")
        delta_ps = sem("delta_ps")
        delta_sb = sem("delta_sb")
        pool_y = sem("pool_y")
        x_mixed = per_layer("x_mixed")
        state_out = sem("state_out")
        hT_ps = sem("hT_ps")
        hT_hi_sb = sem("hT_hi_sb")
        hT_sb = sem("hT_sb")
        xn_stored = per_layer("xn_stored")
        logit_ps = sem("logit_ps")
        route_exp_in = sem("route_exp_in")
        route_exp = sem("route_exp")
        chosen = sem("chosen")
        ranks_ps = sem("ranks_ps")
        slots_ready = sem("slots_ready")
        table_ps = sem("table_ps")
        table_sb = sem("table_sb")
        xg_zero = sem("xg_zero")
        gcol_set = per_layer("gcol_set")
        scol_set = per_layer("scol_set")
        gathered = [[sem(f"gathered{l}_{u}") for u in range(2)] for l in range(L)]
        xT_ps = per_layer("xT_ps")
        xT_hi_sb = per_layer("xT_hi_sb")
        xT_sb = per_layer("xT_sb")
        hidT_ps = per_layer("hidT_ps")
        hidT_hi_sb = per_layer("hidT_hi_sb")
        hidT_sb = per_layer("hidT_sb")
        silu_sb = per_layer("silu_sb")
        hidden_sb = per_layer("hidden_sb")
        y_lo = per_layer("y_lo")
        y_hi = per_layer("y_hi")
        scattered = [[sem(f"scattered{l}_{u}") for u in range(2)] for l in range(L)]
        o_piece_in = per_layer("o_piece_in")
        o_col = per_layer("o_col")
        o_gathered = per_layer("o_gathered")
        o_xT_ps = per_layer("o_xT_ps")
        o_xT_hi = per_layer("o_xT_hi")
        o_xT_sb = per_layer("o_xT_sb")
        o_split_hi = per_layer("o_split_hi")
        o_split_lo = per_layer("o_split_lo")
        o_used = per_layer("o_used")
        o_hidT_ps = per_layer("o_hidT_ps")
        o_hidT_hi = per_layer("o_hidT_hi")
        o_hidT_sb = per_layer("o_hidT_sb")
        o_silu = per_layer("o_silu")
        o_hidden = per_layer("o_hidden")
        o_y_lo = per_layer("o_y_lo")
        o_y_hi = per_layer("o_y_hi")
        o_scattered = per_layer("o_scattered")
        yc_in = [[sem(f"yc_in{l}_{u}") for u in range(2)] for l in range(L)]
        x_done = per_layer("x_done")
        qk_gain_in = sem("qk_gain_in")
        raw_ps = sem("raw_ps")
        q_sq = sem("q_sq")
        q_ssq = sem("q_ssq")
        q_std = sem("q_std")
        q_scaled = sem("q_scaled")
        q_gained = sem("q_gained")
        qkT_ps = sem("qkT_ps")
        qkT_sb = sem("qkT_sb")
        v_sb = sem("v_sb")
        k_out = [sem(f"k_out{u}") for u in range(4)]
        v_out = sem("v_out")
        kc_in = sem("kc_in")
        vc_in = sem("vc_in")
        kcT_ps = sem("kcT_ps")
        kcT_sb = sem("kcT_sb")
        bias_in = [sem(f"bias_in{u}") for u in range(2)]
        bias_ready = sem("bias_ready")
        s_ps = sem("s_ps")
        s_biased = sem("s_biased")
        s_max = sem("s_max")
        p_ready = sem("p_ready")
        pT_ps = sem("pT_ps")
        pT_ready = sem("pT_ready")
        o_ps = sem("o_ps")
        o_sb = sem("o_sb")
        oT_ps = sem("oT_ps")
        oT_hi_sb = sem("oT_hi_sb")
        oT_sb = sem("oT_sb")
        att_y = sem("att_y")
        x_half = sem("x_half")
        out_done = sem("out_done")
        wait_carrier = sem("wait_carrier")

        wg = A["moe_w_gate"].rearrange("l e (p k) f -> (l e) p (k f)", k=KT)
        wu = A["moe_w_up"].rearrange("l e (p k) f -> (l e) p (k f)", k=KT)
        wd = A["moe_w_down"].rearrange("l e (k p) d -> (l e) p k d", p=P)
        wqkv = A["attn_w_qkv"][0].rearrange("(p k) e -> p k e", k=KT)
        wo = A["attn_w_o"][0].rearrange("(k p) d -> p k d", p=P)
        x_rows = A["x_prompt"][0]
        xs_rows = A["x_sample"][0]
        rel_t = A["rel_bias_reversed"]
        REL_W = rel_t.shape[1]

        def x_source(i):
            return x_rows[i * P:(i + 1) * P, :] if i < NT - 1 else xs_rows

        def tok(i):
            return slice(i * P, i * P + ROWS[i])

        FIRST = [0, 3 * NEXP + ATT_PIECES]
        att_first = 3 * NEXP

        def first_of_block(l, b):
            return b * 3 + (FIRST[l] - 1)

        GATE, UP, DOWN = range(3)

        def landed(l, b, m):
            at = FIRST[l] - 1 + m
            return at % SLOTS, b * 16 + 16 * (at // SLOTS + 1)

        def f32(a):
            return a.bitcast(F32)

        BLOCKS_PEELED = 5

        def blocks(eng, body):
            for b in range(BLOCKS_PEELED):
                body(b, b % 2, b // 2, b)
            with eng.Fori(BLOCKS_PEELED // 2, NEXP // 2 - 1) as it:
                for u in range(2):
                    body(it * 2 + (1 + u), (1 + u) % 2, it + u, BLOCKS_PEELED)
            body(NEXP - 1, 1, NEXP // 2 - 1, NEXP - 1)

        XT_BANK, GATE_BANK, UP_BANK, HT_BANK, Y_BANK = 0, 1, 2, 3, 4
        S_BANK, PT_BANK, O_BANK, OT_BANK = 0, 2, 4, 6
        RAW_BANKS, QKT_BANK = 6, 6
        LOGIT_BANK = 4

        block = ctx.enter_context(nc.Block())

        @block.sync
        def _(sp):
            for i in range(NT):
                sp.dma_start(x[0:ROWS[i], i, :], x_source(i)).then_inc(x_in[i], 16)
            sp.dma_start(pool_gain, A["norm_mix"][0:1, :].broadcast_to((P, D))).then_inc(pool_gain_in, 16)
            sp.dma_start(cst[:, :], A["consts"]).then_inc(consts_in, 16)
            sp.dma_start(gain[:, :], A["bands"]).then_inc(bands_in, 16)
            sp.wait_ge(hist_zero, 1)
            sp.dma_start(hist[P - HIST:P, :], A["cache_pool"][0, 0]).then_inc(hist_in, 16)
            sp.dma_start(band_w, A["pool_w"][0].rearrange("g (k p) n -> p (g k) n", p=P)).then_inc(pool_w_in, 16)
            sp.dma_start(pool_scale, A["pool_scale"][0:1, :].broadcast_to((P, D))).then_inc(pool_scale_in, 16)

            def slot_free(n):
                if n >= SLOTS:
                    sp.wait_ge(split_lo, QUARTERS * (n - SLOTS + 1))

            def expert_piece(e, m, s):
                to = ring[:, s, :]
                src = (wg, wu, wd)[m][bass.ds(e, 1)]
                if m == DOWN:
                    return to.rearrange("p (k d) -> p k d", k=FT), src.rearrange("e p k d -> (e p) k d")
                return to, src.rearrange("e p n -> (e p) n")

            for l in range(L):
                first = FIRST[l]
                order = [(GATE, 0), (UP, 0)] + [(m, b - (m == DOWN)) for b in range(1, 3) for m in range(3)]
                for k, (m, b) in enumerate(order):
                    n = first + k
                    slot_free(n)
                    if l == 1 and k == 0:
                        sp.wait_ge(oT_sb, PAIRS)
                    to, src = expert_piece(l * NEXP + b, m, n % SLOTS)
                    sp.dma_start(to, src).then_inc(piece_in[n % SLOTS], 16)
                with sp.Fori(3, NEXP) as b:
                    for m in range(3):
                        s, _ = landed(l, b, m)
                        to, src = expert_piece(b + (l * NEXP - (m == DOWN)), m, s)
                        sp.wait_ge(split_lo, b * (3 * QUARTERS) + QUARTERS * (first - 1 + m - SLOTS + 1))
                        sp.dma_start(to, src).then_inc(piece_in[s], 16)
                n = first + 3 * NEXP - 1
                slot_free(n)
                to, src = expert_piece(l * NEXP + NEXP - 1, DOWN, n % SLOTS)
                sp.dma_start(to, src).then_inc(piece_in[n % SLOTS], 16)
                sp.wait_ge(table_sb, l + 1)
                n_ovf = sp.value_load(ovf_count[0:1, 0:1], min_val=0, max_val=OVF)
                with sp.If(n_ovf > 0):
                    sp.wait_ge(split_lo, QUARTERS * (first + 3 * NEXP))
                    with sp.Fori(0, n_ovf) as j:
                        e = sp.value_load(ovf_expert[0:1, bass.ds(j, 1)], min_val=0, max_val=NEXP - 1)
                        for m in range(3):
                            to, src = expert_piece(e + l * NEXP, m, m)
                            sp.dma_start(to, src).then_inc(o_piece_in[l], 16)
                        sp.wait_ge(o_split_lo[l], j * 12 + 12)
                        sp.sem_inc(wait_carrier, 1)
                if l == 0:
                    for j in range(ATT_PIECES):
                        n = att_first + j
                        slot_free(n)
                        if j == ATT_PIECES - 1:
                            sp.wait_ge(oT_sb, PAIRS)
                        to = ring[:, n % SLOTS, :].rearrange("p (k e) -> p k e", k=KT)
                        src = (wqkv[:, :, j * 512:(j + 1) * 512] if j < QKV_PIECES
                               else wo[:, :, (j - QKV_PIECES) * 512:(j - QKV_PIECES + 1) * 512])
                        sp.dma_start(to, src).then_inc(piece_in[n % SLOTS], 16)

        def piece_count(n):
            return 16 * (n // SLOTS + 1)

        @block.gpsimd
        def _(pool):
            pool.memset(hist, 0.0).then_inc(hist_zero, 1)
            rw1 = lambda l: A["moe_w_r1"][l].rearrange("(p k) g -> p k g", k=KT)
            rw2 = lambda l, g: A["moe_w_r2"][l, g].rearrange("(p k) e -> p k e", k=KT)

            def load_router(l):
                pool.dma_start(rw[:, :, 0:NG], rw1(l)).then_inc(router_in[l], 16)
                for g in range(NG):
                    pool.dma_start(rw[:, :, NG + g * EPG:NG + (g + 1) * EPG], rw2(l, g)).then_inc(router_in[l], 16)
                pool.dma_start(r["bias"][:, 0:NG], A["moe_b_r1"][l:l + 1, :].broadcast_to((P, NG))).then_inc(router_in[l], 16)
                pool.dma_start(r["bias"][:, NG:NR], A["moe_b_r2"][l:l + 1].rearrange("o g e -> o (g e)").broadcast_to((P, NEXP))).then_inc(router_in[l], 16)

            def gather(l, j, v, half, stage):
                if stage >= 2:
                    pool.wait_ge(gathered[l][v], half * 16)
                pool.tensor_copy(gcol[v][:, :], idx_gather[:, bass.ds(j, 1)]).then_inc(gcol_set[l], 1)
                if stage >= 2:
                    pool.wait_ge(xT_ps[l], j - 1)
                pool.wait_ge(gcol_set[l], j + 1)
                pool.sem_inc(wait_carrier, 1)
                pool.indirect_dma_start(
                    out=xg[v], out_offset=None, in_=xn_dram[l],
                    in_offset=bass.IndirectOffsetOnAxis(ap=gcol[v][:, :], axis=0),
                    bounds_check=XROWS - 1, oob_is_err=False).then_inc(gathered[l][v], 16)

            def scatter(l, j, v, half, stage):
                if stage >= 2:
                    pool.wait_ge(scattered[l][v], half * 16)
                pool.tensor_copy(scol[v][:, :], idx_scatter[:, bass.ds(j, 1)]).then_inc(scol_set[l], 1)
                pool.wait_ge(scol_set[l], j + 1)
                pool.wait_ge(y_lo[l], j + 1)
                pool.wait_ge(y_hi[l], j + 1)
                pool.sem_inc(wait_carrier, 1)
                pool.indirect_dma_start(
                    out=yb_dram[l], out_offset=bass.IndirectOffsetOnAxis(ap=scol[v][:, :], axis=0),
                    in_=yb[v], in_offset=None,
                    bounds_check=YROWS - 1, oob_is_err=False).then_inc(scattered[l][v], 16)

            def experts(l):
                pool.wait_ge(table_sb, l + 1)
                for u in range(2):
                    last = pool.memset(xg[u], 0.0)
                last.then_inc(xg_zero, 1)
                pool.wait_ge(xg_zero, l + 1)
                pool.wait_ge(xn_stored[l], 16 * NT)
                gather(l, 0, 0, 0, 0)

                def body(b, par, half, stage):
                    if stage < NEXP - 1:
                        gather(l, b + 1, 1 - par, half + par, stage + 1)
                    if stage >= 2:
                        scatter(l, b - 2, par, half - 1, stage - 2)

                blocks(pool, body)
                for j in (NEXP - 2, NEXP - 1):
                    scatter(l, j, j % 2, j // 2, j)
                n_ovf = pool.value_load(ovf_count[0:1, 0:1], min_val=0, max_val=OVF)
                with pool.If(n_ovf > 0):
                    for u in range(2):
                        pool.wait_ge(gathered[l][u], 16 * (NEXP // 2))
                        pool.wait_ge(scattered[l][u], 16 * (NEXP // 2))
                    pool.wait_ge(xT_ps[l], NEXP)
                    with pool.Fori(0, n_ovf) as j:
                        pool.tensor_copy(gcol[0][:, :], idx_gather[:, bass.ds(j + NEXP, 1)]).then_inc(o_col[l], 1)
                        pool.tensor_copy(scol[0][:, :], idx_scatter[:, bass.ds(j + NEXP, 1)]).then_inc(o_col[l], 1)
                        pool.wait_ge(o_col[l], 2 * j + 2)
                        pool.sem_inc(wait_carrier, 1)
                        pool.indirect_dma_start(
                            out=xg[0], out_offset=None, in_=xn_dram[l],
                            in_offset=bass.IndirectOffsetOnAxis(ap=gcol[0][:, :], axis=0),
                            bounds_check=XROWS - 1, oob_is_err=False).then_inc(o_gathered[l], 16)
                        pool.wait_ge(o_y_lo[l], j + 1)
                        pool.wait_ge(o_y_hi[l], j + 1)
                        pool.sem_inc(wait_carrier, 1)
                        pool.indirect_dma_start(
                            out=yb_dram[l], out_offset=bass.IndirectOffsetOnAxis(ap=scol[0][:, :], axis=0),
                            in_=yb[0], in_offset=None,
                            bounds_check=YROWS - 1, oob_is_err=False).then_inc(o_scattered[l], 16)
                        pool.wait_ge(o_scattered[l], j * 16 + 16)
                        pool.sem_inc(wait_carrier, 1)
                for u in range(2):
                    pool.wait_ge(scattered[l][u], 16 * (NEXP // 2))

            def combine_loads(l):
                for i in range(NT):
                    if i >= 2:
                        pool.wait_ge(x_done[l], i - 1)
                    n = ROWS[i]
                    pool.dma_start(yc[i % 2][0:n, :], yb_dram[l][2 * i * P:2 * (i * P + n), :].rearrange(
                        "(t k) d -> t (k d)", k=2)).then_inc(yc_in[l][i % 2], 16)

            load_router(0)
            experts(0)
            combine_loads(0)
            load_router(1)

            units = (QKV_PIECES - 2) * NT
            for m in range(units):
                j, i = divmod(m, NT)
                n = ROWS[i]
                if m == 0:
                    pool.wait_ge(qk_gain_in, 32)
                pool.wait_ge(q_scaled, m + 1)
                v = qn[m % 4][0:n, :].rearrange("p (h d) -> p h d", d=HD)
                g = qk_gain[0:n, j // 2, :].unsqueeze(1).broadcast_to((n, 512 // HD, HD))
                pool.tensor_tensor(v, v, g, ALU.mult).then_inc(q_gained, 1)
                if j >= 2:
                    pool.wait_ge(q_gained, m + 1)
                    half = slice((j - 2) * 512, (j - 1) * 512)
                    dst = (O[4][0, 0].rearrange("t h d -> t (h d)")[i * P:(i + 1) * P, half] if i < NT - 1
                           else O[6][0, 0].rearrange("t h d -> t (h d)")[:, half])
                    pool.dma_start(dst, qn[m % 4][0:n, :]).then_inc(k_out[m % 4], 16)
            for m in range(2 * NT):
                j, i = divmod(m, NT)
                n = ROWS[i]
                half = slice(j * 512, (j + 1) * 512)
                pool.wait_ge(v_sb, m + 1)
                dst = (O[5][0, 0].rearrange("t h d -> t (h d)")[i * P:(i + 1) * P, half] if i < NT - 1
                       else O[7][0, 0].rearrange("t h d -> t (h d)")[:, half])
                pool.dma_start(dst, v_nat[0:n, i, half]).then_inc(v_out, 16)
            pool.wait_ge(split_lo, QUARTERS * (att_first + QKV_PIECES))
            pool.dma_start(k_cache_nat, A["cache_k"][0, 0].rearrange("t h d -> t (h d)")).then_inc(kc_in, 16)
            pool.dma_start(v_cache, A["cache_v"][0, 0].rearrange("t h d -> t (h d)")).then_inc(vc_in, 16)
            for h in range(NH):
                if h >= 2:
                    pool.wait_ge(s_biased, NT * (h - 1))
                pool.dma_start(bias_h[h % 2], bass.AP(tensor=rel_t.tensor, offset=h * REL_W,
                                                      ap=[[1, P], [1, 512]])).then_inc(bias_in[h % 2], 16)
            experts(1)
            combine_loads(1)
            for i in range(NT):
                pool.wait_ge(x_done[1], i + 1)
                dst = O[0][0, i * P:(i + 1) * P, :] if i < NT - 1 else O[1][0]
                pool.dma_start(dst, x[0:ROWS[i], i, :]).then_inc(out_done, 16)
            pool.wait_ge(out_done, 16 * NT)
            for u in range(4):
                n_k = len([m for m in range(2 * NT, 4 * NT) if m % 4 == u])
                pool.wait_ge(k_out[u], 16 * n_k)
            pool.wait_ge(state_out, 32)

        @block.scalar
        def _(act):
            own = [0]

            def link(ins):
                own[0] += 1
                ins.then_inc(act_own, 1)
                act.wait_ge(act_own, own[0])

            def root_mean_square(ph, i, out):
                n = ROWS[i]
                link(act.activation(out, x[0:n, i, :], ACT.Square, accum_out=ssq[0:n, ph, i:i + 1]))
                act.activation(std[0:n, ph, i:i + 1], ssq[0:n, ph, i:i + 1], ACT.Sqrt,
                               bias=const("eps", n), scale=1.0 / D).then_inc(std_ready, 1)

            def split_piece(s, value, quarter, first=False):
                act.wait_ge(piece_in[s], value)
                for q in range(QUARTERS):
                    if not first:
                        act.wait_ge(quarters_used, quarter + (q - QUARTERS + 1))
                    act.activation(w_hi[:, q, :], ring[:, s, q * QUART:(q + 1) * QUART], ACT.Copy).then_inc(split_hi, 1)

            def split_static(n, quarters=range(QUARTERS)):
                for q in quarters:
                    act.wait_ge(piece_in[n % SLOTS], piece_count(n))
                    if QUARTERS * n + q >= QUARTERS:
                        act.wait_ge(quarters_used, QUARTERS * n + q - QUARTERS + 1)
                    act.activation(w_hi[:, q, :], ring[:, n % SLOTS, q * QUART:(q + 1) * QUART],
                                   ACT.Copy).then_inc(split_hi, 1)

            def transpose_out(ph, i):
                n = ROWS[i]
                act.wait_ge(hT_ps, (ph - 1) * NT + i + 1)
                b = 2 * (i % 2)
                act.activation(hT_hi[:, 0:KT, i * P:i * P + n],
                               ps[:, b:b + 2, :].rearrange("p b (c t) -> p (b c) t", c=4)[:, :, 0:n],
                               ACT.Copy).then_inc(hT_hi_sb, 1)

            act.wait_ge(consts_in, 16)
            for i in range(NT):
                act.wait_ge(x_in[i], 16)
                root_mean_square(0, i, pool_h[0:ROWS[i], i, :])
            act.wait_ge(h_ready, NT)
            act.dma_start(O[2][0, 0], pool_h[P - HIST:P, NT - 2, :]).then_inc(state_out, 16)
            act.dma_start(O[3][0, 0], pool_h[SS - HIST:SS, NT - 1, :]).then_inc(state_out, 16)
            for i in range(NT):
                n = ROWS[i]
                act.wait_ge(delta_ps, i + 1)
                b = 2 * (i % 2)
                if i >= 2:
                    act.wait_ge(pool_y, i - 1)
                act.activation(dT[i % 2][:, :, 0:n],
                               ps[:, b:b + 2, :].rearrange("p b (c t) -> p (b c) t", c=4)[:, :, 0:n],
                               ACT.Copy).then_inc(delta_sb, 1)
            act.dma_start(gain[:, :], A["norm_ffn"][0:1, :].broadcast_to((P, D))).then_inc(gain_in[0], 16)

            def route_rows(l):
                ph = 1 + 2 * l
                for i in range(NT + 1):
                    if i < NT:
                        act.wait_ge(x_mixed[l], i + 1)
                        if i == 0 and l == 0:
                            act.wait_ge(x_mixed[0], NT)
                        root_mean_square(ph, i, rows_h[0:ROWS[i], i, :])
                    if i > 0:
                        k = i - 1
                        act.wait_ge(h_ready, ph * NT + k + 1)
                        act.dma_start(xn_dram[l][k * P:k * P + ROWS[k], :],
                                      rows_h[0:ROWS[k], k, :]).then_inc(xn_stored[l], 16)
                        transpose_out(ph, k)
                if l == 0:
                    act.dma_start(gain[:, :], A["norm_mix"][1:2, :].broadcast_to((P, D))).then_inc(gain_in[1], 16)
                act.wait_ge(route_exp_in, l * 2 + 1)
                act.activation(r["e1"], r["d1"], ACT.Exp).then_inc(route_exp, 1)
                act.wait_ge(route_exp_in, l * 2 + 2)
                act.activation(r["eg"], r["dg"], ACT.Exp).then_inc(route_exp, 1)

            def xT_out(l, b, u):
                act.wait_ge(xT_ps[l], b + 1)
                act.activation(xT_hi[:, u, :], ps[:, XT_BANK, 0:KT * BLK], ACT.Copy).then_inc(xT_hi_sb[l], 1)

            def hidT_out(l, b):
                act.wait_ge(hidT_ps[l], b + 1)
                act.activation(hid_hi[:, :], ps[:, HT_BANK, 0:FT * BLK], ACT.Copy).then_inc(hidT_hi_sb[l], 1)

            def y_out(l, j, v, half, stage, done):
                act.wait_ge(quarters_used, done)
                if stage >= 2:
                    act.wait_ge(scattered[l][v], half * 16)
                act.activation(yb[v][:, 0:512], ps[0:BLK, Y_BANK, :], ACT.Copy,
                               scale=slot_gate[:, bass.ds(j, 1)]).then_inc(y_lo[l], 1)

            def experts(l):
                xT_out(l, 0, 0)

                def body(b, par, half, stage):
                    n = first_of_block(l, b) if stage else FIRST[l]
                    quarter = n * QUARTERS
                    if stage:
                        split_piece(*landed(l, b, GATE), quarter)
                    if stage >= 2:
                        y_out(l, b - 2, par, half - 1, stage - 2, quarter)
                    if stage:
                        split_piece(*landed(l, b, UP), quarter + QUARTERS)
                        hidT_out(l, b - 1)
                    else:
                        split_static(FIRST[l] + 1)
                    act.wait_ge(quarters_used, quarter + QUARTERS)
                    if stage:
                        act.wait_ge(hidden_sb[l], b)
                    act.activation(silu, ps[0:BLK, GATE_BANK, :], ACT.Silu).then_inc(silu_sb[l], 1)
                    if stage < NEXP - 1:
                        xT_out(l, b + 1, 1 - par)
                    if stage:
                        split_piece(*landed(l, b, DOWN), quarter + 2 * QUARTERS)

                blocks(act, body)
                n = FIRST[l] + 3 * NEXP - 1
                split_static(n)
                y_out(l, NEXP - 2, 0, NEXP // 2 - 1, NEXP - 2, n * QUARTERS)
                hidT_out(l, NEXP - 1)
                y_out(l, NEXP - 1, 1, NEXP // 2 - 1, NEXP - 1, (n + 1) * QUARTERS)
                n_ovf = act.value_load(ovf_count[0:1, 0:1], min_val=0, max_val=OVF)
                with act.If(n_ovf > 0):
                    with act.Fori(0, n_ovf) as j:
                        act.wait_ge(o_xT_ps[l], j + 1)
                        act.activation(xT_hi[:, 0, :], ps[:, XT_BANK, 0:KT * BLK], ACT.Copy).then_inc(o_xT_hi[l], 1)
                        act.wait_ge(o_piece_in[l], j * 48 + 48)
                        for m in range(3):
                            for q in range(QUARTERS):
                                if m:
                                    act.wait_ge(o_used[l], j * 12 + (m * QUARTERS + q - QUARTERS + 1))
                                act.activation(w_hi[:, q, :], ring[:, m, q * QUART:(q + 1) * QUART],
                                               ACT.Copy).then_inc(o_split_hi[l], 1)
                            if m == UP:
                                act.wait_ge(o_used[l], j * 12 + QUARTERS)
                                act.activation(silu, ps[0:BLK, GATE_BANK, :], ACT.Silu).then_inc(o_silu[l], 1)
                        act.wait_ge(o_hidT_ps[l], j + 1)
                        act.activation(hid_hi[:, :], ps[:, HT_BANK, 0:FT * BLK], ACT.Copy).then_inc(o_hidT_hi[l], 1)
                        act.wait_ge(o_used[l], j * 12 + 12)
                        act.activation(yb[0][:, 0:512], ps[0:BLK, Y_BANK, :], ACT.Copy,
                                       scale=slot_gate[:, bass.ds(j + NEXP, 1)]).then_inc(o_y_lo[l], 1)

            split_static(FIRST[0])
            route_rows(0)
            experts(0)

            for k in range(2):
                src = A["attn_q_gain" if k == 0 else "attn_k_gain"]
                act.dma_start(qk_gain[:, k, :], src[0:1, :].broadcast_to((P, HD))).then_inc(qk_gain_in, 16)
            for i in range(NT):
                act.wait_ge(x_done[0], i + 1)
                root_mean_square(2, i, rows_h[0:ROWS[i], i, :])
            for i in range(NT):
                transpose_out(2, i)
            act.dma_start(gain[:, :], A["norm_ffn"][1:2, :].broadcast_to((P, D))).then_inc(gain_in[2], 16)
            units = (QKV_PIECES - 2) * NT

            def qkT_out(m):
                j, i = divmod(m, NT)
                n = ROWS[i]
                act.wait_ge(qkT_ps, m + 1)
                dst = (qT if j < 2 else kT)[:, 4 * (j % 2):4 * (j % 2) + 4, i * P:i * P + n]
                act.activation(dst, ps[:, QKT_BANK + m % 2, :].rearrange("p (c t) -> p c t", c=4)[:, :, 0:n],
                               ACT.Copy).then_inc(qkT_sb, 1)

            def raw_out(m):
                j, i = divmod(m, NT)
                n = ROWS[i]
                act.wait_ge(raw_ps, m + 1)
                if m < units:
                    if m >= 2:
                        act.wait_ge(q_ssq, m - 1)
                    act.activation(sq[m % 2][0:n, :], ps[0:n, m % RAW_BANKS, :], ACT.Square).then_inc(q_sq, 1)
                    act.wait_ge(q_ssq, m + 1)
                    c = 24 * (m % 2)
                    act.activation(qstat[0:n, c + 8:c + 16], qstat[0:n, c:c + 8], ACT.Sqrt,
                                   bias=const("eps", n), scale=1.0 / HD).then_inc(q_std, 1)
                    return
                if m == units:
                    act.wait_ge(qkT_ps, units)
                    for u in range(4):
                        act.wait_ge(k_out[u], 16 * len([q for q in range(2 * NT, 4 * NT) if q % 4 == u]))
                m -= units
                j, i = divmod(m, NT)
                act.activation(v_nat[0:n, i, j * 512:(j + 1) * 512], ps[0:n, (units + m) % RAW_BANKS, :],
                               ACT.Copy).then_inc(v_sb, 1)

            split_static(att_first)
            for j in range(QKV_PIECES + 1):
                if j:
                    for i in range(NT):
                        raw_out((j - 1) * NT + i)
                for q in range(NT):
                    if q < QUARTERS and j < QKV_PIECES:
                        split_static(att_first + j + 1, [q])
                    if 1 <= j <= QKV_PIECES - 2:
                        qkT_out((j - 1) * NT + q)
            for c in range(2):
                act.wait_ge(kcT_ps, c + 1)
                act.activation(kcT[:, 4 * c:4 * c + 4, :], ps[:, QKT_BANK + c, :].rearrange("p (c t) -> p c t", c=4),
                               ACT.Copy).then_inc(kcT_sb, 1)

            UNITS = NH * NT
            for t in range(UNITS + 4):
                if t < UNITS:
                    i = t % NT
                    n = ROWS[i]
                    nk = (i + 1) * P if i < NT - 1 else KEEP + SS
                    c = 4 * (t % 4)
                    act.wait_ge(s_max, t + 1)
                    if t >= 2:
                        act.wait_ge(pT_ps, t - 1)
                    act.activation(p_sb[t % 2][0:n, 0:nk], s_sb[t % 2][0:n, 0:nk], ACT.Exp,
                                   bias=small[0:n, c + 1:c + 2], accum_out=small[0:n, c + 2:c + 3]).then_inc(p_ready, 1)
                if t >= 3 and (t - 3) % (2 * NT) == 2 * NT - 1:
                    pr = (t - 3) // (2 * NT)
                    act.wait_ge(oT_ps, pr + 1)
                    act.activation(hT_hi[:, pr, 0:S], ps[:, OT_BANK, :], ACT.Copy)
                    act.activation(hT_hi[:, pr, S:T], ps[:, OT_BANK + 1, 0:SS], ACT.Copy).then_inc(oT_hi_sb, 1)
            split_static(att_first + QKV_PIECES + 1)
            split_static(FIRST[1])
            route_rows(1)
            experts(1)

        @block.vector
        def _(dve):
            own = [0]

            def link(ins):
                own[0] += 1
                ins.then_inc(dve_own, 1)
                dve.wait_ge(dve_own, own[0])

            V = nc.vector

            def normalise(ph, i, out, g):
                n = ROWS[i]
                dve.wait_ge(std_ready, ph * NT + i + 1)
                link(V.reciprocal(rstd[0:n, ph, i:i + 1], std[0:n, ph, i:i + 1]))
                V.scalar_tensor_tensor(out=out, in0=x[0:n, i, :], scalar=rstd[0:n, ph, i:i + 1], in1=g[0:n, :],
                                       op0=ALU.mult, op1=ALU.mult).then_inc(h_ready, 1)

            def split_piece(s, quarter):
                for q in range(QUARTERS):
                    dve.wait_ge(split_hi, quarter + (q + 1))
                    V.tensor_tensor(w_lo[:, q, :], ring[:, s, q * QUART:(q + 1) * QUART], f32(w_hi[:, q, :]),
                                    ALU.subtract).then_inc(split_lo, 1)

            def split_static(n, quarters=range(QUARTERS)):
                for q in quarters:
                    dve.wait_ge(split_hi, QUARTERS * n + q + 1)
                    V.tensor_tensor(w_lo[:, q, :], ring[:, n % SLOTS, q * QUART:(q + 1) * QUART],
                                    f32(w_hi[:, q, :]), ALU.subtract).then_inc(split_lo, 1)

            def transpose_out(ph, i):
                n = ROWS[i]
                b = 2 * (i % 2)
                cols_i = slice(i * P, i * P + n)
                dve.wait_ge(hT_hi_sb, (ph - 1) * NT + i + 1)
                V.tensor_tensor(hT_lo[:, 0:KT, cols_i],
                                ps[:, b:b + 2, :].rearrange("p b (c t) -> p (b c) t", c=4)[:, :, 0:n],
                                f32(hT_hi[:, 0:KT, cols_i]), ALU.subtract).then_inc(hT_sb, 1)

            dve.wait_ge(pool_gain_in, 16)
            for i in range(NT):
                normalise(0, i, pool_h[0:ROWS[i], i, :], pool_gain)
            dve.wait_ge(pool_scale_in, 16)
            for i in range(NT):
                n = ROWS[i]
                dve.wait_ge(pool_y, i + 1)
                b = 4 + 2 * (i % 2)
                link(V.tensor_tensor(y_tmp[0:n, :], ps[0:n, b:b + 2, :].rearrange("p b c -> p (b c)"),
                                     pool_scale[0:n, :], ALU.mult))
                ins = V.tensor_tensor(x[0:n, i, :], x[0:n, i, :], y_tmp[0:n, :], ALU.add)
                ins.then_inc(x_mixed[0], 1)
                dve.wait_ge(x_mixed[0], i + 1)

            def bc(a, shape, axis):
                return a.unsqueeze(axis).broadcast_to(shape)

            def route(l):
                ph = 1 + 2 * l
                lg = r["logit"]
                if l == 0:
                    dve.wait_ge(state_out, 32)
                else:
                    dve.wait_ge(v_out, 16 * 2 * NT)
                link(V.memset(lg, 0.0))
                dve.wait_ge(gain_in[2 * l], 16)
                for i in range(NT + 1):
                    if i < NT:
                        normalise(ph, i, rows_h[0:ROWS[i], i, :], gain)
                    if i:
                        transpose_out(ph, i - 1)
                dve.wait_ge(router_in[l], 16 * (NG + 3))
                dve.wait_ge(logit_ps, l + 1)
                full = NT - 1
                V.tensor_tensor(lg[:, 0:full, :], ps[:, LOGIT_BANK, 0:full * NR].rearrange("p (i c) -> p i c", c=NR),
                                bc(r["bias"], (P, full, NR), 1), ALU.add)
                link(V.tensor_tensor(lg[0:SS, full, :], ps[0:SS, LOGIT_BANK, full * NR:NT * NR], r["bias"][0:SS, :],
                                     ALU.add))
                l1 = lg[:, :, 0:NG]
                sg = (P, NT, NG)
                se = (P, NT, EPG)
                sx = (P, NT, NEXP)
                link(V.reduce_max(r["m1"], l1, AX.X))
                ins = V.tensor_tensor(r["d1"], l1, bc(r["m1"], sg, 2), ALU.subtract)
                ins.then_inc(route_exp_in, 1)
                link(V.tensor_tensor(r["eq1"], l1, bc(r["m1"], sg, 2), ALU.is_equal))
                link(V.tensor_tensor(r["eq1"], r["eq1"], bc(const("rank_group"), sg, 1), ALU.mult))
                link(V.reduce_max(r["kk"], r["eq1"], AX.X))
                link(V.tensor_tensor(r["oh1"], r["eq1"], bc(r["kk"], sg, 2), ALU.is_equal))
                link(V.tensor_tensor(r["oh1"], r["oh1"], bc(const("valid"), sg, 2), ALU.mult))
                t4 = r["tmp"][:, 0:NT * NEXP].rearrange("p (i g e) -> p i g e", i=NT, g=NG)
                l2g = lg[:, :, NG:NR].rearrange("p i (g e) -> p i g e", g=NG)
                oh4 = r["oh1"].unsqueeze(3).broadcast_to((P, NT, NG, EPG))
                link(V.tensor_tensor(t4, l2g, oh4, ALU.mult))
                link(V.reduce_sum(r["l2"], t4.rearrange("p i g e -> p i e g"), AX.X))
                src = r["l2"]
                for k in range(2):
                    m = r["ma" if k == 0 else "mb"]
                    link(V.reduce_max(m, src, AX.X))
                    link(V.tensor_tensor(r["eq2"], src, bc(m, se, 2), ALU.is_equal))
                    link(V.tensor_tensor(r["eq2"], r["eq2"], bc(const("rank_expert"), se, 1), ALU.mult))
                    link(V.reduce_max(r["kk"], r["eq2"], AX.X))
                    link(V.tensor_tensor(r[f"a{k}"], r["eq2"], bc(r["kk"], se, 2), ALU.is_equal))
                    if k == 0:
                        link(V.scalar_tensor_tensor(out=r["l2b"], in0=r["a0"], scalar=NEG, in1=r["l2"],
                                                    op0=ALU.mult, op1=ALU.add))
                        src = r["l2b"]
                V.tensor_tensor(r["dg"], r["mb"], r["ma"], ALU.subtract).then_inc(route_exp_in, 1)
                for k in range(2):
                    a4 = r[f"a{k}"].unsqueeze(2).broadcast_to((P, NT, NG, EPG))
                    link(V.tensor_tensor(r[f"A{k}"].rearrange("p i (g e) -> p i g e", g=NG), a4, oh4, ALU.mult))
                V.tensor_tensor(r["M"], r["A0"], r["A1"], ALU.add).then_inc(chosen, 1)
                dve.wait_ge(route_exp, l * 2 + 2)
                link(V.reduce_sum(r["s1"], r["e1"], AX.X))
                link(V.reciprocal(r["pg"], r["s1"]))
                link(V.tensor_scalar(r["den"], r["eg"], 1.0, None, ALU.add))
                link(V.reciprocal(r["rden"], r["den"]))
                link(V.tensor_tensor(r["gate0"], r["pg"], r["rden"], ALU.mult))
                link(V.tensor_tensor(r["gate1"], r["gate0"], r["eg"], ALU.mult))
                dve.wait_ge(ranks_ps, l + 1)
                link(V.tensor_copy(r["C"], ps[:, 0, 0:(NT + 1) * NEXP].rearrange("p (i e) -> p i e", e=NEXP)))
                cnt = r["C"][:, NT, :]
                sc = (P, NEXP, STEPS)
                t = r["tmp"][:, 0:NEXP * STEPS].rearrange("p (e s) -> p e s", e=NEXP)
                link(V.tensor_tensor(t, bc(cnt, sc, 2), bc(const("steps"), sc, 1), ALU.is_gt))
                link(V.reduce_sum(r["extra"], t, AX.X))
                link(V.tensor_tensor_scan(out=r["incl"], data0=const("ones")[:, 0:NEXP], data1=r["extra"],
                                          initial=0.0, op0=ALU.mult, op1=ALU.add))
                link(V.tensor_tensor(r["offs"], r["incl"], r["extra"], ALU.subtract))
                for k in range(2):
                    t = r["tmp"][:, 0:NT * NEXP].rearrange("p (i e) -> p i e", i=NT)
                    for name, w in (("pos", r["C"][:, 0:NT, :]), ("exp", bc(const("iota_expert"), sx, 1)),
                                    ("off", bc(r["offs"], sx, 1))):
                        link(V.tensor_tensor(t, r[f"A{k}"], w, ALU.mult))
                        link(V.reduce_sum(r[f"{name}{k}"], t, AX.X))
                    ts = r["tmp"][:, 0:NT * STEPS].rearrange("p (i s) -> p i s", i=NT)
                    ss = (P, NT, STEPS)
                    link(V.tensor_tensor(ts, bc(r[f"pos{k}"], ss, 2), bc(const("steps"), ss, 1), ALU.is_ge))
                    link(V.reduce_sum(r[f"step{k}"], ts, AX.X))
                    link(V.scalar_tensor_tensor(out=r[f"slot{k}"], in0=r[f"step{k}"], scalar=-float(BLK),
                                                in1=r[f"pos{k}"], op0=ALU.mult, op1=ALU.add))
                    link(V.tensor_scalar(r["pad"], const("valid"), 1.0, PAD, ALU.subtract, ALU.mult))
                    link(V.tensor_tensor(r[f"slot{k}"], r[f"slot{k}"], r["pad"], ALU.add))
                    link(V.tensor_scalar(r[f"is0{k}"], r[f"step{k}"], 0.0, None, ALU.is_equal))
                    link(V.tensor_tensor(r[f"blk{k}"], r[f"off{k}"], r[f"step{k}"], ALU.add))
                    link(V.tensor_scalar(r[f"blk{k}"], r[f"blk{k}"], float(NEXP - 1), None, ALU.add))
                    link(V.tensor_tensor(r[f"exp{k}"], r[f"exp{k}"], r[f"blk{k}"], ALU.subtract))
                    link(V.tensor_tensor(r[f"exp{k}"], r[f"exp{k}"], r[f"is0{k}"], ALU.mult))
                    link(V.tensor_tensor(r[f"blk{k}"], r[f"blk{k}"], r[f"exp{k}"], ALU.add))
                    so, sn = (P, NT, BLK), (P, NT, NB)
                    V.tensor_tensor(r[f"S{k}"], bc(r[f"slot{k}"], so, 2), bc(const("iota_slot"), so, 1), ALU.is_equal)
                    tb = r["tmp2"][:, 0:NT * NB].rearrange("p (i b) -> p i b", i=NT)
                    link(V.tensor_tensor(tb, bc(r[f"blk{k}"], sn, 2), bc(const("iota_block"), sn, 1), ALU.is_equal))
                    for c, val in enumerate((const("token"), const(f"row{k}"), r[f"gate{k}"])):
                        link(V.tensor_tensor(r[f"V{k}"][:, :, c, :], tb, bc(val, sn, 2), ALU.mult))
                so = (P, OVF, NEXP)
                ta = r["tmp"][:, 0:OVF * NEXP].rearrange("p (b e) -> p b e", e=NEXP)
                tb = r["tmp2"][:, 0:OVF * NEXP].rearrange("p (b e) -> p b e", e=NEXP)
                iota_o = bc(const("iota_block")[:, 0:OVF], so, 2)
                ins = V.tensor_tensor(ta, iota_o, bc(r["offs"], so, 1), ALU.is_ge)
                ins.then_inc(slots_ready, 1)
                dve.wait_ge(slots_ready, l + 1)
                link(V.tensor_tensor(tb, iota_o, bc(r["incl"], so, 1), ALU.is_lt))
                link(V.tensor_tensor(ta, ta, tb, ALU.mult))
                link(V.tensor_tensor(ta, ta, bc(const("iota_expert"), so, 1), ALU.mult))
                link(V.reduce_sum(r["extra"][:, 0:OVF], ta, AX.X))
                link(V.tensor_copy(ovf_expert[0:1, :], r["extra"][0:1, 0:OVF]))
                V.tensor_copy(ovf_count[0:1, :], r["incl"][0:1, NEXP - 1:NEXP])
                dve.wait_ge(table_ps, l + 1)
                V.tensor_scalar(idx_gather[:, :], ps[0:BLK, 1, 0:NB], PAD, None, ALU.add)
                V.tensor_scalar(idx_scatter[:, :], ps[0:BLK, 1, NB:2 * NB], PAD, None, ALU.add)
                V.tensor_copy(slot_gate[:, :], ps[0:BLK, 1, 2 * NB:3 * NB]).then_inc(table_sb, 1)

            def xT_out(l, b, u):
                dve.wait_ge(xT_hi_sb[l], b + 1)
                V.tensor_tensor(xT_lo[:, u, :], ps[:, XT_BANK, 0:KT * BLK], f32(xT_hi[:, u, :]),
                                ALU.subtract).then_inc(xT_sb[l], 1)

            def hidT_out(l, b):
                dve.wait_ge(hidT_hi_sb[l], b + 1)
                V.tensor_tensor(hid_lo[:, :], ps[:, HT_BANK, 0:FT * BLK], f32(hid_hi[:, :]),
                                ALU.subtract).then_inc(hidT_sb[l], 1)

            def y_out(l, j, v, half, stage, done):
                dve.wait_ge(quarters_used, done)
                if stage >= 2:
                    dve.wait_ge(scattered[l][v], half * 16)
                V.tensor_scalar(yb[v][:, 512:D], ps[0:BLK, Y_BANK + 1, :], slot_gate[:, bass.ds(j, 1)], None,
                                ALU.mult).then_inc(y_hi[l], 1)

            def experts(l):
                xT_out(l, 0, 0)

                def body(b, par, half, stage):
                    n = first_of_block(l, b) if stage else FIRST[l]
                    quarter = n * QUARTERS
                    if stage:
                        split_piece(landed(l, b, GATE)[0], quarter)
                    if stage >= 2:
                        y_out(l, b - 2, par, half - 1, stage - 2, quarter)
                    if stage:
                        split_piece(landed(l, b, UP)[0], quarter + QUARTERS)
                        hidT_out(l, b - 1)
                    else:
                        split_static(FIRST[l] + 1)
                    if stage < NEXP - 1:
                        xT_out(l, b + 1, 1 - par)
                    if stage:
                        split_piece(landed(l, b, DOWN)[0], quarter + 2 * QUARTERS)
                    dve.wait_ge(quarters_used, quarter + 2 * QUARTERS)
                    dve.wait_ge(silu_sb[l], b + 1)
                    if stage:
                        dve.wait_ge(hidT_ps[l], b)
                    V.tensor_tensor(hidden, silu, ps[0:BLK, UP_BANK, :], ALU.mult).then_inc(hidden_sb[l], 1)

                blocks(dve, body)
                n = FIRST[l] + 3 * NEXP - 1
                split_static(n)
                y_out(l, NEXP - 2, 0, NEXP // 2 - 1, NEXP - 2, n * QUARTERS)
                hidT_out(l, NEXP - 1)
                y_out(l, NEXP - 1, 1, NEXP // 2 - 1, NEXP - 1, (n + 1) * QUARTERS)
                n_ovf = dve.value_load(ovf_count[0:1, 0:1], min_val=0, max_val=OVF)
                with dve.If(n_ovf > 0):
                    with dve.Fori(0, n_ovf) as j:
                        dve.wait_ge(o_xT_hi[l], j + 1)
                        V.tensor_tensor(xT_lo[:, 0, :], ps[:, XT_BANK, 0:KT * BLK], f32(xT_hi[:, 0, :]),
                                        ALU.subtract).then_inc(o_xT_sb[l], 1)
                        for m in range(3):
                            for q in range(QUARTERS):
                                dve.wait_ge(o_split_hi[l], j * 12 + (m * QUARTERS + q + 1))
                                V.tensor_tensor(w_lo[:, q, :], ring[:, m, q * QUART:(q + 1) * QUART],
                                                f32(w_hi[:, q, :]), ALU.subtract).then_inc(o_split_lo[l], 1)
                        dve.wait_ge(o_used[l], j * 12 + 2 * QUARTERS)
                        dve.wait_ge(o_silu[l], j + 1)
                        V.tensor_tensor(hidden, silu, ps[0:BLK, UP_BANK, :], ALU.mult).then_inc(o_hidden[l], 1)
                        dve.wait_ge(o_hidT_hi[l], j + 1)
                        V.tensor_tensor(hid_lo[:, :], ps[:, HT_BANK, 0:FT * BLK], f32(hid_hi[:, :]),
                                        ALU.subtract).then_inc(o_hidT_sb[l], 1)
                        dve.wait_ge(o_used[l], j * 12 + 12)
                        V.tensor_scalar(yb[0][:, 512:D], ps[0:BLK, Y_BANK + 1, :],
                                        slot_gate[:, bass.ds(j + NEXP, 1)], None, ALU.mult).then_inc(o_y_hi[l], 1)

            def combine(l):
                for i in range(NT):
                    n = ROWS[i]
                    dve.wait_ge(yc_in[l][i % 2], 16 * (i // 2 + 1))
                    link(V.tensor_tensor(x[0:n, i, :], x[0:n, i, :], yc[i % 2][0:n, 0:D], ALU.add))
                    V.tensor_tensor(x[0:n, i, :], x[0:n, i, :], yc[i % 2][0:n, D:2 * D], ALU.add).then_inc(x_done[l], 1)

            split_static(FIRST[0])
            route(0)
            experts(0)
            combine(0)

            dve.wait_ge(gain_in[1], 16)
            for i in range(NT + 1):
                if i < NT:
                    normalise(2, i, rows_h[0:ROWS[i], i, :], gain)
                if i:
                    transpose_out(2, i - 1)
            units = (QKV_PIECES - 2) * NT

            def head_sums(m):
                n = ROWS[m % NT]
                dve.wait_ge(q_sq, m + 1)
                c = 24 * (m % 2)
                V.reduce_sum(qstat[0:n, c:c + 8], sq[m % 2][0:n, :].rearrange("p (h d) -> p h d", d=HD),
                             AX.X).then_inc(q_ssq, 1)

            def scale_heads(m):
                n = ROWS[m % NT]
                c = 24 * (m % 2)
                dve.wait_ge(q_std, m + 1)
                link(V.reciprocal(qstat[0:n, c + 16:c + 24], qstat[0:n, c + 8:c + 16]))
                if m >= 4:
                    dve.wait_ge(qkT_ps, m - 3)
                    if m - 4 >= 2 * NT:
                        n_k = len([q for q in range(2 * NT, m - 3) if q % 4 == m % 4])
                        dve.wait_ge(k_out[m % 4], 16 * n_k)
                V.tensor_tensor(qn[m % 4][0:n, :].rearrange("p (h d) -> p h d", d=HD),
                                ps[0:n, m % RAW_BANKS, :].rearrange("p (h d) -> p h d", d=HD),
                                bc(qstat[0:n, c + 16:c + 24], (n, 512 // HD, HD), 2),
                                ALU.mult).then_inc(q_scaled, 1)

            split_static(att_first)
            for j in range(QKV_PIECES):
                if 1 <= j <= QKV_PIECES - 2:
                    for i in range(NT):
                        head_sums((j - 1) * NT + i)
                        scale_heads((j - 1) * NT + i)
                split_static(att_first + j + 1)

            def scores(h, i):
                a = h * NT + i
                n = ROWS[i]
                nk = (i + 1) * P if i < NT - 1 else KEEP + SS
                m0 = 512 - nk
                if i == 0:
                    dve.wait_ge(bias_in[h % 2], 16 * (h // 2 + 1))
                    link(V.tensor_scalar(bias_h[h % 2], bias_h[h % 2], float(HD) ** 0.5, None, ALU.mult))
                    link(V.memset(bias_h[h % 2][CHUNK:P, 512 - CHUNK:512], NEG))
                dve.wait_ge(s_ps, a + 1)
                if a >= 2:
                    dve.wait_ge(p_ready, a - 1)
                c = 4 * (a % 4)
                V.tensor_tensor_reduce(out=s_sb[a % 2][0:n, 0:nk], in0=ps[0:n, S_BANK + a % 2, 0:nk],
                                       in1=bias_h[h % 2][0:n, m0:512], scale=float(HD) ** -0.5, scalar=-3e38,
                                       op0=ALU.add, op1=ALU.max, accum_out=small[0:n, c:c + 1]).then_inc(s_biased, 1)
                dve.wait_ge(s_biased, a + 1)
                V.tensor_scalar(small[0:n, c + 1:c + 2], small[0:n, c:c + 1], -1.0, None,
                                ALU.mult).then_inc(s_max, 1)

            def pT_out(a):
                i = a % NT
                nk = (i + 1) * P if i < NT - 1 else KEEP + SS
                kt = -(-nk // P)
                n = ROWS[i]
                dve.wait_ge(pT_ps, a + 1)
                if a >= 2:
                    dve.wait_ge(o_ps, a - 1)
                if i < NT - 1:
                    V.tensor_copy(pT_sb[a % 2][:, 0:kt * P], ps[:, PT_BANK + a % 2, 0:kt * P]).then_inc(pT_ready, 1)
                else:
                    V.tensor_copy(pT_sb[a % 2][:, 0:n], ps[:, PT_BANK + a % 2, 0:n])
                    V.tensor_copy(pT_sb[a % 2][0:SS, P:P + n], ps[0:SS, PT_BANK + a % 2, P:P + n]).then_inc(pT_ready, 1)

            def o_out(a):
                h, i = divmod(a, NT)
                n = ROWS[i]
                c = 4 * (a % 4)
                dve.wait_ge(p_ready, a + 1)
                link(V.reciprocal(small[0:n, c + 3:c + 4], small[0:n, c + 2:c + 3]))
                dve.wait_ge(o_ps, a + 1)
                if i == 0 and h % 2 == 0 and h >= 4:
                    dve.wait_ge(oT_ps, h // 2 - 1)
                V.tensor_scalar(o_nat[(h // 2) % 2][0:n, i, (h % 2) * HD:(h % 2 + 1) * HD],
                                ps[0:n, O_BANK + a % 2, 0:HD], small[0:n, c + 3:c + 4], None,
                                ALU.mult).then_inc(o_sb, 1)

            UNITS = NH * NT
            for a in range(UNITS + 4):
                if a < UNITS:
                    scores(*divmod(a, NT))
                if 0 <= a - 1 < UNITS:
                    pT_out(a - 1)
                if 0 <= a - 2 < UNITS:
                    o_out(a - 2)
                if a >= 3 and (a - 3) % (2 * NT) == 2 * NT - 1:
                    pr = (a - 3) // (2 * NT)
                    dve.wait_ge(oT_hi_sb, pr + 1)
                    V.tensor_tensor(hT_lo[:, pr, 0:S], ps[:, OT_BANK, :], f32(hT_hi[:, pr, 0:S]), ALU.subtract)
                    V.tensor_tensor(hT_lo[:, pr, S:T], ps[:, OT_BANK + 1, 0:SS], f32(hT_hi[:, pr, S:T]),
                                    ALU.subtract).then_inc(oT_sb, 1)
            split_static(att_first + QKV_PIECES + 1)

            for hf in range(2):
                for i in range(NT):
                    n = ROWS[i]
                    m = hf * NT + i
                    dve.wait_ge(att_y, m + 1)
                    ins = V.tensor_tensor(x[0:n, i, hf * 512:(hf + 1) * 512], x[0:n, i, hf * 512:(hf + 1) * 512],
                                          ps[0:n, m % RAW_BANKS, :], ALU.add)
                    ins.then_inc(x_mixed[1] if hf == 1 else x_half, 1)
            split_static(FIRST[1])
            route(1)
            experts(1)
            combine(1)

        @block.tensor
        def _(pe):
            mm = nc.tensor.matmul

            def split_product(out, x_hi, x_lo, w_h, w_l, start, stop):
                mm(out, x_hi, w_h, start=start, stop=False)
                mm(out, x_lo, w_h, start=False, stop=False)
                return mm(out, x_hi, w_l, start=False, stop=stop)

            def transposes(ph, i):
                n = ROWS[i]
                pe.wait_ge(h_ready, ph * NT + i + 1)
                if i >= 2:
                    pe.wait_ge(hT_sb, (ph - 1) * NT + i - 1)
                src = rows_h[0:n, i, :].rearrange("p (c k) -> p k c", k=KT)
                for k in range(KT):
                    last = nc.tensor.transpose(ps[:, 2 * (i % 2) + k // 4, 128 * (k % 4):128 * (k % 4) + n],
                                               src[:, k, :], ident[0:n, 0:n])
                last.then_inc(hT_ps, 1)

            pe.wait_ge(consts_in, 16)

            pe.wait_ge(bands_in, 16)

            def deltas(i):
                n = ROWS[i]
                pe.wait_ge(h_ready, i + 1)
                if i >= 2:
                    pe.wait_ge(delta_sb, i - 1)
                if i == NT - 1:
                    pe.wait_ge(hist_in, 16)
                for c in range(KT):
                    g = c * P // PW
                    out = ps[:, 2 * (i % 2) + c // 4, 128 * (c % 4):128 * (c % 4) + n]
                    band = gain[:, (2 * g + (i == 0)) * P:(2 * g + (i == 0) + 1) * P]
                    last = mm(out, pool_h[0:n, i, c * P:(c + 1) * P], band[0:n, 0:n], start=True, stop=True,
                              skip_group_check=True)
                    if i > 0:
                        prev = pool_h[:, i - 1, :] if i < NT - 1 else hist
                        last = mm(out[:, 0:HALO], prev[:, c * P:(c + 1) * P], const(f"band_halo{g}"),
                                  start=False, stop=True, skip_group_check=True)
                last.then_inc(delta_ps, 1)

            deltas(0)
            pe.wait_ge(pool_w_in, 16)
            for i in range(NT):
                if i + 1 < NT:
                    deltas(i + 1)
                n = ROWS[i]
                pe.wait_ge(delta_sb, i + 1)
                if i >= 2:
                    pe.wait_ge(x_mixed[0], i - 1)
                for g in range(len(POOL_WINDOWS)):
                    out = ps[0:n, 4 + 2 * (i % 2) + g // 2, PW * (g % 2):PW * (g % 2 + 1)]
                    for k in range(2):
                        last = mm(out, dT[i % 2][:, 2 * g + k, 0:n], band_w[:, 2 * g + k, :], start=(k == 0), stop=(k == 1))
                last.then_inc(pool_y, 1)

            def route(l):
                ph = 1 + 2 * l
                pe.wait_ge(x_mixed[l], NT)
                transposes(ph, 0)
                pe.wait_ge(router_in[l], 16 * (NG + 3))
                for i in range(NT):
                    if i + 1 < NT:
                        transposes(ph, i + 1)
                    n = ROWS[i]
                    pe.wait_ge(hT_sb, (ph - 1) * NT + i + 1)
                    out = ps[0:n, LOGIT_BANK, i * NR:(i + 1) * NR]
                    for k in range(KT):
                        mm(out, f32(hT_hi[:, k, tok(i)]), rw[:, k, :], start=(k == 0), stop=False)
                        last = mm(out, f32(hT_lo[:, k, tok(i)]), rw[:, k, :], start=False, stop=(k == KT - 1))
                last.then_inc(logit_ps, 1)
                pe.wait_ge(chosen, l + 1)
                pe.wait_ge(hT_sb, (ph - 1) * NT + NT)
                M = r["M"]
                mm(ps[:, 0, 0:NT * NEXP], const("before"), M.rearrange("p i e -> p (i e)"), start=True, stop=True,
                   skip_group_check=True)
                for i in range(NT):
                    for k in range(i + 1, NT + 1):
                        last = mm(ps[:, 0, k * NEXP:(k + 1) * NEXP], const("ones"), M[:, i, :],
                                  start=False, stop=True, skip_group_check=True)
                last.then_inc(ranks_ps, 1)
                pe.wait_ge(slots_ready, l + 1)
                for k in range(2):
                    for i in range(NT):
                        last = mm(ps[0:BLK, 1, 0:3 * NB], r[f"S{k}"][:, i, :],
                                  r[f"V{k}"][:, i, :, :].rearrange("p c b -> p (c b)"),
                                  start=(k == 0 and i == 0), stop=(k == 1 and i == NT - 1))
                last.then_inc(table_ps, 1)

            def block_transposes(u):
                src = xg[u].rearrange("s (c k) -> s k c", k=KT)
                for k in range(KT):
                    last = nc.tensor.transpose(ps[:, XT_BANK, k * BLK:(k + 1) * BLK], src[:, k, :], ident[0:BLK, 0:BLK])
                return last

            def product(bank, quarter, split, used, buf):
                for q in range(QUARTERS):
                    pe.wait_ge(split, quarter + (q + 1))
                    for kk in range(KT // QUARTERS):
                        k = q * KT // QUARTERS + kk
                        at = slice(k * BLK, (k + 1) * BLK)
                        last = split_product(ps[0:BLK, bank, :], xT_hi[:, buf, at], xT_lo[:, buf, at],
                                             w_hi[:, q, kk * 512:(kk + 1) * 512], w_lo[:, q, kk * 512:(kk + 1) * 512],
                                             k == 0, k == KT - 1)
                    last.then_inc(used, 1)

            def down(quarter, split, used):
                for q in range(QUARTERS):
                    pe.wait_ge(split, quarter + (q + 1))
                    at = slice(q * BLK, (q + 1) * BLK)
                    for hf in range(2):
                        half = slice(hf * 512, (hf + 1) * 512)
                        last = split_product(ps[0:BLK, Y_BANK + hf, :], hid_hi[:, at], hid_lo[:, at],
                                             w_hi[:, q, half], w_lo[:, q, half], q == 0, q == FT - 1)
                    last.then_inc(used, 1)

            def hidden_transposes():
                for k in range(FT):
                    last = nc.tensor.transpose(ps[:, HT_BANK, k * BLK:(k + 1) * BLK], hidden[:, k * P:(k + 1) * P],
                                               ident[0:BLK, 0:BLK])
                return last

            def experts(l):
                def transpose_hidden(b, stage):
                    if stage:
                        pe.wait_ge(hidT_sb[l], b)
                    pe.wait_ge(hidden_sb[l], b + 1)
                    pe.sem_inc(wait_carrier, 1)
                    hidden_transposes().then_inc(hidT_ps[l], 1)

                def down_block(b, stage, quarter):
                    pe.wait_ge(hidT_sb[l], b + 1)
                    if stage:
                        pe.wait_ge(y_lo[l], b)
                        pe.wait_ge(y_hi[l], b)
                    down(quarter, split_lo, quarters_used)

                def body(b, par, half, stage):
                    quarter = (first_of_block(l, b) if stage else FIRST[l]) * QUARTERS
                    pe.wait_ge(xT_sb[l], b + 1)
                    if stage:
                        pe.wait_ge(silu_sb[l], b)
                    product(GATE_BANK, quarter, split_lo, quarters_used, par)
                    if stage:
                        transpose_hidden(b - 1, stage - 1)
                    if stage < NEXP - 1:
                        pe.wait_ge(gathered[l][1 - par], (half + par) * 16 + 16)
                        pe.sem_inc(wait_carrier, 1)
                        block_transposes(1 - par).then_inc(xT_ps[l], 1)
                    product(UP_BANK, quarter + QUARTERS, split_lo, quarters_used, par)
                    if stage:
                        down_block(b - 1, stage - 1, quarter + 2 * QUARTERS)

                pe.wait_ge(table_sb, l + 1)
                pe.wait_ge(gathered[l][0], 16)
                block_transposes(0).then_inc(xT_ps[l], 1)
                blocks(pe, body)
                transpose_hidden(NEXP - 1, NEXP - 1)
                down_block(NEXP - 1, NEXP - 1, (FIRST[l] + 3 * NEXP - 1) * QUARTERS)
                n_ovf = pe.value_load(ovf_count[0:1, 0:1], min_val=0, max_val=OVF)
                with pe.If(n_ovf > 0):
                    pe.wait_ge(y_lo[l], NEXP)
                    pe.wait_ge(y_hi[l], NEXP)
                    with pe.Fori(0, n_ovf) as j:
                        pe.wait_ge(o_gathered[l], j * 16 + 16)
                        pe.sem_inc(wait_carrier, 1)
                        block_transposes(0).then_inc(o_xT_ps[l], 1)
                        pe.wait_ge(o_xT_sb[l], j + 1)
                        product(GATE_BANK, j * 12, o_split_lo[l], o_used[l], 0)
                        product(UP_BANK, j * 12 + QUARTERS, o_split_lo[l], o_used[l], 0)
                        pe.wait_ge(o_hidden[l], j + 1)
                        pe.sem_inc(wait_carrier, 1)
                        hidden_transposes().then_inc(o_hidT_ps[l], 1)
                        pe.wait_ge(o_hidT_sb[l], j + 1)
                        down(j * 12 + 2 * QUARTERS, o_split_lo[l], o_used[l])

            route(0)
            experts(0)

            pe.wait_ge(x_done[0], NT)
            for i in range(NT):
                transposes(2, i)
            units = (QKV_PIECES - 2) * NT

            def qk_transposes(m):
                j, i = divmod(m, NT)
                n = ROWS[i]
                pe.wait_ge(q_gained, m + 1)
                if m >= 2:
                    pe.wait_ge(qkT_sb, m - 1)
                for c in range(4):
                    out = ps[:, QKT_BANK + m % 2, 128 * c:128 * c + n]
                    src = qn[m % 4][0:n, 128 * c:128 * (c + 1)]
                    if j < 2:
                        flip = const("flip") if i < NT - 1 else flip_sample[0:n, :]
                        last = mm(out, src, flip, start=True, stop=True)
                    else:
                        last = nc.tensor.transpose(out, src, ident[0:n, 0:n])
                last.then_inc(qkT_ps, 1)

            pe.wait_ge(hT_sb, (2 - 1) * NT + NT)

            def token_product(piece, m0, free, done, between=None):
                for q in range(QUARTERS):
                    pe.wait_ge(split_lo, QUARTERS * piece + q + 1)
                    for i in range(NT):
                        n = ROWS[i]
                        if q == 0:
                            free(m0 + i)
                        for kk in range(KT // QUARTERS):
                            k = q * KT // QUARTERS + kk
                            at = slice(kk * 512, (kk + 1) * 512)
                            last = split_product(ps[0:n, (m0 + i) % RAW_BANKS, :], hT_hi[:, k, tok(i)],
                                                 hT_lo[:, k, tok(i)], w_hi[:, q, at], w_lo[:, q, at],
                                                 k == 0, k == KT - 1)
                        if q == QUARTERS - 1:
                            last.then_inc(done, 1)
                    if q < QUARTERS - 1:
                        last.then_inc(quarters_used, 1)
                    else:
                        pe.wait_ge(done, m0 + NT)
                        pe.sem_inc(quarters_used, 1)
                    if between is not None:
                        between(q)
                if between is not None:
                    between(QUARTERS)

            def raw_free(m):
                m -= RAW_BANKS
                if m >= units:
                    pe.wait_ge(v_sb, m + 1 - units)
                elif m >= 0:
                    pe.wait_ge(q_scaled, m + 1)

            for j in range(QKV_PIECES):
                before = (lambda q, j=j: qk_transposes((j - 1) * NT + q)) if 1 <= j <= QKV_PIECES - 2 else None
                token_product(att_first + j, j * NT, raw_free, raw_ps, before)
            pe.wait_ge(kc_in, 16)
            pe.wait_ge(qkT_sb, units)
            for c in range(KT):
                last = nc.tensor.transpose(ps[:, QKT_BANK + c // 4, 128 * (c % 4):128 * (c % 4 + 1)],
                                           k_cache_nat[:, c * P:(c + 1) * P], ident)
                if c % 4 == 3:
                    last.then_inc(kcT_ps, 1)
            pe.wait_ge(kcT_sb, 2)
            pe.wait_ge(vc_in, 16)
            pe.wait_ge(v_sb, 2 * NT)

            def scores(a):
                h, i = divmod(a, NT)
                n = ROWS[i]
                lo = HD * (h % 2)
                if a >= 2:
                    pe.wait_ge(s_biased, a - 1)
                q = qT[lo:lo + HD, h // 2, tok(i)]
                if i < NT - 1:
                    last = mm(ps[0:n, S_BANK + a % 2, 0:(i + 1) * P], q, kT[lo:lo + HD, h // 2, 0:(i + 1) * P], start=True, stop=True)
                else:
                    mm(ps[0:n, S_BANK + a % 2, 0:KEEP], q, kcT[lo:lo + HD, h // 2, :], start=True, stop=True)
                    last = mm(ps[0:n, S_BANK + a % 2, KEEP:KEEP + SS], q, kT[lo:lo + HD, h // 2, tok(i)], start=True, stop=True)
                last.then_inc(s_ps, 1)

            def p_transposes(a):
                i = a % NT
                n = ROWS[i]
                nk = (i + 1) * P if i < NT - 1 else KEEP + SS
                pe.wait_ge(p_ready, a + 1)
                if a >= 2:
                    pe.wait_ge(pT_ready, a - 1)
                for k in range(-(-nk // P)):
                    w = min(P, nk - k * P)
                    last = nc.tensor.transpose(ps[0:w, PT_BANK + a % 2, k * P:k * P + n],
                                               p_sb[a % 2][0:n, k * P:k * P + w], ident[0:n, 0:n])
                last.then_inc(pT_ps, 1)

            def values(a):
                h, i = divmod(a, NT)
                n = ROWS[i]
                pe.wait_ge(pT_ready, a + 1)
                if a >= 2:
                    pe.wait_ge(o_sb, a - 1)
                out = ps[0:n, O_BANK + a % 2, 0:HD]
                cols_h = slice(h * HD, (h + 1) * HD)
                if i < NT - 1:
                    for k in range(i + 1):
                        last = mm(out, pT_sb[a % 2][:, k * P:(k + 1) * P], v_nat[:, k, cols_h], start=(k == 0), stop=(k == i))
                else:
                    mm(out, pT_sb[a % 2][:, 0:n], v_cache[:, cols_h], start=True, stop=False)
                    last = mm(out, pT_sb[a % 2][0:SS, P:P + n], v_nat[0:SS, i, cols_h], start=False, stop=True)
                last.then_inc(o_ps, 1)

            def pair_out(pr):
                pe.wait_ge(o_sb, 2 * NT * (pr + 1))
                if pr >= 1:
                    pe.wait_ge(oT_sb, pr)
                o = o_nat[pr % 2]
                for i in range(NT):
                    n = ROWS[i]
                    out = ps[:, OT_BANK, i * P:(i + 1) * P] if i < NT - 1 else ps[:, OT_BANK + 1, 0:n]
                    flip = const("flip") if i < NT - 1 else flip_sample[0:n, :]
                    last = mm(out, o[0:n, i, :], flip, start=True, stop=True)
                last.then_inc(oT_ps, 1)

            UNITS = NH * NT
            for a in range(UNITS + 3):
                if a < UNITS:
                    scores(a)
                if 0 <= a - 1 < UNITS:
                    p_transposes(a - 1)
                if 0 <= a - 2 < UNITS:
                    values(a - 2)
                if a - 3 >= 0 and (a - 3) % (2 * NT) == 2 * NT - 1:
                    pair_out((a - 3) // (2 * NT))
            pe.wait_ge(oT_sb, PAIRS)
            pe.wait_ge(o_sb, UNITS)
            def sum_free(m):
                if m >= RAW_BANKS:
                    pe.wait_ge(*((x_half, m - RAW_BANKS + 1) if m - RAW_BANKS < NT else
                                 (x_mixed[1], m - RAW_BANKS + 1 - NT)))

            for hf in range(2):
                token_product(att_first + QKV_PIECES + hf, hf * NT, sum_free, att_y)
            route(1)
            experts(1)


_INS = ["x_prompt", "x_sample", "cache_pool", "cache_k", "cache_v", "norm_mix", "norm_ffn", "pool_w", "pool_scale",
        "attn_w_qkv", "attn_w_o", "attn_q_gain", "attn_k_gain", "moe_w_r1", "moe_b_r1", "moe_w_r2", "moe_b_r2",
        "moe_w_gate", "moe_w_up", "moe_w_down"]


def kernel(**inputs):
    import numpy as _np
    import concourse.bacc as _bacc
    from concourse import mybir as _mybir
    from concourse.bass_utils import run_bass_kernel_spmd as _run

    nc = _bacc.Bacc("TRN2", target_bir_lowering=False, num_devices=1)
    arrays, aps = {}, {}

    def give(name, a):
        a = _np.ascontiguousarray(a)
        arrays[f"in_{name}"] = a
        aps[name] = nc.dram_tensor(f"in_{name}", a.shape, _mybir.dt.from_np(a.dtype), kind="ExternalInput").ap()

    for name in _INS:
        give(name, inputs[name])
    B, S, D = inputs["x_prompt"].shape
    SS = inputs["x_sample"].shape[1]
    T = S + SS
    NEXP = inputs["moe_w_gate"].shape[1]
    NG, _, EPG = inputs["moe_w_r2"].shape[1:]
    distance = (S - 1) - _np.arange(S + P - 1)
    index = _np.clip(distance, -(CHUNK - 1), REL_MAX) + CHUNK - 1
    give("rel_bias_reversed", _np.asarray(inputs["attn_rel_bias"])[0][:, index])
    consts, bands, cols = shape_constants(T, -(-T // P), NEXP + (2 * T - 1) // BLK, NEXP, EPG, NG)
    give("consts", consts)
    give("bands", bands)

    NH, HD = inputs["cache_k"].shape[3:]
    hist = inputs["cache_pool"].shape[2]
    shapes = [(1, S, D), (1, SS, D), (1, 1, hist, D), (1, 1, hist, D),
              (1, 1, S, NH, HD), (1, 1, S, NH, HD), (1, 1, SS, NH, HD), (1, 1, SS, NH, HD)]
    outs = [nc.dram_tensor(f"out_{i}", s, F32, kind="ExternalOutput").ap() for i, s in enumerate(shapes)]
    encoder(nc, aps, outs, cols)
    res = _run(nc, [arrays], core_ids=[0])
    return tuple(res.results[0][f"out_{i}"] for i in range(len(shapes)))
```

```python
from contextlib import ExitStack

import numpy as np

import concourse.bass as bass
from concourse import mybir

P = 128
F32 = mybir.dt.float32
F32R = mybir.dt.float32r
I32 = mybir.dt.int32
ALU = mybir.AluOpType
ACT = mybir.ActivationFunctionType
AX = mybir.AxisListType

EPS = 1e-6
POOL_WINDOWS = (2, 4, 8, 16)
HIST = max(POOL_WINDOWS) - 1
HALO = 16
BLK = 64
NEG = -1e30
PAD = 4096.0
CHUNK = 64
REL_MAX = 256


def shape_constants(T, NT, NB, NEXP, EPG, NG):
    cols, parts = {}, []

    def put(name, a):
        a = np.asarray(a, np.float32)
        if a.ndim == 1:
            a = np.broadcast_to(a, (P, a.size))
        a = a.reshape(P, -1)
        at = sum(x.shape[1] for x in parts)
        cols[name] = (at, a.shape[1])
        parts.append(a)

    p = np.arange(P)
    put("ident", np.eye(P))
    put("flip", np.eye(P)[::-1])
    put("before", p[:, None] < p[None, :])
    put("ones", np.ones((P, P)))
    d = p[None, :] - p[:, None]
    bands = []
    for g, w in enumerate(POOL_WINDOWS):
        inside = (d >= 0) & (d < w)
        bands += [inside / np.float32(w) - np.eye(P),
                  inside / np.minimum(p + 1, w)[None, :].astype(np.float32) - np.eye(P)]
        put(f"band_halo{g}", ((d + P < w)[:, :HALO]) / np.float32(w))
    tok = np.arange(NT)[None, :] * P + p[:, None]
    put("valid", tok < T)
    put("token", (tok - PAD) * (tok < T))
    put("row", np.concatenate([2 * tok - PAD, 2 * tok + 1 - PAD], 1) * np.concatenate([tok < T] * 2, 1))
    put("rank_group", NG - np.arange(NG))
    put("rank_expert", EPG - np.arange(EPG))
    put("iota_expert", np.arange(NEXP))
    put("iota_slot", np.arange(BLK))
    put("iota_block", np.arange(NB))
    put("steps", BLK * (1 + np.arange(-(-T // BLK))))
    put("eps", np.full(1, EPS))
    return np.concatenate(parts, 1), np.concatenate(bands, 1).astype(np.float32), cols


def encoder(nc, A, O, cols):
    S, D = A["x_prompt"].shape[1:]
    SS = A["x_sample"].shape[1]
    T = S + SS
    NT = -(-T // P)
    ROWS = [P] * (NT - 1) + [SS]
    assert S == (NT - 1) * P and SS == 32 and T == S + SS
    KT = D // P
    NH, HD = A["cache_k"].shape[3:]
    PAIRS = NH // 2
    KEEP = A["cache_k"].shape[2]
    L, NEXP, _, FE = A["moe_w_gate"].shape
    FT = FE // P
    NG = A["moe_w_r1"].shape[2]
    EPG = A["moe_w_r2"].shape[3]
    NR = NG + NEXP
    OVF = (2 * T - 1) // BLK
    NB = NEXP + OVF
    STEPS = -(-T // BLK)
    PW = D // len(POOL_WINDOWS)
    XROWS, YROWS = T, 2 * T
    SLOTS = 3
    QUARTERS = 4
    SLOT = KT * 512
    QUART = SLOT // QUARTERS
    assert FE == 512 and FT * D == SLOT and KEEP == P
    ATT_PIECES = 3 * D // 512 + D // 512
    QKV_PIECES = 3 * D // 512

    xn_dram = [nc.dram_tensor(f"xn{l}", (XROWS, D), F32, kind="Internal").ap() for l in range(L)]
    yb_dram = [nc.dram_tensor(f"yb{l}", (YROWS, D), F32, kind="Internal").ap() for l in range(L)]

    ctx = ExitStack()
    with ctx:
        def sb(name, shape, dt=F32):
            return ctx.enter_context(nc.sbuf_tensor(name, shape, dt))

        def sem(name):
            return ctx.enter_context(nc.semaphore(name))

        def per_layer(name):
            return [sem(f"{name}_{l}") for l in range(L)]

        ring = sb("ring", [P, SLOTS, SLOT])
        w_hi = sb("w_hi", [P, QUARTERS, QUART], F32R)
        w_lo = sb("w_lo", [P, QUARTERS, QUART], F32R)
        x = sb("x", [P, NT, D])
        nat = sb("nat", [P, NT * D])
        hT_hi = sb("hT_hi", [P, KT, T], F32R)
        hT_lo = sb("hT_lo", [P, KT, T], F32R)
        xT_hi = sb("xT_hi", [P, 2, KT * BLK], F32R)
        xT_lo = sb("xT_lo", [P, 2, KT * BLK], F32R)
        hid_hi = sb("hid_hi", [P, FT * BLK], F32R)
        hid_lo = sb("hid_lo", [P, FT * BLK], F32R)
        qk = sb("qk", [P, 2, KT * T])
        gain = sb("gain", [P, D])
        cst = sb("cst", [P, A["consts"].shape[1]])
        qk_gain = sb("qk_gain", [P, 2, HD])
        ssq = sb("ssq", [P, 4, NT])
        std = sb("std", [P, 4, NT])
        rstd = sb("rstd", [P, 4, NT])
        idx_gather = sb("idx_gather", [BLK, NB], I32)
        idx_scatter = sb("idx_scatter", [BLK, NB], I32)
        slot_gate = sb("slot_gate", [BLK, NB])
        ovf_expert = sb("ovf_expert", [1, OVF], I32)
        ovf_count = sb("ovf_count", [1, 1], I32)
        gcol = [sb(f"gcol{u}", [BLK, 1], I32) for u in range(2)]
        scol = [sb(f"scol{u}", [BLK, 1], I32) for u in range(2)]
        ps = ctx.enter_context(nc.psum_tensor("ps", [P, 8, 512], F32))

        def const(name, rows=P):
            at, n = cols[name]
            return cst[0:rows, at:at + n]

        ident = const("ident")
        flip_sample = const("flip")[0:SS, P - SS:P]

        up_hi, up_lo = (h[:, :, :].rearrange("p k t -> p (k t)")[:, 0:SLOT].rearrange("p (q n) -> p q n", q=QUARTERS)
                        for h in (hT_hi, hT_lo))

        pool_h = nat[:, :].rearrange("p (i d) -> p i d", i=NT)
        v_nat = pool_h
        xg = [nat[0:BLK, u * D:(u + 1) * D] for u in range(2)]
        yb = [nat[0:BLK, (2 + u) * D:(3 + u) * D] for u in range(2)]
        qk_flat = qk[:, :, :].rearrange("p a n -> p (a n)")
        qT = qk[:, 0, :].rearrange("p (c t) -> p c t", c=PAIRS)
        kT = qk[:, 1, :].rearrange("p (c t) -> p c t", c=PAIRS)
        rows_h = qk_flat[:, 0:NT * D].rearrange("p (i d) -> p i d", i=NT)
        at = NT * D
        silu = qk_flat[0:BLK, at:at + FE]
        hidden = qk_flat[0:BLK, at + FE:at + 2 * FE]
        route_at = at + 2 * FE
        yc = [nat[:, 0:2 * D], nat[:, 2 * D:4 * D], qk_flat[:, route_at:route_at + 2 * D], rows_h[:, 3:5, :].rearrange(
            "p a d -> p (a d)")]
        assert NT == len(yc) + 1
        pool_gain = qk_flat[:, 0:D]
        pool_scale = qk_flat[:, D:2 * D]
        hist = qk_flat[:, 2 * D:3 * D]
        band_w = qk_flat[:, 3 * D:3 * D + 2 * PW * len(POOL_WINDOWS)].rearrange(
            "p (c n) -> p c n", c=2 * len(POOL_WINDOWS))
        y_tmp = qk_flat[:, 3 * D + 2 * PW * len(POOL_WINDOWS):4 * D + 2 * PW * len(POOL_WINDOWS)]
        dT_at = 4 * D + 2 * PW * len(POOL_WINDOWS)
        dT = [qk_flat[:, dT_at + u * D:dT_at + (u + 1) * D].rearrange("p (c t) -> p c t", c=KT) for u in range(2)]
        assert dT_at + 2 * D <= 2 * KT * T

        taken = {"nat": 2 * D, "qk": route_at}

        def scratch(where, *shape):
            n = int(np.prod(shape))
            flat = nat[:, :] if where == "nat" else qk_flat
            a = flat[:, taken[where]:taken[where] + n]
            taken[where] += n
            assert taken[where] <= (NT * D if where == "nat" else 2 * KT * T), where
            names = "abcd"[:len(shape)]
            if len(shape) > 1:
                a = a.rearrange(f"p ({' '.join(names)}) -> p {' '.join(names)}", **dict(zip(names, shape)))
            return a

        PT = 2 * NT
        r = {}
        for name in ("m1", "s1", "pg", "kk", "ma", "mb", "dg", "eg", "den", "rden"):
            r[name] = scratch("nat", NT)
        for name in ("gate", "exp", "step", "slot", "blk", "away"):
            r[name] = scratch("nat", PT)
        r["pos_off"] = scratch("nat", 2, PT)
        r["A"] = scratch("nat", 2, NT, NEXP)
        r["V"] = scratch("nat", 2, NT, 3, NB)
        r["logit"] = scratch("nat", NT, NR)
        for name in ("d1", "e1", "eq1", "oh1"):
            r[name] = scratch("nat", NT, NG)
        for name in ("l2", "l2b", "eq2", "a0", "a1"):
            r[name] = scratch("nat", NT, EPG)
        r["M"] = scratch("nat", NT, NEXP)
        for name in ("extra", "incl", "offs"):
            r[name] = scratch("nat", NEXP)
        r["S"] = scratch("qk", PT, BLK)
        r["logT"] = scratch("qk", T)
        r["tmp"] = scratch("qk", max(2 * PT * NEXP, NEXP * STEPS, OVF * NEXP))
        r["tmp2"] = scratch("qk", max(PT * NB, OVF * NEXP))
        r["bias"] = sb("router_bias", [P, NR])[:, :]
        rw = sb("rw", [P, KT, NR])
        rw_hi = xT_hi[:, 0, 0:KT * NR].rearrange("p (k c) -> p k c", k=KT)
        rw_lo = xT_lo[:, 0, 0:KT * NR].rearrange("p (k c) -> p k c", k=KT)

        a4 = ring[:, 1, :]
        a5 = ring[:, 2, :]
        k_cache_nat = gain[:, :]
        kcT = a4[:, 0:PAIRS * KEEP].rearrange("p (c t) -> p c t", c=PAIRS)
        v_cache = a4[:, D:2 * D]
        o_nat = [a4[:, 2 * D + u * NT * P:2 * D + (u + 1) * NT * P].rearrange("p (i c) -> p i c", i=NT)
                 for u in range(2)]
        small = a4[:, 2 * D + 2 * NT * P:2 * D + 2 * NT * P + 64]
        bias_h = [a5[:, u * 512:(u + 1) * 512] for u in range(2)]
        s_sb = [a5[:, (2 + u) * 512:(3 + u) * 512] for u in range(2)]
        p_sb = [a5[:, 2048:2560], a5[:, 2560:3072], a4[:, SLOT - 512:SLOT]]
        pT_sb = [a5[:, (6 + u) * 512:(7 + u) * 512] for u in range(2)]
        sq = [nat[:, u * 512:(u + 1) * 512] for u in range(2)]
        qn = [nat[:, (2 + u) * 512:(3 + u) * 512] for u in range(NT)]
        qstat = nat[:, (2 + NT) * 512:(2 + NT) * 512 + 64]

        x_in = [sem(f"x_in{i}") for i in range(NT)]
        zeroed = sem("zeroed")
        hist_in = sem("hist_in")
        consts_in = sem("consts_in")
        bands_in = sem("bands_in")
        pool_gain_in = sem("pool_gain_in")
        pool_maps_in = sem("pool_maps_in")
        gain_in = sem("gain_in")
        router_in = per_layer("router_in")
        piece_in = [sem(f"piece_in{s}") for s in range(SLOTS)]
        split_hi = sem("split_hi")
        split_lo = sem("split_lo")
        quarters_used = sem("quarters_used")
        act_own = sem("act_own")
        dve_own = sem("dve_own")
        std_ready = sem("std_ready")
        h_ready = sem("h_ready")
        delta_ps = sem("delta_ps")
        delta_sb = sem("delta_sb")
        pool_y = sem("pool_y")
        x_mixed = per_layer("x_mixed")
        rows_out = sem("rows_out")
        hT_ps = sem("hT_ps")
        hT_hi_sb = sem("hT_hi_sb")
        hT_sb = sem("hT_sb")
        xn_stored = per_layer("xn_stored")
        rw_hi_sb = sem("rw_hi_sb")
        rw_sb = sem("rw_sb")
        logT_ps = sem("logT_ps")
        logT_sb = sem("logT_sb")
        logit_ps = sem("logit_ps")
        route_exp_in = sem("route_exp_in")
        route_exp = sem("route_exp")
        chosen = sem("chosen")
        ranks_ps = sem("ranks_ps")
        slots_ready = sem("slots_ready")
        table_ps = sem("table_ps")
        table_sb = sem("table_sb")
        gcol_set = per_layer("gcol_set")
        scol_set = per_layer("scol_set")
        gathered = [[sem(f"gathered{l}_{u}") for u in range(2)] for l in range(L)]
        xT_ps = per_layer("xT_ps")
        xT_hi_sb = per_layer("xT_hi_sb")
        xT_sb = per_layer("xT_sb")
        hidT_ps = per_layer("hidT_ps")
        hidT_hi_sb = per_layer("hidT_hi_sb")
        hidT_sb = per_layer("hidT_sb")
        silu_sb = per_layer("silu_sb")
        hidden_sb = per_layer("hidden_sb")
        y_lo = per_layer("y_lo")
        y_hi = per_layer("y_hi")
        scattered = [[sem(f"scattered{l}_{u}") for u in range(2)] for l in range(L)]
        o_piece_in = per_layer("o_piece_in")
        o_col = per_layer("o_col")
        o_gathered = per_layer("o_gathered")
        o_xT_ps = per_layer("o_xT_ps")
        o_xT_hi = per_layer("o_xT_hi")
        o_xT_sb = per_layer("o_xT_sb")
        o_split_hi = per_layer("o_split_hi")
        o_split_lo = per_layer("o_split_lo")
        o_used = per_layer("o_used")
        o_hidT_ps = per_layer("o_hidT_ps")
        o_hidT_hi = per_layer("o_hidT_hi")
        o_hidT_sb = per_layer("o_hidT_sb")
        o_silu = per_layer("o_silu")
        o_hidden = per_layer("o_hidden")
        o_y_lo = per_layer("o_y_lo")
        o_y_hi = per_layer("o_y_hi")
        o_scattered = per_layer("o_scattered")
        yc_in = [sem(f"yc_in{i}") for i in range(NT)]
        yc_sum = sem("yc_sum")
        x_done = per_layer("x_done")
        qk_gain_in = sem("qk_gain_in")
        raw_ps = sem("raw_ps")
        q_sq = sem("q_sq")
        q_ssq = sem("q_ssq")
        q_std = sem("q_std")
        q_scaled = sem("q_scaled")
        q_gained = sem("q_gained")
        qkT_ps = sem("qkT_ps")
        qkT_sb = sem("qkT_sb")
        v_sb = sem("v_sb")
        k_out = [sem(f"k_out{i}") for i in range(NT)]
        v_out = sem("v_out")
        k_cache_in = sem("k_cache_in")
        v_cache_in = sem("v_cache_in")
        kcT_ps = sem("kcT_ps")
        kcT_sb = sem("kcT_sb")
        bias_in = [sem(f"bias_in{u}") for u in range(2)]
        bias_ready = sem("bias_ready")
        s_ps = sem("s_ps")
        s_biased = sem("s_biased")
        p_ready = sem("p_ready")
        pT_ps = sem("pT_ps")
        pT_ready = sem("pT_ready")
        o_ps = sem("o_ps")
        o_sb = sem("o_sb")
        oT_ps = sem("oT_ps")
        oT_hi_sb = sem("oT_hi_sb")
        oT_sb = sem("oT_sb")
        att_y = sem("att_y")
        x_half = sem("x_half")
        wait_carrier = sem("wait_carrier")

        wg = A["moe_w_gate"].rearrange("l e (p k) f -> (l e) p (k f)", k=KT)
        wu = A["moe_w_up"].rearrange("l e (p k) f -> (l e) p (k f)", k=KT)
        wd = A["moe_w_down"].rearrange("l e (k p) d -> (l e) p k d", p=P)
        wqkv = A["attn_w_qkv"][0].rearrange("(p k) e -> p k e", k=KT)
        wo = A["attn_w_o"][0].rearrange("(k p) d -> p k d", p=P)
        x_rows = A["x_prompt"][0]
        xs_rows = A["x_sample"][0]
        rel_t = A["rel_bias_reversed"]
        REL_W = rel_t.shape[1]

        def x_source(i):
            return x_rows[i * P:(i + 1) * P, :] if i < NT - 1 else xs_rows

        def tok(i):
            return slice(i * P, i * P + ROWS[i])

        FIRST = [0, 3 * NEXP + ATT_PIECES]
        att_first = 3 * NEXP

        def first_of_block(l, b):
            return b * 3 + (FIRST[l] - 1)

        GATE, UP, DOWN = range(3)

        def landed(l, b, m):
            at = FIRST[l] - 1 + m
            return at % SLOTS, b * 16 + 16 * (at // SLOTS + 1)

        def pool_sums(l, i):
            return l == 0 or i % 2 == 1

        def sums_before(l, i):
            return l * NT + len([k for k in range(i) if pool_sums(l, k)])

        def f32(a):
            return a.bitcast(F32)

        BLOCKS_PEELED = 5

        def blocks(eng, body):
            for b in range(BLOCKS_PEELED):
                body(b, b % 2, b // 2, b)
            with eng.Fori(BLOCKS_PEELED // 2, NEXP // 2 - 1) as it:
                for u in range(2):
                    body(it * 2 + (1 + u), (1 + u) % 2, it + u, BLOCKS_PEELED)
            body(NEXP - 1, 1, NEXP // 2 - 1, NEXP - 1)

        XT_BANK, GATE_BANK, UP_BANK, HT_BANK, Y_BANK = 0, 1, 2, 3, 4
        S_BANK, PT_BANK, O_BANK, OT_BANK = 0, 2, 4, 6
        RAW_BANKS, QKT_BANK = 6, 6
        QK_TILES = [(0, 1), (2, 3), (4,)]
        LOGT_BANK, LOGIT_BANK = 4, 6
        LOGIT_TILES = [(0, 2), (2, NT)]

        block = ctx.enter_context(nc.Block())

        @block.sync
        def _(sp):
            sp.dma_start(cst[:, :], A["consts"]).then_inc(consts_in, 16)
            for i in range(NT):
                sp.dma_start(x[0:ROWS[i], i, :], x_source(i)).then_inc(x_in[i], 16)
                if i == 0:
                    sp.dma_start(pool_gain, A["norm_mix"][0:1, :].broadcast_to((P, D))).then_inc(pool_gain_in, 16)
                    sp.dma_start(gain[:, :], A["bands"]).then_inc(bands_in, 16)
                if i == 1:
                    sp.dma_start(band_w, A["pool_w"][0].rearrange("g (k p) n -> p (g k) n", p=P)).then_inc(pool_maps_in, 16)
                    sp.dma_start(pool_scale, A["pool_scale"][0:1, :].broadcast_to((P, D))).then_inc(pool_maps_in, 16)
            sp.wait_ge(zeroed, 1)
            sp.dma_start(hist[P - HIST:P, :], A["cache_pool"][0, 0]).then_inc(hist_in, 16)

            def slot_free(n):
                if n >= SLOTS:
                    sp.wait_ge(split_lo, QUARTERS * (n - SLOTS + 1))

            def expert_piece(e, m, s):
                to = ring[:, s, :]
                src = (wg, wu, wd)[m][bass.ds(e, 1)]
                if m == DOWN:
                    return to.rearrange("p (k d) -> p k d", k=FT), src.rearrange("e p k d -> (e p) k d")
                return to, src.rearrange("e p n -> (e p) n")

            for l in range(L):
                first = FIRST[l]
                order = [(GATE, 0), (UP, 0)] + [(m, b - (m == DOWN)) for b in range(1, 3) for m in range(3)]
                for k, (m, b) in enumerate(order):
                    n = first + k
                    slot_free(n)
                    if l == 1 and k == 0:
                        sp.wait_ge(oT_sb, PAIRS)
                    to, src = expert_piece(l * NEXP + b, m, n % SLOTS)
                    sp.dma_start(to, src).then_inc(piece_in[n % SLOTS], 16)
                with sp.Fori(3, NEXP) as b:
                    for m in range(3):
                        s, _ = landed(l, b, m)
                        to, src = expert_piece(b + (l * NEXP - (m == DOWN)), m, s)
                        sp.wait_ge(split_lo, b * (3 * QUARTERS) + QUARTERS * (first - 1 + m - SLOTS + 1))
                        sp.dma_start(to, src).then_inc(piece_in[s], 16)
                n = first + 3 * NEXP - 1
                slot_free(n)
                to, src = expert_piece(l * NEXP + NEXP - 1, DOWN, n % SLOTS)
                sp.dma_start(to, src).then_inc(piece_in[n % SLOTS], 16)
                sp.wait_ge(table_sb, l + 1)
                n_ovf = sp.value_load(ovf_count[0:1, 0:1], min_val=0, max_val=OVF)
                with sp.If(n_ovf > 0):
                    sp.wait_ge(split_lo, QUARTERS * (first + 3 * NEXP))
                    with sp.Fori(0, n_ovf) as j:
                        e = sp.value_load(ovf_expert[0:1, bass.ds(j, 1)], min_val=0, max_val=NEXP - 1)
                        for m in range(3):
                            to, src = expert_piece(e + l * NEXP, m, m)
                            sp.dma_start(to, src).then_inc(o_piece_in[l], 16)
                        sp.wait_ge(o_split_lo[l], j * 12 + 12)
                        sp.sem_inc(wait_carrier, 1)
                if l == 0:
                    for j in range(ATT_PIECES):
                        n = att_first + j
                        slot_free(n)
                        if j == 2:
                            sp.wait_ge(yc_in[len(yc) - 1], 16)
                        if j == ATT_PIECES - 1:
                            sp.wait_ge(oT_sb, PAIRS)
                        to = ring[:, n % SLOTS, :].rearrange("p (k e) -> p k e", k=KT)
                        src = (wqkv[:, :, j * 512:(j + 1) * 512] if j < QKV_PIECES
                               else wo[:, :, (j - QKV_PIECES) * 512:(j - QKV_PIECES + 1) * 512])
                        sp.dma_start(to, src).then_inc(piece_in[n % SLOTS], 16)

        def piece_count(n):
            return 16 * (n // SLOTS + 1)

        @block.gpsimd
        def _(pool):
            pool.memset(hist, 0.0).then_inc(zeroed, 1)
            rw1 = lambda l: A["moe_w_r1"][l].rearrange("(p k) g -> p k g", k=KT)
            rw2 = lambda l, g: A["moe_w_r2"][l, g].rearrange("(p k) e -> p k e", k=KT)

            def load_router(l):
                pool.dma_start(rw[:, :, 0:NG], rw1(l)).then_inc(router_in[l], 16)
                for g in range(NG):
                    pool.dma_start(rw[:, :, NG + g * EPG:NG + (g + 1) * EPG], rw2(l, g)).then_inc(router_in[l], 16)
                group_bias = A["moe_b_r1"][l:l + 1, :]
                expert_bias = A["moe_b_r2"][l:l + 1].rearrange("o g e -> o (g e)")
                pool.dma_start(r["bias"][:, 0:NG], group_bias.broadcast_to((P, NG))).then_inc(router_in[l], 16)
                pool.dma_start(r["bias"][:, NG:NR], expert_bias.broadcast_to((P, NEXP))).then_inc(router_in[l], 16)

            def gather(l, j, v, half, stage):
                if stage >= 2:
                    pool.wait_ge(gathered[l][v], half * 16)
                pool.tensor_copy(gcol[v][:, :], idx_gather[:, bass.ds(j, 1)]).then_inc(gcol_set[l], 1)
                if stage >= 2:
                    pool.wait_ge(xT_ps[l], j - 1)
                pool.wait_ge(gcol_set[l], j + 1)
                pool.sem_inc(wait_carrier, 1)
                pool.indirect_dma_start(
                    out=xg[v], out_offset=None, in_=xn_dram[l],
                    in_offset=bass.IndirectOffsetOnAxis(ap=gcol[v][:, :], axis=0),
                    bounds_check=XROWS - 1, oob_is_err=False).then_inc(gathered[l][v], 16)

            def scatter(l, j, v, half, stage):
                if stage >= 2:
                    pool.wait_ge(scattered[l][v], half * 16)
                pool.tensor_copy(scol[v][:, :], idx_scatter[:, bass.ds(j, 1)]).then_inc(scol_set[l], 1)
                pool.wait_ge(scol_set[l], j + 1)
                pool.wait_ge(y_lo[l], j + 1)
                pool.wait_ge(y_hi[l], j + 1)
                pool.sem_inc(wait_carrier, 1)
                pool.indirect_dma_start(
                    out=yb_dram[l], out_offset=bass.IndirectOffsetOnAxis(ap=scol[v][:, :], axis=0),
                    in_=yb[v], in_offset=None,
                    bounds_check=YROWS - 1, oob_is_err=False).then_inc(scattered[l][v], 16)

            def experts(l):
                pool.wait_ge(x_mixed[l], NT)
                if l == 1:
                    pool.wait_ge(v_out, 16 * 2 * NT)
                for u in range(2):
                    last = pool.memset(xg[u], 0.0)
                last.then_inc(zeroed, 1)
                pool.wait_ge(zeroed, l + 2)
                pool.wait_ge(table_sb, l + 1)
                pool.wait_ge(xn_stored[l], 16 * NT)
                gather(l, 0, 0, 0, 0)

                def body(b, par, half, stage):
                    if stage < NEXP - 1:
                        gather(l, b + 1, 1 - par, half + par, stage + 1)
                    if stage >= 2:
                        scatter(l, b - 2, par, half - 1, stage - 2)

                blocks(pool, body)
                for j in (NEXP - 2, NEXP - 1):
                    scatter(l, j, j % 2, j // 2, j)
                n_ovf = pool.value_load(ovf_count[0:1, 0:1], min_val=0, max_val=OVF)
                with pool.If(n_ovf > 0):
                    for u in range(2):
                        pool.wait_ge(gathered[l][u], 16 * (NEXP // 2))
                        pool.wait_ge(scattered[l][u], 16 * (NEXP // 2))
                    pool.wait_ge(xT_ps[l], NEXP)
                    with pool.Fori(0, n_ovf) as j:
                        pool.tensor_copy(gcol[0][:, :], idx_gather[:, bass.ds(j + NEXP, 1)]).then_inc(o_col[l], 1)
                        pool.tensor_copy(scol[0][:, :], idx_scatter[:, bass.ds(j + NEXP, 1)]).then_inc(o_col[l], 1)
                        pool.wait_ge(o_col[l], 2 * j + 2)
                        pool.sem_inc(wait_carrier, 1)
                        pool.indirect_dma_start(
                            out=xg[0], out_offset=None, in_=xn_dram[l],
                            in_offset=bass.IndirectOffsetOnAxis(ap=gcol[0][:, :], axis=0),
                            bounds_check=XROWS - 1, oob_is_err=False).then_inc(o_gathered[l], 16)
                        pool.wait_ge(o_y_lo[l], j + 1)
                        pool.wait_ge(o_y_hi[l], j + 1)
                        pool.sem_inc(wait_carrier, 1)
                        pool.indirect_dma_start(
                            out=yb_dram[l], out_offset=bass.IndirectOffsetOnAxis(ap=scol[0][:, :], axis=0),
                            in_=yb[0], in_offset=None,
                            bounds_check=YROWS - 1, oob_is_err=False).then_inc(o_scattered[l], 16)
                        pool.wait_ge(o_scattered[l], j * 16 + 16)
                        pool.sem_inc(wait_carrier, 1)
                for u in range(2):
                    pool.wait_ge(scattered[l][u], 16 * (NEXP // 2))

            def combine_rows(l):
                def load(i):
                    n = ROWS[i]
                    pool.dma_start(yc[i % len(yc)][0:n, :], yb_dram[l][2 * i * P:2 * (i * P + n), :].rearrange(
                        "(t k) d -> t (k d)", k=2)).then_inc(yc_in[i], 16)

                for i in range(len(yc)):
                    load(i)
                for i in range(NT):
                    pool.wait_ge(yc_in[i], 16 * (l + 1))
                    if i:
                        pool.wait_ge(yc_sum, sums_before(l, i))
                    rows = yc[i % len(yc)][0:ROWS[i], :]
                    if pool_sums(l, i):
                        pool.tensor_tensor(rows[:, 0:D], rows[:, 0:D], rows[:, D:2 * D], ALU.add).then_inc(yc_sum, 1)
                    if i == 1:
                        pool.wait_ge(x_done[l], 1)
                        load(len(yc))

            load_router(0)
            experts(0)
            combine_rows(0)
            load_router(1)

            units = (QKV_PIECES - 2) * NT
            for m in range(units):
                j, i = divmod(m, NT)
                n = ROWS[i]
                if m == 0:
                    pool.wait_ge(qk_gain_in, 32)
                pool.wait_ge(q_scaled, m + 1)
                v = qn[m % NT][0:n, :].rearrange("p (h d) -> p h d", d=HD)
                g = qk_gain[0:n, j // 2, :].unsqueeze(1).broadcast_to((n, 512 // HD, HD))
                pool.tensor_tensor(v, v, g, ALU.mult).then_inc(q_gained, 1)
                if j >= 2:
                    pool.wait_ge(q_gained, m + 1)
                    half = slice((j - 2) * 512, (j - 1) * 512)
                    dst = (O[4][0, 0].rearrange("t h d -> t (h d)")[i * P:(i + 1) * P, half] if i < NT - 1
                           else O[6][0, 0].rearrange("t h d -> t (h d)")[:, half])
                    pool.dma_start(dst, qn[m % NT][0:n, :]).then_inc(k_out[i], 16)
            def store_v(j):
                half = slice(j * 512, (j + 1) * 512)
                for i in range(NT):
                    pool.wait_ge(v_sb, j * NT + i + 1)
                    dst = (O[5][0, 0].rearrange("t h d -> t (h d)")[i * P:(i + 1) * P, half] if i < NT - 1
                           else O[7][0, 0].rearrange("t h d -> t (h d)")[:, half])
                    pool.dma_start(dst, v_nat[0:ROWS[i], i, half]).then_inc(v_out, 16)

            def load_bias(h):
                if h >= 2:
                    pool.wait_ge(s_biased, NT * (h - 1))
                pool.dma_start(bias_h[h % 2], bass.AP(tensor=rel_t.tensor, offset=h * REL_W,
                                                      ap=[[1, P], [1, 512]])).then_inc(bias_in[h % 2], 16)

            store_v(0)
            pool.wait_ge(split_lo, QUARTERS * (att_first + QKV_PIECES))
            pool.dma_start(v_cache, A["cache_v"][0, 0].rearrange("t h d -> t (h d)")).then_inc(v_cache_in, 16)
            for h in range(2):
                load_bias(h)

            def scale_bias(h):
                pool.wait_ge(bias_in[h % 2], 16 * (h // 2 + 1))
                if h:
                    pool.wait_ge(bias_ready, 2 * h)
                pool.tensor_scalar(bias_h[h % 2], bias_h[h % 2], float(HD) ** 0.5, None, ALU.mult).then_inc(bias_ready, 1)
                pool.wait_ge(bias_ready, 2 * h + 1)
                pool.memset(bias_h[h % 2][CHUNK:P, 512 - CHUNK:512], NEG).then_inc(bias_ready, 1)

            scale_bias(0)
            store_v(1)
            for h in range(1, NH):
                scale_bias(h)
                if h + 1 < NH:
                    load_bias(h + 1)
            experts(1)
            combine_rows(1)
            pool.wait_ge(rows_out, 32 + 16 * NT)
            pool.wait_ge(v_out, 16 * 2 * NT)
            for i in range(NT):
                pool.wait_ge(k_out[i], 32)

        @block.scalar
        def _(act):
            own = [0]

            def link(ins):
                own[0] += 1
                ins.then_inc(act_own, 1)
                act.wait_ge(act_own, own[0])

            def root_mean_square(ph, i, out):
                n = ROWS[i]
                link(act.activation(out, x[0:n, i, :], ACT.Square, accum_out=ssq[0:n, ph, i:i + 1]))
                act.activation(std[0:n, ph, i:i + 1], ssq[0:n, ph, i:i + 1], ACT.Sqrt,
                               bias=const("eps", n), scale=1.0 / D).then_inc(std_ready, 1)

            def split_piece(s, value, quarter, behind=QUARTERS):
                act.wait_ge(piece_in[s], value)
                for q in range(QUARTERS):
                    act.wait_ge(quarters_used, quarter + (q - behind + 1))
                    act.activation(w_hi[:, q, :], ring[:, s, q * QUART:(q + 1) * QUART], ACT.Copy).then_inc(split_hi, 1)

            def split_static(n, quarters=range(QUARTERS)):
                for q in quarters:
                    act.wait_ge(piece_in[n % SLOTS], piece_count(n))
                    if n > 0:
                        act.wait_ge(quarters_used, QUARTERS * n + q - QUARTERS + 1)
                    act.activation(w_hi[:, q, :], ring[:, n % SLOTS, q * QUART:(q + 1) * QUART],
                                   ACT.Copy).then_inc(split_hi, 1)

            def transpose_out(ph, i):
                n = ROWS[i]
                act.wait_ge(hT_ps, (ph - 1) * NT + i + 1)
                b = 2 * (i % 2)
                act.activation(hT_hi[:, 0:KT, i * P:i * P + n],
                               ps[:, b:b + 2, :].rearrange("p b (c t) -> p (b c) t", c=4)[:, :, 0:n],
                               ACT.Copy).then_inc(hT_hi_sb, 1)

            act.wait_ge(consts_in, 16)
            for i in range(NT):
                act.wait_ge(x_in[i], 16)
                root_mean_square(0, i, pool_h[0:ROWS[i], i, :])
            act.wait_ge(h_ready, NT)
            act.dma_start(O[2][0, 0], pool_h[P - HIST:P, NT - 2, :]).then_inc(rows_out, 16)
            act.dma_start(O[3][0, 0], pool_h[SS - HIST:SS, NT - 1, :]).then_inc(rows_out, 16)
            for i in range(NT):
                n = ROWS[i]
                act.wait_ge(delta_ps, i + 1)
                b = 2 * (i % 2)
                if i >= 2:
                    act.wait_ge(pool_y, i - 1)
                act.activation(dT[i % 2][:, :, 0:n],
                               ps[:, b:b + 2, :].rearrange("p b (c t) -> p (b c) t", c=4)[:, :, 0:n],
                               ACT.Copy).then_inc(delta_sb, 1)
            act.dma_start(gain[:, :], A["norm_ffn"][0:1, :].broadcast_to((P, D))).then_inc(gain_in, 16)

            def route_rows(l):
                ph = 1 + 2 * l
                act.wait_ge(router_in[l], 16 * (NG + 3))
                act.activation(rw_hi, rw[:, :, :], ACT.Copy).then_inc(rw_hi_sb, 1)
                for i in range(NT + 1):
                    if i < NT:
                        act.wait_ge(x_mixed[l], i + 1)
                        if i == 0 and l == 0:
                            act.wait_ge(x_mixed[0], NT)
                        root_mean_square(ph, i, rows_h[0:ROWS[i], i, :])
                    if i > 0:
                        k = i - 1
                        act.wait_ge(h_ready, ph * NT + k + 1)
                        act.dma_start(xn_dram[l][k * P:k * P + ROWS[k], :],
                                      rows_h[0:ROWS[k], k, :]).then_inc(xn_stored[l], 16)
                        transpose_out(ph, k)
                if l == 0:
                    act.dma_start(gain[:, :], A["norm_mix"][1:2, :].broadcast_to((P, D))).then_inc(gain_in, 16)
                split_static(FIRST[l])
                for g, (first, end) in enumerate(LOGIT_TILES):
                    act.wait_ge(logT_ps, l * 2 + g + 1)
                    at = slice(first * P, min(end * P, T))
                    act.activation(r["logT"][0:NR, at], ps[0:NR, LOGT_BANK + g, 0:at.stop - at.start],
                                   ACT.Copy).then_inc(logT_sb, 1)
                act.wait_ge(route_exp_in, l * 2 + 1)
                act.activation(r["e1"], r["d1"], ACT.Exp).then_inc(route_exp, 1)
                act.wait_ge(route_exp_in, l * 2 + 2)
                act.activation(r["eg"], r["dg"], ACT.Exp).then_inc(route_exp, 1)
                n = FIRST[l] + 1
                act.wait_ge(piece_in[n % SLOTS], piece_count(n))
                for q in range(QUARTERS):
                    act.activation(up_hi[:, q, :], ring[:, n % SLOTS, q * QUART:(q + 1) * QUART],
                                   ACT.Copy).then_inc(split_hi, 1)

            def xT_out(l, b, u):
                act.wait_ge(xT_ps[l], b + 1)
                act.activation(xT_hi[:, u, :], ps[:, XT_BANK, 0:KT * BLK], ACT.Copy).then_inc(xT_hi_sb[l], 1)

            def hidT_out(l, b):
                act.wait_ge(hidT_ps[l], b + 1)
                act.activation(hid_hi[:, :], ps[:, HT_BANK, 0:FT * BLK], ACT.Copy).then_inc(hidT_hi_sb[l], 1)

            def y_out(l, j, v, half, stage, done):
                act.wait_ge(quarters_used, done)
                if stage >= 2:
                    act.wait_ge(scattered[l][v], half * 16)
                act.activation(yb[v][:, 0:512], ps[0:BLK, Y_BANK, :], ACT.Copy,
                               scale=slot_gate[:, bass.ds(j, 1)]).then_inc(y_lo[l], 1)

            def experts(l):
                xT_out(l, 0, 0)

                def body(b, par, half, stage):
                    n = first_of_block(l, b) if stage else FIRST[l]
                    quarter = n * QUARTERS
                    if stage:
                        split_piece(*landed(l, b, GATE), quarter, 2 * QUARTERS if stage == 1 else QUARTERS)
                    if stage >= 2:
                        y_out(l, b - 2, par, half - 1, stage - 2, quarter)
                    if stage:
                        split_piece(*landed(l, b, UP), quarter + QUARTERS)
                        hidT_out(l, b - 1)
                    act.wait_ge(quarters_used, quarter + QUARTERS)
                    if stage:
                        act.wait_ge(hidden_sb[l], b)
                    act.activation(silu, ps[0:BLK, GATE_BANK, :], ACT.Silu).then_inc(silu_sb[l], 1)
                    if stage < NEXP - 1:
                        xT_out(l, b + 1, 1 - par)
                    if stage:
                        split_piece(*landed(l, b, DOWN), quarter + 2 * QUARTERS)

                blocks(act, body)
                n = FIRST[l] + 3 * NEXP - 1
                split_static(n)
                y_out(l, NEXP - 2, 0, NEXP // 2 - 1, NEXP - 2, n * QUARTERS)
                hidT_out(l, NEXP - 1)
                y_out(l, NEXP - 1, 1, NEXP // 2 - 1, NEXP - 1, (n + 1) * QUARTERS)
                n_ovf = act.value_load(ovf_count[0:1, 0:1], min_val=0, max_val=OVF)
                with act.If(n_ovf > 0):
                    with act.Fori(0, n_ovf) as j:
                        act.wait_ge(o_xT_ps[l], j + 1)
                        act.activation(xT_hi[:, 0, :], ps[:, XT_BANK, 0:KT * BLK], ACT.Copy).then_inc(o_xT_hi[l], 1)
                        act.wait_ge(o_piece_in[l], j * 48 + 48)
                        for m in range(3):
                            for q in range(QUARTERS):
                                if m:
                                    act.wait_ge(o_used[l], j * 12 + (m * QUARTERS + q - QUARTERS + 1))
                                act.activation(w_hi[:, q, :], ring[:, m, q * QUART:(q + 1) * QUART],
                                               ACT.Copy).then_inc(o_split_hi[l], 1)
                            if m == UP:
                                act.wait_ge(o_used[l], j * 12 + QUARTERS)
                                act.activation(silu, ps[0:BLK, GATE_BANK, :], ACT.Silu).then_inc(o_silu[l], 1)
                        act.wait_ge(o_hidT_ps[l], j + 1)
                        act.activation(hid_hi[:, :], ps[:, HT_BANK, 0:FT * BLK], ACT.Copy).then_inc(o_hidT_hi[l], 1)
                        act.wait_ge(o_used[l], j * 12 + 12)
                        act.activation(yb[0][:, 0:512], ps[0:BLK, Y_BANK, :], ACT.Copy,
                                       scale=slot_gate[:, bass.ds(j + NEXP, 1)]).then_inc(o_y_lo[l], 1)

            route_rows(0)
            experts(0)

            split_static(att_first)
            for k in range(2):
                src = A["attn_q_gain" if k == 0 else "attn_k_gain"]
                act.dma_start(qk_gain[:, k, :], src[0:1, :].broadcast_to((P, HD))).then_inc(qk_gain_in, 16)
            for t in range(NT + 1):
                if t < NT:
                    act.wait_ge(x_done[0], t + 1)
                    root_mean_square(2, t, rows_h[0:ROWS[t], t, :])
                if t:
                    transpose_out(2, t - 1)
            act.dma_start(k_cache_nat, A["cache_k"][0, 0].rearrange("t h d -> t (h d)")).then_inc(k_cache_in, 16)
            units = (QKV_PIECES - 2) * NT

            def qkT_out(m):
                j, i = divmod(m, NT)
                n = ROWS[i]
                act.wait_ge(qkT_ps, m + 1)
                dst = (qT if j < 2 else kT)[:, 4 * (j % 2):4 * (j % 2) + 4, i * P:i * P + n]
                act.activation(dst, ps[:, QKT_BANK + m % 2, :].rearrange("p (c t) -> p c t", c=4)[:, :, 0:n],
                               ACT.Copy).then_inc(qkT_sb, 1)

            def squares(m):
                n = ROWS[m % NT]
                act.wait_ge(raw_ps, m + 1)
                if m >= 2:
                    act.wait_ge(q_ssq, m - 1)
                act.activation(sq[m % 2][0:n, :], ps[0:n, m % RAW_BANKS, :], ACT.Square).then_inc(q_sq, 1)

            def head_roots(m):
                n = ROWS[m % NT]
                act.wait_ge(q_ssq, m + 1)
                c = 24 * (m % 2)
                act.activation(qstat[0:n, c + 8:c + 16], qstat[0:n, c:c + 8], ACT.Sqrt,
                               bias=const("eps", n), scale=1.0 / HD).then_inc(q_std, 1)

            def v_out_of_ps(m):
                j, i = divmod(m, NT)
                n = ROWS[i]
                act.wait_ge(raw_ps, units + m + 1)
                if m == 0:
                    act.wait_ge(qkT_ps, units)
                    for u in range(NT):
                        act.wait_ge(k_out[u], 32)
                act.activation(v_nat[0:n, i, j * 512:(j + 1) * 512], ps[0:n, (units + m) % RAW_BANKS, :],
                               ACT.Copy).then_inc(v_sb, 1)

            for j in range(QKV_PIECES):
                for q in range(QUARTERS - 1):
                    split_static(att_first + j + 1, [q])
                    if 1 <= j <= QKV_PIECES - 2:
                        for i in QK_TILES[q]:
                            qkT_out((j - 1) * NT + i)
                if j == QKV_PIECES - 1:
                    act.wait_ge(split_lo, QUARTERS * (att_first + QKV_PIECES - 1))
                    for c in range(2):
                        act.wait_ge(kcT_ps, c + 1)
                        act.activation(kcT[:, 4 * c:4 * c + 4, :],
                                       ps[:, QKT_BANK + c, :].rearrange("p (c t) -> p c t", c=4),
                                       ACT.Copy).then_inc(kcT_sb, 1)
                if j < QKV_PIECES - 2:
                    squares(j * NT)
                    for i in range(NT):
                        if i + 1 < NT:
                            squares(j * NT + i + 1)
                        head_roots(j * NT + i)
                else:
                    for i in range(NT):
                        v_out_of_ps((j - QKV_PIECES + 2) * NT + i)
                split_static(att_first + j + 1, [QUARTERS - 1])
            act.dma_start(gain[:, :], A["norm_ffn"][1:2, :].broadcast_to((P, D))).then_inc(gain_in, 16)

            def pT_out(a):
                i = a % NT
                nk = (i + 1) * P if i < NT - 1 else KEEP + SS
                kt = -(-nk // P)
                n = ROWS[i]
                act.wait_ge(pT_ps, a + 1)
                if a >= 2:
                    act.wait_ge(o_ps, a - 1)
                if i < NT - 1:
                    act.activation(pT_sb[a % 2][:, 0:kt * P], ps[:, PT_BANK + a % 2, 0:kt * P], ACT.Copy).then_inc(pT_ready, 1)
                else:
                    act.activation(pT_sb[a % 2][:, 0:n], ps[:, PT_BANK + a % 2, 0:n], ACT.Copy)
                    act.activation(pT_sb[a % 2][0:SS, P:P + n], ps[0:SS, PT_BANK + a % 2, P:P + n],
                                   ACT.Copy).then_inc(pT_ready, 1)

            UNITS = NH * NT
            for t in range(UNITS + 5):
                if 0 <= t - 2 < UNITS:
                    pT_out(t - 2)
                if t < UNITS:
                    i = t % NT
                    n = ROWS[i]
                    nk = (i + 1) * P if i < NT - 1 else KEEP + SS
                    c = 4 * (t % 4)
                    act.wait_ge(s_biased, t + 1)
                    if t >= 3:
                        act.wait_ge(pT_ps, t - 2)
                    act.activation(p_sb[t % 3][0:n, 0:nk], s_sb[t % 2][0:n, 0:nk], ACT.Exp, scale=-1.0,
                                   bias=small[0:n, c:c + 1], accum_out=small[0:n, c + 2:c + 3]).then_inc(p_ready, 1)
                if t >= 4 and (t - 4) % (2 * NT) == 2 * NT - 1:
                    pr = (t - 4) // (2 * NT)
                    act.wait_ge(oT_ps, pr + 1)
                    act.activation(hT_hi[:, pr, 0:S], ps[:, OT_BANK, :], ACT.Copy)
                    act.activation(hT_hi[:, pr, S:T], ps[:, OT_BANK + 1, 0:SS], ACT.Copy).then_inc(oT_hi_sb, 1)
            split_static(att_first + QKV_PIECES + 1)
            route_rows(1)
            experts(1)
            for i in range(NT):
                act.wait_ge(x_done[1], i + 1)
                dst = O[0][0, i * P:(i + 1) * P, :] if i < NT - 1 else O[1][0]
                act.dma_start(dst, x[0:ROWS[i], i, :]).then_inc(rows_out, 16)

        @block.vector
        def _(dve):
            own = [0]

            def link(ins):
                own[0] += 1
                ins.then_inc(dve_own, 1)
                dve.wait_ge(dve_own, own[0])

            V = nc.vector

            def normalise(ph, i, out, g):
                n = ROWS[i]
                dve.wait_ge(std_ready, ph * NT + i + 1)
                link(V.reciprocal(rstd[0:n, ph, i:i + 1], std[0:n, ph, i:i + 1]))
                V.scalar_tensor_tensor(out=out, in0=x[0:n, i, :], scalar=rstd[0:n, ph, i:i + 1], in1=g[0:n, :],
                                       op0=ALU.mult, op1=ALU.mult).then_inc(h_ready, 1)

            def split_piece(s, quarter):
                for q in range(QUARTERS):
                    dve.wait_ge(split_hi, quarter + (q + 1))
                    V.tensor_tensor(w_lo[:, q, :], ring[:, s, q * QUART:(q + 1) * QUART], f32(w_hi[:, q, :]),
                                    ALU.subtract).then_inc(split_lo, 1)

            def split_static(n, quarters=range(QUARTERS)):
                for q in quarters:
                    dve.wait_ge(split_hi, QUARTERS * n + q + 1)
                    V.tensor_tensor(w_lo[:, q, :], ring[:, n % SLOTS, q * QUART:(q + 1) * QUART],
                                    f32(w_hi[:, q, :]), ALU.subtract).then_inc(split_lo, 1)

            def transpose_out(ph, i):
                n = ROWS[i]
                b = 2 * (i % 2)
                cols_i = slice(i * P, i * P + n)
                dve.wait_ge(hT_hi_sb, (ph - 1) * NT + i + 1)
                V.tensor_tensor(hT_lo[:, 0:KT, cols_i],
                                ps[:, b:b + 2, :].rearrange("p b (c t) -> p (b c) t", c=4)[:, :, 0:n],
                                f32(hT_hi[:, 0:KT, cols_i]), ALU.subtract).then_inc(hT_sb, 1)

            dve.wait_ge(pool_gain_in, 16)
            for i in range(NT):
                normalise(0, i, pool_h[0:ROWS[i], i, :], pool_gain)
            dve.wait_ge(pool_maps_in, 32)
            for i in range(NT):
                n = ROWS[i]
                dve.wait_ge(pool_y, i + 1)
                b = 4 + 2 * (i % 2)
                link(V.tensor_tensor(y_tmp[0:n, :], ps[0:n, b:b + 2, :].rearrange("p b c -> p (b c)"),
                                     pool_scale[0:n, :], ALU.mult))
                ins = V.tensor_tensor(x[0:n, i, :], x[0:n, i, :], y_tmp[0:n, :], ALU.add)
                ins.then_inc(x_mixed[0], 1)
                dve.wait_ge(x_mixed[0], i + 1)

            def bc(a, shape, axis):
                return a.unsqueeze(axis).broadcast_to(shape)

            def route(l):
                ph = 1 + 2 * l
                lg = r["logit"]
                if l == 0:
                    dve.wait_ge(rows_out, 32)
                else:
                    dve.wait_ge(v_out, 16 * 2 * NT)
                link(V.memset(lg, 0.0))
                dve.wait_ge(rw_hi_sb, l + 1)
                V.tensor_tensor(rw_lo, rw[:, :, :], f32(rw_hi), ALU.subtract).then_inc(rw_sb, 1)
                dve.wait_ge(gain_in, 16 * (2 * l + 1))
                for i in range(NT + 1):
                    if i < NT:
                        normalise(ph, i, rows_h[0:ROWS[i], i, :], gain)
                    if i:
                        transpose_out(ph, i - 1)
                split_static(FIRST[l])
                dve.wait_ge(logit_ps, l + 1)
                full = NT - 1
                V.tensor_tensor(lg[:, 0:full, :], ps[:, LOGIT_BANK, 0:full * NR].rearrange("p (i c) -> p i c", c=NR),
                                bc(r["bias"], (P, full, NR), 1), ALU.add)
                link(V.tensor_tensor(lg[0:SS, full, :], ps[0:SS, LOGIT_BANK, full * NR:NT * NR], r["bias"][0:SS, :],
                                     ALU.add))
                l1 = lg[:, :, 0:NG]
                sg = (P, NT, NG)
                se = (P, NT, EPG)
                link(V.reduce_max(r["m1"], l1, AX.X))
                ins = V.tensor_tensor(r["d1"], l1, bc(r["m1"], sg, 2), ALU.subtract)
                ins.then_inc(route_exp_in, 1)
                link(V.tensor_tensor(r["eq1"], l1, bc(r["m1"], sg, 2), ALU.is_equal))
                link(V.tensor_tensor(r["eq1"], r["eq1"], bc(const("rank_group"), sg, 1), ALU.mult))
                link(V.reduce_max(r["kk"], r["eq1"], AX.X))
                link(V.tensor_tensor(r["oh1"], r["eq1"], bc(r["kk"], sg, 2), ALU.is_equal))
                link(V.tensor_tensor(r["oh1"], r["oh1"], bc(const("valid"), sg, 2), ALU.mult))
                t4 = r["tmp"][:, 0:NT * NEXP].rearrange("p (i g e) -> p i g e", i=NT, g=NG)
                l2g = lg[:, :, NG:NR].rearrange("p i (g e) -> p i g e", g=NG)
                oh4 = r["oh1"].unsqueeze(3).broadcast_to((P, NT, NG, EPG))
                link(V.tensor_tensor(t4, l2g, oh4, ALU.mult))
                link(V.reduce_sum(r["l2"], t4.rearrange("p i g e -> p i e g"), AX.X))
                src = r["l2"]
                for k in range(2):
                    m = r["ma" if k == 0 else "mb"]
                    link(V.reduce_max(m, src, AX.X))
                    link(V.tensor_tensor(r["eq2"], src, bc(m, se, 2), ALU.is_equal))
                    link(V.tensor_tensor(r["eq2"], r["eq2"], bc(const("rank_expert"), se, 1), ALU.mult))
                    link(V.reduce_max(r["kk"], r["eq2"], AX.X))
                    link(V.tensor_tensor(r[f"a{k}"], r["eq2"], bc(r["kk"], se, 2), ALU.is_equal))
                    if k == 0:
                        link(V.scalar_tensor_tensor(out=r["l2b"], in0=r["a0"], scalar=NEG, in1=r["l2"],
                                                    op0=ALU.mult, op1=ALU.add))
                        src = r["l2b"]
                V.tensor_tensor(r["dg"], r["mb"], r["ma"], ALU.subtract).then_inc(route_exp_in, 1)
                for k in range(2):
                    a4 = r[f"a{k}"].unsqueeze(2).broadcast_to((P, NT, NG, EPG))
                    ins = V.tensor_tensor(r["A"][:, k, :, :].rearrange("p i (g e) -> p i g e", g=NG), a4, oh4, ALU.mult)
                link(ins)
                V.tensor_tensor(r["M"], r["A"][:, 0, :, :], r["A"][:, 1, :, :], ALU.add).then_inc(chosen, 1)
                chosen_rows = r["A"].rearrange("p k i e -> p (k i) e")
                sp = (P, PT, NEXP)
                tmp = r["tmp"][:, 0:2 * PT * NEXP].rearrange("p (v m e) -> p v m e", v=2, e=NEXP)
                link(V.tensor_tensor(tmp[:, 0, :, :], chosen_rows, bc(const("iota_expert"), sp, 1), ALU.mult))
                link(V.reduce_sum(r["exp"], tmp[:, 0, :, :], AX.X))
                dve.wait_ge(route_exp, l * 2 + 2)
                link(V.reduce_sum(r["s1"], r["e1"], AX.X))
                V.tensor_scalar(r["den"], r["eg"], 1.0, None, ALU.add)
                link(V.reciprocal(r["pg"], r["s1"]))
                V.reciprocal(r["rden"], r["den"])
                link(V.tensor_tensor(r["pg"], r["pg"], const("valid"), ALU.mult))
                link(V.tensor_tensor(r["gate"][:, 0:NT], r["pg"], r["rden"], ALU.mult))
                link(V.tensor_tensor(r["gate"][:, NT:PT], r["gate"][:, 0:NT], r["eg"], ALU.mult))
                dve.wait_ge(ranks_ps, l + 1)
                ranks = ps[:, 0, 0:NT * NEXP].rearrange("p (i e) -> p i e", e=NEXP)
                cnt = ps[:, 0, NT * NEXP:(NT + 1) * NEXP]
                sc = (P, NEXP, STEPS)
                t = r["tmp2"][:, 0:NEXP * STEPS].rearrange("p (e s) -> p e s", e=NEXP)
                link(V.tensor_tensor(t, bc(cnt, sc, 2), bc(const("steps"), sc, 1), ALU.is_gt))
                V.tensor_tensor(tmp[:, 0, :, :].rearrange("p (k i) e -> p k i e", k=2), r["A"],
                                bc(ranks, (P, 2, NT, NEXP), 1), ALU.mult)
                link(V.reduce_sum(r["extra"], t, AX.X))
                link(V.tensor_tensor_scan(out=r["incl"], data0=const("ones")[:, 0:NEXP], data1=r["extra"],
                                          initial=0.0, op0=ALU.mult, op1=ALU.add))
                link(V.tensor_tensor(r["offs"], r["incl"], r["extra"], ALU.subtract))
                link(V.tensor_tensor(tmp[:, 1, :, :], chosen_rows, bc(r["offs"], sp, 1), ALU.mult))
                link(V.reduce_sum(r["pos_off"], tmp, AX.X))
                pos, off = r["pos_off"][:, 0, :], r["pos_off"][:, 1, :]
                ts = r["tmp2"][:, 0:PT * STEPS].rearrange("p (m s) -> p m s", m=PT)
                ss = (P, PT, STEPS)
                link(V.tensor_tensor(ts, bc(pos, ss, 2), bc(const("steps"), ss, 1), ALU.is_ge))
                link(V.reduce_sum(r["step"], ts, AX.X))
                link(V.scalar_tensor_tensor(out=r["blk"], in0=off, scalar=float(NEXP - 1), in1=r["step"],
                                            op0=ALU.add, op1=ALU.add))
                V.scalar_tensor_tensor(out=r["slot"], in0=r["step"], scalar=-float(BLK), in1=pos,
                                       op0=ALU.mult, op1=ALU.add)
                link(V.tensor_tensor(r["away"], r["exp"], r["blk"], ALU.subtract))
                link(V.scalar_tensor_tensor(out=r["away"], in0=r["step"], scalar=0.0, in1=r["away"],
                                            op0=ALU.is_equal, op1=ALU.mult))
                link(V.tensor_tensor(r["blk"], r["blk"], r["away"], ALU.add))
                so, sn, s4 = (P, PT, BLK), (P, PT, NB), (P, 2, NT, NB)
                tb = r["tmp2"][:, 0:PT * NB].rearrange("p (m b) -> p m b", m=PT)
                link(V.tensor_tensor(tb, bc(r["blk"], sn, 2), bc(const("iota_block"), sn, 1), ALU.is_equal))
                V.tensor_tensor(r["S"], bc(r["slot"], so, 2), bc(const("iota_slot"), so, 1), ALU.is_equal)
                tb4 = tb.rearrange("p (k i) b -> p k i b", k=2)
                for c, val in enumerate((const("token").unsqueeze(1).broadcast_to((P, 2, NT)),
                                         const("row").rearrange("p (k i) -> p k i", k=2),
                                         r["gate"].rearrange("p (k i) -> p k i", k=2))):
                    ins = V.tensor_tensor(r["V"][:, :, :, c, :], tb4, bc(val, s4, 3), ALU.mult)
                link(ins)
                so = (P, OVF, NEXP)
                ta = r["tmp"][:, 0:OVF * NEXP].rearrange("p (b e) -> p b e", e=NEXP)
                tb = r["tmp2"][:, 0:OVF * NEXP].rearrange("p (b e) -> p b e", e=NEXP)
                iota_o = bc(const("iota_block")[:, 0:OVF], so, 2)
                ins = V.tensor_tensor(ta, iota_o, bc(r["offs"], so, 1), ALU.is_ge)
                ins.then_inc(slots_ready, 1)
                dve.wait_ge(slots_ready, l + 1)
                link(V.tensor_tensor(tb, iota_o, bc(r["incl"], so, 1), ALU.is_lt))
                link(V.tensor_tensor(ta, ta, tb, ALU.mult))
                link(V.tensor_tensor(ta, ta, bc(const("iota_expert"), so, 1), ALU.mult))
                link(V.reduce_sum(r["extra"][:, 0:OVF], ta, AX.X))
                link(V.tensor_copy(ovf_expert[0:1, :], r["extra"][0:1, 0:OVF]))
                V.tensor_copy(ovf_count[0:1, :], r["incl"][0:1, NEXP - 1:NEXP])
                dve.wait_ge(table_ps, l + 1)
                V.tensor_scalar(idx_gather[:, :], ps[0:BLK, 1, 0:NB], PAD, None, ALU.add)
                V.tensor_scalar(idx_scatter[:, :], ps[0:BLK, 1, NB:2 * NB], PAD, None, ALU.add)
                V.tensor_copy(slot_gate[:, :], ps[0:BLK, 1, 2 * NB:3 * NB]).then_inc(table_sb, 1)
                n = FIRST[l] + 1
                for q in range(QUARTERS):
                    dve.wait_ge(split_hi, QUARTERS * n + q + 1)
                    V.tensor_tensor(up_lo[:, q, :], ring[:, n % SLOTS, q * QUART:(q + 1) * QUART],
                                    f32(up_hi[:, q, :]), ALU.subtract).then_inc(split_lo, 1)

            def xT_out(l, b, u):
                dve.wait_ge(xT_hi_sb[l], b + 1)
                V.tensor_tensor(xT_lo[:, u, :], ps[:, XT_BANK, 0:KT * BLK], f32(xT_hi[:, u, :]),
                                ALU.subtract).then_inc(xT_sb[l], 1)

            def hidT_out(l, b):
                dve.wait_ge(hidT_hi_sb[l], b + 1)
                V.tensor_tensor(hid_lo[:, :], ps[:, HT_BANK, 0:FT * BLK], f32(hid_hi[:, :]),
                                ALU.subtract).then_inc(hidT_sb[l], 1)

            def y_out(l, j, v, half, stage, done):
                dve.wait_ge(quarters_used, done)
                if stage >= 2:
                    dve.wait_ge(scattered[l][v], half * 16)
                V.tensor_scalar(yb[v][:, 512:D], ps[0:BLK, Y_BANK + 1, :], slot_gate[:, bass.ds(j, 1)], None,
                                ALU.mult).then_inc(y_hi[l], 1)

            def experts(l):
                xT_out(l, 0, 0)

                def body(b, par, half, stage):
                    n = first_of_block(l, b) if stage else FIRST[l]
                    quarter = n * QUARTERS
                    if stage:
                        split_piece(landed(l, b, GATE)[0], quarter)
                    if stage >= 2:
                        y_out(l, b - 2, par, half - 1, stage - 2, quarter)
                    if stage:
                        split_piece(landed(l, b, UP)[0], quarter + QUARTERS)
                        hidT_out(l, b - 1)
                    if stage < NEXP - 1:
                        xT_out(l, b + 1, 1 - par)
                    if stage:
                        split_piece(landed(l, b, DOWN)[0], quarter + 2 * QUARTERS)
                    dve.wait_ge(quarters_used, quarter + 2 * QUARTERS)
                    dve.wait_ge(silu_sb[l], b + 1)
                    if stage:
                        dve.wait_ge(hidT_ps[l], b)
                    V.tensor_tensor(hidden, silu, ps[0:BLK, UP_BANK, :], ALU.mult).then_inc(hidden_sb[l], 1)

                blocks(dve, body)
                n = FIRST[l] + 3 * NEXP - 1
                split_static(n)
                y_out(l, NEXP - 2, 0, NEXP // 2 - 1, NEXP - 2, n * QUARTERS)
                hidT_out(l, NEXP - 1)
                y_out(l, NEXP - 1, 1, NEXP // 2 - 1, NEXP - 1, (n + 1) * QUARTERS)
                n_ovf = dve.value_load(ovf_count[0:1, 0:1], min_val=0, max_val=OVF)
                with dve.If(n_ovf > 0):
                    with dve.Fori(0, n_ovf) as j:
                        dve.wait_ge(o_xT_hi[l], j + 1)
                        V.tensor_tensor(xT_lo[:, 0, :], ps[:, XT_BANK, 0:KT * BLK], f32(xT_hi[:, 0, :]),
                                        ALU.subtract).then_inc(o_xT_sb[l], 1)
                        for m in range(3):
                            for q in range(QUARTERS):
                                dve.wait_ge(o_split_hi[l], j * 12 + (m * QUARTERS + q + 1))
                                V.tensor_tensor(w_lo[:, q, :], ring[:, m, q * QUART:(q + 1) * QUART],
                                                f32(w_hi[:, q, :]), ALU.subtract).then_inc(o_split_lo[l], 1)
                        dve.wait_ge(o_used[l], j * 12 + 2 * QUARTERS)
                        dve.wait_ge(o_silu[l], j + 1)
                        V.tensor_tensor(hidden, silu, ps[0:BLK, UP_BANK, :], ALU.mult).then_inc(o_hidden[l], 1)
                        dve.wait_ge(o_hidT_hi[l], j + 1)
                        V.tensor_tensor(hid_lo[:, :], ps[:, HT_BANK, 0:FT * BLK], f32(hid_hi[:, :]),
                                        ALU.subtract).then_inc(o_hidT_sb[l], 1)
                        dve.wait_ge(o_used[l], j * 12 + 12)
                        V.tensor_scalar(yb[0][:, 512:D], ps[0:BLK, Y_BANK + 1, :],
                                        slot_gate[:, bass.ds(j + NEXP, 1)], None, ALU.mult).then_inc(o_y_hi[l], 1)

            def combine(l, i):
                n = ROWS[i]
                rows = yc[i % len(yc)]
                if pool_sums(l, i):
                    dve.wait_ge(yc_sum, sums_before(l, i) + 1)
                else:
                    dve.wait_ge(yc_in[i], 16 * (l + 1))
                    link(V.tensor_tensor(rows[0:n, 0:D], rows[0:n, 0:D], rows[0:n, D:2 * D], ALU.add))
                V.tensor_tensor(x[0:n, i, :], x[0:n, i, :], rows[0:n, 0:D], ALU.add).then_inc(x_done[l], 1)
                dve.wait_ge(x_done[l], i + 1)

            route(0)
            experts(0)
            split_static(att_first)

            dve.wait_ge(gain_in, 32)
            for t in range(NT + 2):
                if t < NT:
                    combine(0, t)
                if 1 <= t <= NT:
                    normalise(2, t - 1, rows_h[0:ROWS[t - 1], t - 1, :], gain)
                if t >= 2:
                    transpose_out(2, t - 2)
            units = (QKV_PIECES - 2) * NT

            def head_sums(m):
                n = ROWS[m % NT]
                dve.wait_ge(q_sq, m + 1)
                c = 24 * (m % 2)
                V.reduce_sum(qstat[0:n, c:c + 8], sq[m % 2][0:n, :].rearrange("p (h d) -> p h d", d=HD),
                             AX.X).then_inc(q_ssq, 1)

            def scale_heads(m):
                n = ROWS[m % NT]
                c = 24 * (m % 2)
                dve.wait_ge(q_std, m + 1)
                link(V.reciprocal(qstat[0:n, c + 16:c + 24], qstat[0:n, c + 8:c + 16]))
                if m >= NT:
                    dve.wait_ge(qkT_ps, m - NT + 1)
                    if m >= 3 * NT:
                        dve.wait_ge(k_out[m % NT], 16 * (m // NT - 2))
                V.tensor_tensor(qn[m % NT][0:n, :].rearrange("p (h d) -> p h d", d=HD),
                                ps[0:n, m % RAW_BANKS, :].rearrange("p (h d) -> p h d", d=HD),
                                bc(qstat[0:n, c + 16:c + 24], (n, 512 // HD, HD), 2),
                                ALU.mult).then_inc(q_scaled, 1)

            for j in range(QKV_PIECES):
                split_static(att_first + j + 1, range(QUARTERS - 1))
                if j < QKV_PIECES - 2:
                    head_sums(j * NT)
                    for i in range(NT):
                        if i + 1 < NT:
                            head_sums(j * NT + i + 1)
                        scale_heads(j * NT + i)
                split_static(att_first + j + 1, [QUARTERS - 1])

            def scores(h, i):
                a = h * NT + i
                n = ROWS[i]
                nk = (i + 1) * P if i < NT - 1 else KEEP + SS
                m0 = 512 - nk
                if i == 0:
                    dve.wait_ge(bias_ready, 2 * h + 2)
                dve.wait_ge(s_ps, a + 1)
                if a >= 2:
                    dve.wait_ge(p_ready, a - 1)
                c = 4 * (a % 4)
                V.tensor_tensor_reduce(out=s_sb[a % 2][0:n, 0:nk], in0=ps[0:n, S_BANK + a % 2, 0:nk],
                                       in1=bias_h[h % 2][0:n, m0:512], scale=-float(HD) ** -0.5, scalar=3e38,
                                       op0=ALU.add, op1=ALU.min, accum_out=small[0:n, c:c + 1]).then_inc(s_biased, 1)

            def o_out(a):
                h, i = divmod(a, NT)
                n = ROWS[i]
                c = 4 * (a % 4)
                dve.wait_ge(p_ready, a + 1)
                link(V.reciprocal(small[0:n, c + 3:c + 4], small[0:n, c + 2:c + 3]))
                dve.wait_ge(o_ps, a + 1)
                if i == 0 and h % 2 == 0 and h >= 4:
                    dve.wait_ge(oT_ps, h // 2 - 1)
                V.tensor_scalar(o_nat[(h // 2) % 2][0:n, i, (h % 2) * HD:(h % 2 + 1) * HD],
                                ps[0:n, O_BANK + a % 2, 0:HD], small[0:n, c + 3:c + 4], None,
                                ALU.mult).then_inc(o_sb, 1)

            UNITS = NH * NT
            for a in range(UNITS + 5):
                if a < UNITS:
                    scores(*divmod(a, NT))
                if 0 <= a - 3 < UNITS:
                    o_out(a - 3)
                if a >= 4 and (a - 4) % (2 * NT) == 2 * NT - 1:
                    pr = (a - 4) // (2 * NT)
                    dve.wait_ge(oT_hi_sb, pr + 1)
                    V.tensor_tensor(hT_lo[:, pr, 0:S], ps[:, OT_BANK, :], f32(hT_hi[:, pr, 0:S]), ALU.subtract)
                    V.tensor_tensor(hT_lo[:, pr, S:T], ps[:, OT_BANK + 1, 0:SS], f32(hT_hi[:, pr, S:T]),
                                    ALU.subtract).then_inc(oT_sb, 1)

            split_static(att_first + QKV_PIECES + 1, range(QUARTERS - 1))
            for hf in range(2):
                if hf == 1:
                    split_static(att_first + QKV_PIECES + 1, [QUARTERS - 1])
                for i in range(NT):
                    n = ROWS[i]
                    m = hf * NT + i
                    dve.wait_ge(att_y, m + 1)
                    ins = V.tensor_tensor(x[0:n, i, hf * 512:(hf + 1) * 512], x[0:n, i, hf * 512:(hf + 1) * 512],
                                          ps[0:n, m % RAW_BANKS, :], ALU.add)
                    ins.then_inc(x_mixed[1] if hf == 1 else x_half, 1)
            route(1)
            experts(1)
            for i in range(NT):
                combine(1, i)

        @block.tensor
        def _(pe):
            mm = nc.tensor.matmul

            def split_product(out, x_hi, x_lo, w_h, w_l, start, stop):
                mm(out, x_hi, w_h, start=start, stop=False)
                mm(out, x_lo, w_h, start=False, stop=False)
                return mm(out, x_hi, w_l, start=False, stop=stop)

            def transposes(ph, i):
                n = ROWS[i]
                pe.wait_ge(h_ready, ph * NT + i + 1)
                if i >= 2:
                    pe.wait_ge(hT_sb, (ph - 1) * NT + i - 1)
                src = rows_h[0:n, i, :].rearrange("p (c k) -> p k c", k=KT)
                for k in range(KT):
                    last = nc.tensor.transpose(ps[:, 2 * (i % 2) + k // 4, 128 * (k % 4):128 * (k % 4) + n],
                                               src[:, k, :], ident[0:n, 0:n])
                last.then_inc(hT_ps, 1)

            pe.wait_ge(consts_in, 16)
            pe.wait_ge(bands_in, 16)

            def deltas(i):
                n = ROWS[i]
                pe.wait_ge(h_ready, i + 1)
                if i >= 2:
                    pe.wait_ge(delta_sb, i - 1)
                if i == NT - 1:
                    pe.wait_ge(hist_in, 16)
                for c in range(KT):
                    g = c * P // PW
                    out = ps[:, 2 * (i % 2) + c // 4, 128 * (c % 4):128 * (c % 4) + n]
                    band = gain[:, (2 * g + (i == 0)) * P:(2 * g + (i == 0) + 1) * P]
                    last = mm(out, pool_h[0:n, i, c * P:(c + 1) * P], band[0:n, 0:n], start=True, stop=True,
                              skip_group_check=True)
                    if i > 0:
                        prev = pool_h[:, i - 1, :] if i < NT - 1 else hist
                        last = mm(out[:, 0:HALO], prev[:, c * P:(c + 1) * P], const(f"band_halo{g}"),
                                  start=False, stop=True, skip_group_check=True)
                last.then_inc(delta_ps, 1)

            deltas(0)
            pe.wait_ge(pool_maps_in, 32)
            for i in range(NT):
                if i + 1 < NT:
                    deltas(i + 1)
                n = ROWS[i]
                pe.wait_ge(delta_sb, i + 1)
                if i >= 2:
                    pe.wait_ge(x_mixed[0], i - 1)
                for g in range(len(POOL_WINDOWS)):
                    out = ps[0:n, 4 + 2 * (i % 2) + g // 2, PW * (g % 2):PW * (g % 2 + 1)]
                    for k in range(2):
                        last = mm(out, dT[i % 2][:, 2 * g + k, 0:n], band_w[:, 2 * g + k, :], start=(k == 0), stop=(k == 1))
                last.then_inc(pool_y, 1)

            def route(l):
                ph = 1 + 2 * l
                pe.wait_ge(x_mixed[l], NT)
                transposes(ph, 0)
                for i in range(1, NT):
                    transposes(ph, i)
                pe.wait_ge(rw_sb, l + 1)
                for g, (first, end) in enumerate(LOGIT_TILES):
                    pe.wait_ge(hT_sb, (ph - 1) * NT + end)
                    at = slice(first * P, min(end * P, T))
                    for k in range(KT):
                        last = split_product(ps[0:NR, LOGT_BANK + g, 0:at.stop - at.start], rw_hi[:, k, :],
                                             rw_lo[:, k, :], hT_hi[:, k, at], hT_lo[:, k, at], k == 0, k == KT - 1)
                    last.then_inc(logT_ps, 1)
                for i in range(NT):
                    n = ROWS[i]
                    pe.wait_ge(logT_sb, l * 2 + 1 + (i >= LOGIT_TILES[1][0]))
                    last = nc.tensor.transpose(ps[0:n, LOGIT_BANK, i * NR:(i + 1) * NR], r["logT"][0:NR, tok(i)],
                                               ident[0:NR, 0:NR])
                last.then_inc(logit_ps, 1)
                pe.wait_ge(chosen, l + 1)
                M = r["M"]
                mm(ps[:, 0, 0:NT * NEXP], const("before"), M.rearrange("p i e -> p (i e)"), start=True, stop=True,
                   skip_group_check=True)
                for i in range(NT):
                    behind = ps[:, 0, (i + 1) * NEXP:(NT + 1) * NEXP].rearrange("p (k e) -> p k e", e=NEXP)
                    last = mm(behind, const("ones"), M[:, i, :].unsqueeze(1).broadcast_to((P, NT - i, NEXP)),
                              start=False, stop=True, skip_group_check=True)
                last.then_inc(ranks_ps, 1)
                pe.wait_ge(slots_ready, l + 1)
                table_rows = r["V"].rearrange("p k i c b -> p (k i) (c b)")
                for m in range(PT):
                    last = mm(ps[0:BLK, 1, 0:3 * NB], r["S"][:, m, :], table_rows[:, m, :],
                              start=(m == 0), stop=(m == PT - 1))
                last.then_inc(table_ps, 1)

            def block_transposes(u):
                src = xg[u].rearrange("s (c k) -> s k c", k=KT)
                for k in range(KT):
                    last = nc.tensor.transpose(ps[:, XT_BANK, k * BLK:(k + 1) * BLK], src[:, k, :], ident[0:BLK, 0:BLK])
                return last

            def product(bank, quarter, split, used, buf, hi=w_hi, lo=w_lo):
                for q in range(QUARTERS):
                    pe.wait_ge(split, quarter + (q + 1))
                    for kk in range(KT // QUARTERS):
                        k = q * KT // QUARTERS + kk
                        at = slice(k * BLK, (k + 1) * BLK)
                        last = split_product(ps[0:BLK, bank, :], xT_hi[:, buf, at], xT_lo[:, buf, at],
                                             hi[:, q, kk * 512:(kk + 1) * 512], lo[:, q, kk * 512:(kk + 1) * 512],
                                             k == 0, k == KT - 1)
                    last.then_inc(used, 1)

            def down(quarter, split, used):
                for q in range(QUARTERS):
                    pe.wait_ge(split, quarter + (q + 1))
                    at = slice(q * BLK, (q + 1) * BLK)
                    for hf in range(2):
                        half = slice(hf * 512, (hf + 1) * 512)
                        last = split_product(ps[0:BLK, Y_BANK + hf, :], hid_hi[:, at], hid_lo[:, at],
                                             w_hi[:, q, half], w_lo[:, q, half], q == 0, q == FT - 1)
                    last.then_inc(used, 1)

            def hidden_transposes():
                for k in range(FT):
                    last = nc.tensor.transpose(ps[:, HT_BANK, k * BLK:(k + 1) * BLK], hidden[:, k * P:(k + 1) * P],
                                               ident[0:BLK, 0:BLK])
                return last

            def experts(l):
                def transpose_hidden(b, stage):
                    if stage:
                        pe.wait_ge(hidT_sb[l], b)
                    pe.wait_ge(hidden_sb[l], b + 1)
                    pe.sem_inc(wait_carrier, 1)
                    hidden_transposes().then_inc(hidT_ps[l], 1)

                def down_block(b, stage, quarter):
                    pe.wait_ge(hidT_sb[l], b + 1)
                    if stage:
                        pe.wait_ge(y_lo[l], b)
                        pe.wait_ge(y_hi[l], b)
                    down(quarter, split_lo, quarters_used)

                def body(b, par, half, stage):
                    quarter = (first_of_block(l, b) if stage else FIRST[l]) * QUARTERS
                    pe.wait_ge(xT_sb[l], b + 1)
                    if stage:
                        pe.wait_ge(silu_sb[l], b)
                    product(GATE_BANK, quarter, split_lo, quarters_used, par)
                    if stage:
                        transpose_hidden(b - 1, stage - 1)
                    if stage < NEXP - 1:
                        pe.wait_ge(gathered[l][1 - par], (half + par) * 16 + 16)
                        pe.sem_inc(wait_carrier, 1)
                        block_transposes(1 - par).then_inc(xT_ps[l], 1)
                    if stage:
                        product(UP_BANK, quarter + QUARTERS, split_lo, quarters_used, par)
                    else:
                        product(UP_BANK, quarter + QUARTERS, split_lo, quarters_used, par, up_hi, up_lo)
                    if stage:
                        down_block(b - 1, stage - 1, quarter + 2 * QUARTERS)

                pe.wait_ge(table_sb, l + 1)
                pe.wait_ge(gathered[l][0], 16)
                block_transposes(0).then_inc(xT_ps[l], 1)
                blocks(pe, body)
                transpose_hidden(NEXP - 1, NEXP - 1)
                down_block(NEXP - 1, NEXP - 1, (FIRST[l] + 3 * NEXP - 1) * QUARTERS)
                n_ovf = pe.value_load(ovf_count[0:1, 0:1], min_val=0, max_val=OVF)
                with pe.If(n_ovf > 0):
                    pe.wait_ge(y_lo[l], NEXP)
                    pe.wait_ge(y_hi[l], NEXP)
                    with pe.Fori(0, n_ovf) as j:
                        pe.wait_ge(o_gathered[l], j * 16 + 16)
                        pe.sem_inc(wait_carrier, 1)
                        block_transposes(0).then_inc(o_xT_ps[l], 1)
                        pe.wait_ge(o_xT_sb[l], j + 1)
                        product(GATE_BANK, j * 12, o_split_lo[l], o_used[l], 0)
                        product(UP_BANK, j * 12 + QUARTERS, o_split_lo[l], o_used[l], 0)
                        pe.wait_ge(o_hidden[l], j + 1)
                        pe.sem_inc(wait_carrier, 1)
                        hidden_transposes().then_inc(o_hidT_ps[l], 1)
                        pe.wait_ge(o_hidT_sb[l], j + 1)
                        down(j * 12 + 2 * QUARTERS, o_split_lo[l], o_used[l])

            route(0)
            experts(0)

            pe.wait_ge(x_done[0], 1)
            for i in range(NT):
                transposes(2, i)
            units = (QKV_PIECES - 2) * NT

            def qk_transposes(m):
                j, i = divmod(m, NT)
                n = ROWS[i]
                pe.wait_ge(q_gained, m + 1)
                if m >= 2:
                    pe.wait_ge(qkT_sb, m - 1)
                for c in range(4):
                    out = ps[:, QKT_BANK + m % 2, 128 * c:128 * c + n]
                    src = qn[m % NT][0:n, 128 * c:128 * (c + 1)]
                    if j < 2:
                        flip = const("flip") if i < NT - 1 else flip_sample[0:n, :]
                        last = mm(out, src, flip, start=True, stop=True)
                    else:
                        last = nc.tensor.transpose(out, src, ident[0:n, 0:n])
                last.then_inc(qkT_ps, 1)

            pe.wait_ge(hT_sb, (2 - 1) * NT + NT)

            def token_product(piece, m0, free, done, between=None):
                for q in range(QUARTERS):
                    pe.wait_ge(split_lo, QUARTERS * piece + q + 1)
                    for i in range(NT):
                        n = ROWS[i]
                        if q == 0:
                            free(m0 + i)
                        for kk in range(KT // QUARTERS):
                            k = q * KT // QUARTERS + kk
                            at = slice(kk * 512, (kk + 1) * 512)
                            last = split_product(ps[0:n, (m0 + i) % RAW_BANKS, :], hT_hi[:, k, tok(i)],
                                                 hT_lo[:, k, tok(i)], w_hi[:, q, at], w_lo[:, q, at],
                                                 k == 0, k == KT - 1)
                        if q == QUARTERS - 1:
                            last.then_inc(done, 1)
                    if q < QUARTERS - 1:
                        last.then_inc(quarters_used, 1)
                    else:
                        pe.wait_ge(done, m0 + NT)
                        pe.sem_inc(quarters_used, 1)
                    if between is not None and q < QUARTERS - 1:
                        between(q)

            def raw_free(m):
                m -= RAW_BANKS
                if m >= units:
                    pe.wait_ge(v_sb, m + 1 - units)
                elif m >= 0:
                    pe.wait_ge(q_scaled, m + 1)

            for j in range(QKV_PIECES):
                def between(q, j=j):
                    for i in QK_TILES[q]:
                        qk_transposes((j - 1) * NT + i)

                if j == QKV_PIECES - 1:
                    pe.wait_ge(k_cache_in, 16)
                    pe.wait_ge(qkT_sb, units)
                    for c in range(KT):
                        last = nc.tensor.transpose(ps[:, QKT_BANK + c // 4, 128 * (c % 4):128 * (c % 4 + 1)],
                                                   k_cache_nat[:, c * P:(c + 1) * P], ident)
                        if c % 4 == 3:
                            last.then_inc(kcT_ps, 1)
                token_product(att_first + j, j * NT, raw_free, raw_ps, between if 1 <= j <= QKV_PIECES - 2 else None)
            pe.wait_ge(kcT_sb, 2)
            pe.wait_ge(v_cache_in, 16)
            pe.wait_ge(v_sb, 2 * NT)

            def scores(a):
                h, i = divmod(a, NT)
                n = ROWS[i]
                lo = HD * (h % 2)
                if a >= 2:
                    pe.wait_ge(s_biased, a - 1)
                q = qT[lo:lo + HD, h // 2, tok(i)]
                if i < NT - 1:
                    last = mm(ps[0:n, S_BANK + a % 2, 0:(i + 1) * P], q, kT[lo:lo + HD, h // 2, 0:(i + 1) * P],
                              start=True, stop=True)
                else:
                    mm(ps[0:n, S_BANK + a % 2, 0:KEEP], q, kcT[lo:lo + HD, h // 2, :], start=True, stop=True)
                    last = mm(ps[0:n, S_BANK + a % 2, KEEP:KEEP + SS], q, kT[lo:lo + HD, h // 2, tok(i)],
                              start=True, stop=True)
                last.then_inc(s_ps, 1)

            def p_transposes(a):
                i = a % NT
                n = ROWS[i]
                nk = (i + 1) * P if i < NT - 1 else KEEP + SS
                pe.wait_ge(p_ready, a + 1)
                if a >= 2:
                    pe.wait_ge(pT_ready, a - 1)
                for k in range(-(-nk // P)):
                    w = min(P, nk - k * P)
                    last = nc.tensor.transpose(ps[0:w, PT_BANK + a % 2, k * P:k * P + n],
                                               p_sb[a % 3][0:n, k * P:k * P + w], ident[0:n, 0:n])
                last.then_inc(pT_ps, 1)

            def values(a):
                h, i = divmod(a, NT)
                n = ROWS[i]
                pe.wait_ge(pT_ready, a + 1)
                if a >= 2:
                    pe.wait_ge(o_sb, a - 1)
                out = ps[0:n, O_BANK + a % 2, 0:HD]
                cols_h = slice(h * HD, (h + 1) * HD)
                if i < NT - 1:
                    for k in range(i + 1):
                        last = mm(out, pT_sb[a % 2][:, k * P:(k + 1) * P], v_nat[:, k, cols_h], start=(k == 0), stop=(k == i))
                else:
                    mm(out, pT_sb[a % 2][:, 0:n], v_cache[:, cols_h], start=True, stop=False)
                    last = mm(out, pT_sb[a % 2][0:SS, P:P + n], v_nat[0:SS, i, cols_h], start=False, stop=True)
                last.then_inc(o_ps, 1)

            def pair_out(pr):
                pe.wait_ge(o_sb, 2 * NT * (pr + 1))
                if pr >= 1:
                    pe.wait_ge(oT_sb, pr)
                o = o_nat[pr % 2]
                for i in range(NT):
                    n = ROWS[i]
                    out = ps[:, OT_BANK, i * P:(i + 1) * P] if i < NT - 1 else ps[:, OT_BANK + 1, 0:n]
                    flip = const("flip") if i < NT - 1 else flip_sample[0:n, :]
                    last = mm(out, o[0:n, i, :], flip, start=True, stop=True)
                last.then_inc(oT_ps, 1)

            UNITS = NH * NT
            for a in range(UNITS + 4):
                if a < UNITS:
                    scores(a)
                if 0 <= a - 2 < UNITS:
                    p_transposes(a - 2)
                if 0 <= a - 3 < UNITS:
                    values(a - 3)
                if a - 4 >= 0 and (a - 4) % (2 * NT) == 2 * NT - 1:
                    pair_out((a - 4) // (2 * NT))
            pe.wait_ge(oT_sb, PAIRS)
            pe.wait_ge(o_sb, UNITS)

            def sum_free(m):
                if m >= RAW_BANKS:
                    pe.wait_ge(x_half, m - RAW_BANKS + 1)

            for hf in range(2):
                token_product(att_first + QKV_PIECES + hf, hf * NT, sum_free, att_y)
            route(1)
            experts(1)


_INS = ["x_prompt", "x_sample", "cache_pool", "cache_k", "cache_v", "norm_mix", "norm_ffn", "pool_w", "pool_scale",
        "attn_w_qkv", "attn_w_o", "attn_q_gain", "attn_k_gain", "moe_w_r1", "moe_b_r1", "moe_w_r2", "moe_b_r2",
        "moe_w_gate", "moe_w_up", "moe_w_down"]


def kernel(**inputs):
    import numpy as _np
    import concourse.bacc as _bacc
    from concourse import mybir as _mybir
    from concourse.bass_utils import run_bass_kernel_spmd as _run

    nc = _bacc.Bacc("TRN2", target_bir_lowering=False, num_devices=1)
    arrays, aps = {}, {}

    def give(name, a):
        a = _np.ascontiguousarray(a)
        arrays[f"in_{name}"] = a
        aps[name] = nc.dram_tensor(f"in_{name}", a.shape, _mybir.dt.from_np(a.dtype), kind="ExternalInput").ap()

    for name in _INS:
        give(name, inputs[name])
    B, S, D = inputs["x_prompt"].shape
    SS = inputs["x_sample"].shape[1]
    T = S + SS
    NEXP = inputs["moe_w_gate"].shape[1]
    NG, _, EPG = inputs["moe_w_r2"].shape[1:]
    distance = (S - 1) - _np.arange(S + P - 1)
    index = _np.clip(distance, -(CHUNK - 1), REL_MAX) + CHUNK - 1
    give("rel_bias_reversed", _np.asarray(inputs["attn_rel_bias"])[0][:, index])
    consts, bands, cols = shape_constants(T, -(-T // P), NEXP + (2 * T - 1) // BLK, NEXP, EPG, NG)
    give("consts", consts)
    give("bands", bands)

    NH, HD = inputs["cache_k"].shape[3:]
    hist = inputs["cache_pool"].shape[2]
    shapes = [(1, S, D), (1, SS, D), (1, 1, hist, D), (1, 1, hist, D),
              (1, 1, S, NH, HD), (1, 1, S, NH, HD), (1, 1, SS, NH, HD), (1, 1, SS, NH, HD)]
    outs = [nc.dram_tensor(f"out_{i}", s, F32, kind="ExternalOutput").ap() for i, s in enumerate(shapes)]
    encoder(nc, aps, outs, cols)
    res = _run(nc, [arrays], core_ids=[0])
    return tuple(res.results[0][f"out_{i}"] for i in range(len(shapes)))
```
